# Optimizing a Trainium2 kernel written in Bass

```python
import jax, jax.numpy as jnp
from jax import lax
import numpy as np
import math

D_MODEL = 1024
BATCH = 1
SEQ = 1024
DEPTH = 1

N_MIXERS = 2
MLSTM_HEADS = 4
MLSTM_DK = 128
MLSTM_DV = D_MODEL // MLSTM_HEADS
MLSTM_CHUNK = 128
QK_WIDTH = MLSTM_HEADS * MLSTM_DK
V_WIDTH = MLSTM_HEADS * MLSTM_DV
N_GATE_COLS = 4 * MLSTM_HEADS
MLSTM_IN_WIDTH = 2 * QK_WIDTH + 2 * V_WIDTH + N_GATE_COLS
FORGET_BIAS = 3.0
POOL_WINDOWS = (2, 4, 8, 16)
POOL_GROUPS = len(POOL_WINDOWS)
POOL_GROUP_WIDTH = D_MODEL // POOL_GROUPS
D_FF = 4 * D_MODEL
PLE_DIM = 256
N_MLSTM_LAYERS = (DEPTH + N_MIXERS - 1) // N_MIXERS
N_POOL_LAYERS = DEPTH // N_MIXERS
EPS = 1e-6


def rmsnorm(x, gain):
    x32 = x.astype(jnp.float32)
    y = x32 * lax.rsqrt(jnp.mean(jnp.square(x32), axis=-1, keepdims=True) + EPS)
    return (y * gain.astype(jnp.float32)).astype(x.dtype)

def mlstm_scan(q, k, v, i_pre, f_pre):
    B, H, S, DK = q.shape
    DV = v.shape[-1]
    L = MLSTM_CHUNK
    NC = S // L

    def chunks(t):
        return jnp.moveaxis(t.reshape((B, H, NC, L) + t.shape[3:]), 2, 0)

    qc, kc, vc = chunks(q), chunks(k), chunks(v)
    ic = chunks(i_pre)
    bc = jnp.cumsum(chunks(jax.nn.log_sigmoid(f_pre)), axis=-1)
    lower = jnp.tril(jnp.ones((L, L), dtype=bool))

    def step(carry, xs):
        C, n, m = carry
        q_, k_, v_, i_, b_ = xs
        b_last = b_[..., -1]
        log_d = jnp.where(lower, b_[..., :, None] - b_[..., None, :] + i_[..., None, :], -jnp.inf)
        log_inter = b_ + m[..., None]
        m_t = jnp.maximum(log_inter, jnp.max(log_d, axis=-1))
        d = jnp.exp(log_d - m_t[..., None])
        inter = jnp.exp(log_inter - m_t)
        s = jnp.einsum('bhtd,bhsd->bhts', q_, k_) * d
        num = jnp.einsum('bhts,bhsv->bhtv', s, v_) + inter[..., None] * jnp.einsum('bhtd,bhvd->bhtv', q_, C)
        den = jnp.sum(s, axis=-1) + inter * jnp.einsum('bhtd,bhd->bht', q_, n)
        h = num / jnp.maximum(jnp.abs(den), jnp.exp(-m_t))[..., None]
        log_w = b_last[..., None] - b_ + i_
        m_new = jnp.maximum(b_last + m, jnp.max(log_w, axis=-1))
        w = jnp.exp(log_w - m_new[..., None])
        decay = jnp.exp(b_last + m - m_new)
        C = decay[..., None, None] * C + jnp.einsum('bhsv,bhsd->bhvd', w[..., None] * v_, k_)
        n = decay[..., None] * n + jnp.einsum('bhs,bhsd->bhd', w, k_)
        return (C, n, m_new), h

    init = (jnp.zeros((B, H, DV, DK), jnp.float32),
            jnp.zeros((B, H, DK), jnp.float32),
            jnp.zeros((B, H), jnp.float32))
    _, hs = lax.scan(step, init, (qc, kc, vc, ic, bc))
    return jnp.moveaxis(hs, 0, 2).reshape(B, H, S, DV)

def mlstm_mixer(xn, w_in, b_gates, head_norm, w_out):
    B, S, _ = xn.shape
    u = xn @ w_in
    q, k, v, o, g = jnp.split(u, [QK_WIDTH, 2 * QK_WIDTH, 2 * QK_WIDTH + V_WIDTH,
                                  2 * QK_WIDTH + 2 * V_WIDTH], axis=-1)
    q = q.reshape(B, S, MLSTM_HEADS, MLSTM_DK).transpose(0, 2, 1, 3).astype(jnp.float32)
    k = (k.reshape(B, S, MLSTM_HEADS, MLSTM_DK).transpose(0, 2, 1, 3).astype(jnp.float32)
         * (MLSTM_DK ** -0.5))
    v = v.reshape(B, S, MLSTM_HEADS, MLSTM_DV).transpose(0, 2, 1, 3).astype(jnp.float32)
    g = g.reshape(B, S, 4, MLSTM_HEADS).astype(jnp.float32) + b_gates.astype(jnp.float32)
    g = g.transpose(2, 0, 3, 1)
    h_fwd = mlstm_scan(q, k, v, g[0], g[1])
    flip = lambda t: jnp.flip(t, axis=2)
    h_bwd = flip(mlstm_scan(flip(q), flip(k), flip(v), flip(g[2]), flip(g[3])))
    h = (h_fwd + h_bwd).transpose(0, 2, 1, 3)
    h = h * lax.rsqrt(jnp.mean(jnp.square(h), axis=-1, keepdims=True) + EPS)
    h = h * head_norm.astype(jnp.float32).reshape(MLSTM_HEADS, MLSTM_DV)
    h = h.reshape(B, S, V_WIDTH) * jax.nn.sigmoid(o.astype(jnp.float32))
    return h.astype(xn.dtype) @ w_out

def pool_mixer(xn, w_in, w_grp, scale, w_out):
    B, S, D = xn.shape
    u = (xn @ w_in).astype(jnp.float32)
    cs = jnp.concatenate([jnp.zeros((B, 1, D), jnp.float32), jnp.cumsum(u, axis=1)], axis=1)
    t = jnp.arange(S)
    pooled = []
    for gi, win in enumerate(POOL_WINDOWS):
        c0, c1 = gi * POOL_GROUP_WIDTH, (gi + 1) * POOL_GROUP_WIDTH
        lo = jnp.clip(t - win // 2, 0, S)
        hi = jnp.clip(t + win - win // 2, 0, S)
        csg = cs[:, :, c0:c1]
        mean = (csg[:, hi] - csg[:, lo]) / (hi - lo).astype(jnp.float32)[None, :, None]
        pooled.append(mean)
    y = jnp.concatenate(pooled, axis=-1) - u
    y = jnp.einsum('bsgc,gcd->bsgd', y.reshape(B, S, POOL_GROUPS, POOL_GROUP_WIDTH),
                   w_grp.astype(jnp.float32)).reshape(B, S, D)
    y = y * scale.astype(jnp.float32)
    return y.astype(xn.dtype) @ w_out

def sqrelu_mlp(xn, w1, w2):
    return jnp.square(jax.nn.relu(xn @ w1)) @ w2

def first_inputs(seed: int = 0) -> dict:
    key = jax.random.key(seed)
    ks = jax.random.split(key, 24)

    def nrm(k, shape, fan_in):
        return jax.random.normal(k, shape, jnp.float32) * (fan_in ** -0.5)

    def gain(k, shape):
        return 1.0 + 0.05 * jax.random.normal(k, shape, jnp.float32)

    nA, nB = N_MLSTM_LAYERS, N_POOL_LAYERS
    gate_base = jnp.array([0.0, FORGET_BIAS, 0.0, FORGET_BIAS], jnp.float32)[None, :, None]
    return {
        'x': jax.random.normal(ks[0], (BATCH, SEQ, D_MODEL), jnp.float32),
        'p': jax.random.normal(ks[1], (DEPTH, BATCH, SEQ, PLE_DIM), jnp.float32),
        'norm_mix': gain(ks[2], (DEPTH, D_MODEL)),
        'norm_mlp': gain(ks[3], (DEPTH, D_MODEL)),
        'norm_ple': gain(ks[4], (DEPTH, D_MODEL)),
        'norm_final': gain(ks[5], (D_MODEL,)),
        'mlstm_w_in': nrm(ks[6], (nA, D_MODEL, MLSTM_IN_WIDTH), D_MODEL),
        'mlstm_b_gates': gate_base + 0.1 * jax.random.normal(ks[7], (nA, 4, MLSTM_HEADS), jnp.float32),
        'mlstm_head_norm': gain(ks[8], (nA, V_WIDTH)),
        'mlstm_w_out': nrm(ks[9], (nA, V_WIDTH, D_MODEL), V_WIDTH),
        'pool_w_in': nrm(ks[10], (nB, D_MODEL, D_MODEL), D_MODEL),
        'pool_w_grp': nrm(ks[11], (nB, POOL_GROUPS, POOL_GROUP_WIDTH, POOL_GROUP_WIDTH), POOL_GROUP_WIDTH),
        'pool_scale': gain(ks[12], (nB, D_MODEL)),
        'pool_w_out': nrm(ks[13], (nB, D_MODEL, D_MODEL), D_MODEL),
        'mlp_w1': nrm(ks[14], (DEPTH, D_MODEL, D_FF), D_MODEL),
        'mlp_w2': nrm(ks[15], (DEPTH, D_FF, D_MODEL), D_FF),
        'ple_w': nrm(ks[16], (DEPTH, PLE_DIM, D_MODEL), PLE_DIM),
        'ple_gate_w': nrm(ks[17], (DEPTH, D_MODEL, D_MODEL), D_MODEL),
        'ple_gate_b': 0.02 * jax.random.normal(ks[18], (DEPTH, D_MODEL), jnp.float32),
    }

def first_block(x, p, norm_mix, norm_mlp, norm_ple, norm_final,
              mlstm_w_in, mlstm_b_gates, mlstm_head_norm, mlstm_w_out,
              pool_w_in, pool_w_grp, pool_scale, pool_w_out,
              mlp_w1, mlp_w2, ple_w, ple_gate_w, ple_gate_b):
    h = x
    for i in range(DEPTH):
        xn = rmsnorm(h, norm_mix[i])
        j = i // N_MIXERS
        if i % N_MIXERS == 0:
            mix = mlstm_mixer(xn, mlstm_w_in[j], mlstm_b_gates[j], mlstm_head_norm[j], mlstm_w_out[j])
        else:
            mix = pool_mixer(xn, pool_w_in[j], pool_w_grp[j], pool_scale[j], pool_w_out[j])
        h = h + mix
        h = h + sqrelu_mlp(rmsnorm(h, norm_mlp[i]), mlp_w1[i], mlp_w2[i])
        gate = jax.nn.sigmoid((rmsnorm(h, norm_ple[i]) @ ple_gate_w[i] + ple_gate_b[i]).astype(jnp.float32))
        h = h + (gate * (p[i] @ ple_w[i]).astype(jnp.float32)).astype(h.dtype)
    return rmsnorm(h, norm_final)


RWKV_HEADS = 8
RWKV_HEAD_DIM = 64
RWKV_WIDTH = RWKV_HEADS * RWKV_HEAD_DIM
DECAY_LORA = 64
ICLR_LORA = 64
GN_EPS = 64e-5
ATT_HEADS = 8
ATT_HEAD_DIM = 64
ATT_WIDTH = ATT_HEADS * ATT_HEAD_DIM
KV_LATENT = 128
IDX_HEADS = 8
IDX_HEAD_DIM = 64
TOPK_MAX = 256
Q_BLOCK = 128
NUM_BUCKETS = 32
MAX_DISTANCE = 128
NORM_EPS = 1e-6
COL_SIZES = (RWKV_WIDTH, RWKV_WIDTH, RWKV_WIDTH, DECAY_LORA, ICLR_LORA, RWKV_WIDTH,
             ATT_WIDTH, KV_LATENT, ATT_WIDTH, IDX_HEADS * IDX_HEAD_DIM, IDX_HEAD_DIM, IDX_HEADS,
             D_MODEL, D_MODEL)
N_SHIFT = 3 * RWKV_WIDTH + DECAY_LORA + ICLR_LORA
N_IN = sum(COL_SIZES)


def rms_norm(x, g):
    xf = x.astype(jnp.float32)
    y = xf * lax.rsqrt(jnp.mean(xf * xf, axis=-1, keepdims=True) + NORM_EPS)
    return (y * g.astype(jnp.float32)).astype(x.dtype)

def token_shift(u):
    return jnp.pad(u, ((0, 0), (1, 0), (0, 0)))[:, :-1]

def t5_bucket(dist):
    max_exact = NUM_BUCKETS // 2
    is_small = dist < max_exact
    d = jnp.maximum(dist, 1).astype(jnp.float32)
    large = max_exact + (jnp.log(d / max_exact) / math.log(MAX_DISTANCE / max_exact)
                         * (NUM_BUCKETS - max_exact)).astype(jnp.int32)
    large = jnp.minimum(large, NUM_BUCKETS - 1)
    return jnp.where(is_small, dist, large)

def rwkv7_scan(r, w, k, v, a_vec, b_vec):
    B, S, H, N = r.shape

    def step(state, inp):
        r_t, w_t, k_t, v_t, a_t, b_t = inp
        sa = jnp.einsum('bhvk,bhk->bhv', state, a_t)
        state = (state * w_t[:, :, None, :] + sa[..., None] * b_t[:, :, None, :]
                 + v_t[..., None] * k_t[:, :, None, :])
        y_t = jnp.einsum('bhvk,bhk->bhv', state, r_t)
        return state, y_t

    xs = tuple(jnp.moveaxis(t, 1, 0) for t in (r, w, k, v, a_vec, b_vec))
    s0 = jnp.zeros((B, H, N, N), jnp.float32)
    _, y = lax.scan(step, s0, xs)
    return jnp.moveaxis(y, 0, 1)

def rwkv7_branch(pr, pk, pv, pwd, pad_, w0, w2, a0, a2, k_k, k_a, r_k, lnx_g, lnx_b):
    B, S, _ = pr.shape
    f32 = jnp.float32
    heads = lambda t: t.astype(f32).reshape(B, S, RWKV_HEADS, RWKV_HEAD_DIM)
    w_log = -jax.nn.softplus(-(w0 + jnp.tanh(pwd) @ w2).astype(f32)) - 0.5
    decay = jnp.exp(-jnp.exp(w_log))
    a = jax.nn.sigmoid((a0 + pad_ @ a2).astype(f32))
    kk = heads(pk * k_k)
    kk = kk / jnp.maximum(jnp.sqrt(jnp.sum(kk * kk, axis=-1, keepdims=True)), 1e-12)
    k = pk.astype(f32) * (1.0 + (a - 1.0) * k_a)
    r_h, k_h, v_h, a_h, w_h = heads(pr), heads(k), heads(pv), heads(a), heads(decay)
    y = rwkv7_scan(r_h, w_h, k_h, v_h, -kk, kk * a_h)
    mu = jnp.mean(y, axis=-1, keepdims=True)
    var = jnp.mean(jnp.square(y - mu), axis=-1, keepdims=True)
    yn = ((y - mu) * lax.rsqrt(var + GN_EPS)).reshape(B, S, RWKV_WIDTH) * lnx_g + lnx_b
    bonus = jnp.sum(r_h * k_h * r_k.astype(f32), axis=-1, keepdims=True) * v_h
    out = yn + bonus.reshape(B, S, RWKV_WIDTH)
    return out.astype(pr.dtype)

def dsa_branch(q, ckv, qi, ki, wi, kv_norm_g, w_uk, w_uv, rel_bias):
    B, S, _ = q.shape
    topk = min(TOPK_MAX, S // 4)
    nb = S // Q_BLOCK
    q = q.reshape(B, S, ATT_HEADS, ATT_HEAD_DIM)
    lat = rms_norm(ckv, kv_norm_g)
    q_abs = jnp.einsum('bshd,chd->bshc', q, w_uk) * (ATT_HEAD_DIM ** -0.5)
    qi = qi.reshape(B, S, IDX_HEADS, IDX_HEAD_DIM)
    key_pos = jnp.arange(S, dtype=jnp.int32)
    qpos = key_pos.reshape(nb, Q_BLOCK)
    b_idx = jnp.arange(B)[:, None, None]

    def blocks(t):
        return jnp.moveaxis(t.reshape((B, nb, Q_BLOCK) + t.shape[2:]), 1, 0)

    def one_block(args):
        qa_b, qi_b, wi_b, pos_b = args
        s_idx = jax.nn.relu(jnp.einsum('bqhd,bsd->bqhs', qi_b, ki))
        score = jnp.einsum('bqh,bqhs->bqs', wi_b, s_idx).astype(jnp.float32)
        causal = key_pos[None, :] <= pos_b[:, None]
        score = jnp.where(causal[None], score, -jnp.inf)
        _, sel = lax.top_k(score, topk)
        lat_sel = lat[b_idx, sel]
        dist = pos_b[None, :, None] - sel
        valid = dist >= 0
        bias = rel_bias[t5_bucket(jnp.maximum(dist, 0))]
        logits = (jnp.einsum('bqhc,bqkc->bqhk', qa_b, lat_sel).astype(jnp.float32)
                  + jnp.moveaxis(bias, -1, 2).astype(jnp.float32))
        logits = jnp.where(valid[:, :, None, :], logits, -jnp.inf)
        p = jax.nn.softmax(logits, axis=-1)
        return jnp.einsum('bqhk,bqkc->bqhc', p.astype(lat_sel.dtype), lat_sel)

    o_lat = lax.map(one_block, (blocks(q_abs), blocks(qi), blocks(wi), qpos))
    o_lat = jnp.moveaxis(o_lat, 0, 1).reshape(B, S, ATT_HEADS, KV_LATENT)
    o = jnp.einsum('bshc,chd->bshd', o_lat, w_uv)
    return o.reshape(B, S, ATT_WIDTH)

def second_inputs(seed: int = 0) -> dict:
    key = jax.random.key(seed)
    ks = jax.random.split(key, 24)
    f32 = jnp.float32

    def nrm(k, shape, s):
        return jax.random.normal(k, shape, f32) * s

    return {
        "x": nrm(ks[0], (BATCH, SEQ, D_MODEL), 1.0),
        "c": nrm(ks[1], (BATCH, D_MODEL), 1.0),
        "ada_w": nrm(ks[2], (DEPTH, D_MODEL, 3 * D_MODEL), 0.5 * D_MODEL ** -0.5),
        "ada_b": nrm(ks[3], (DEPTH, 3 * D_MODEL), 0.02),
        "norm_g": 1.0 + nrm(ks[4], (DEPTH, D_MODEL), 0.05),
        "w_in": nrm(ks[5], (DEPTH, D_MODEL, N_IN), D_MODEL ** -0.5),
        "shift_mu": jax.random.uniform(ks[6], (DEPTH, N_SHIFT), f32),
        "w0": jax.random.uniform(ks[7], (DEPTH, RWKV_WIDTH), f32, -6.0, -1.0),
        "w2": nrm(ks[8], (DEPTH, DECAY_LORA, RWKV_WIDTH), 0.1),
        "a0": nrm(ks[9], (DEPTH, RWKV_WIDTH), 0.5),
        "a2": nrm(ks[10], (DEPTH, ICLR_LORA, RWKV_WIDTH), 0.1),
        "k_k": 0.85 + nrm(ks[11], (DEPTH, RWKV_WIDTH), 0.05),
        "k_a": 1.0 + nrm(ks[12], (DEPTH, RWKV_WIDTH), 0.05),
        "r_k": nrm(ks[13], (DEPTH, RWKV_HEADS, RWKV_HEAD_DIM), 0.1),
        "lnx_g": 1.0 + nrm(ks[14], (DEPTH, RWKV_WIDTH), 0.05),
        "lnx_b": nrm(ks[15], (DEPTH, RWKV_WIDTH), 0.02),
        "kv_norm_g": 1.0 + nrm(ks[16], (DEPTH, KV_LATENT), 0.05),
        "w_uk": nrm(ks[17], (DEPTH, KV_LATENT, ATT_HEADS, ATT_HEAD_DIM), KV_LATENT ** -0.5),
        "w_uv": nrm(ks[18], (DEPTH, KV_LATENT, ATT_HEADS, ATT_HEAD_DIM), KV_LATENT ** -0.5),
        "w_pa": nrm(ks[19], (DEPTH, RWKV_WIDTH, D_MODEL), RWKV_WIDTH ** -0.5),
        "w_pb": nrm(ks[20], (DEPTH, ATT_WIDTH, D_MODEL), ATT_WIDTH ** -0.5),
        "w_o": nrm(ks[21], (DEPTH, D_MODEL, D_MODEL), D_MODEL ** -0.5),
        "rel_bias": nrm(ks[22], (NUM_BUCKETS, ATT_HEADS), 0.5),
        "final_g": 1.0 + nrm(ks[23], (D_MODEL,), 0.05),
    }

def second_block(x, c, ada_w, ada_b, norm_g, w_in, shift_mu, w0, w2, a0, a2, k_k, k_a, r_k,
              lnx_g, lnx_b, kv_norm_g, w_uk, w_uv, w_pa, w_pb, w_o, rel_bias, final_g):
    split_at = np.cumsum(np.array(COL_SIZES))[:-1].tolist()
    c_act = jax.nn.silu(c)
    for l in range(DEPTH):
        mod = c_act @ ada_w[l] + ada_b[l]
        shift, scale, gate = jnp.split(mod, 3, axis=-1)
        h = rms_norm(x, norm_g[l]) * (1.0 + scale[:, None, :]) + shift[:, None, :]
        p = h @ w_in[l]
        ps = p[..., :N_SHIFT]
        ps = ps + (token_shift(ps) - ps) * shift_mu[l]
        p = jnp.concatenate([ps, p[..., N_SHIFT:]], axis=-1)
        (pr, pk, pv, pwd, pad_, z_a, q, ckv, z_b, qi, ki, wi, g_a, g_b) = jnp.split(p, split_at, axis=-1)
        y_a = rwkv7_branch(pr, pk, pv, pwd, pad_, w0[l], w2[l], a0[l], a2[l], k_k[l], k_a[l],
                           r_k[l], lnx_g[l], lnx_b[l])
        y_b = dsa_branch(q, ckv, qi, ki, wi, kv_norm_g[l], w_uk[l], w_uv[l], rel_bias)
        br_a = (y_a * jax.nn.silu(z_a)) @ w_pa[l]
        br_b = (y_b * jax.nn.silu(z_b)) @ w_pb[l]
        merged = jax.nn.sigmoid(g_a) * br_a + jax.nn.sigmoid(g_b) * br_b
        x = x + gate[:, None, :] * (merged @ w_o[l])
    return rms_norm(x, final_g)


def setup_inputs(seed=0):
    out = dict(first_inputs(seed))
    for name, value in second_inputs(seed + 1).items():
        if name != "x":
            out[name + "_2"] = value
    return out


def reference(
    x, p, norm_mix, norm_mlp, norm_ple, norm_final, mlstm_w_in, mlstm_b_gates, mlstm_head_norm,
    mlstm_w_out, pool_w_in, pool_w_grp, pool_scale, pool_w_out, mlp_w1, mlp_w2, ple_w,
    ple_gate_w, ple_gate_b, c_2, ada_w_2, ada_b_2, norm_g_2, w_in_2, shift_mu_2, w0_2, w2_2,
    a0_2, a2_2, k_k_2, k_a_2, r_k_2, lnx_g_2, lnx_b_2, kv_norm_g_2, w_uk_2, w_uv_2, w_pa_2,
    w_pb_2, w_o_2, rel_bias_2, final_g_2,
):
    x = first_block(
        x, p, norm_mix, norm_mlp, norm_ple, norm_final, mlstm_w_in, mlstm_b_gates,
        mlstm_head_norm, mlstm_w_out, pool_w_in, pool_w_grp, pool_scale, pool_w_out, mlp_w1,
        mlp_w2, ple_w, ple_gate_w, ple_gate_b,
    )
    return second_block(
        x, c_2, ada_w_2, ada_b_2, norm_g_2, w_in_2, shift_mu_2, w0_2, w2_2, a0_2, a2_2, k_k_2,
        k_a_2, r_k_2, lnx_g_2, lnx_b_2, kv_norm_g_2, w_uk_2, w_uv_2, w_pa_2, w_pb_2, w_o_2,
        rel_bias_2, final_g_2,
    )


_drawn_inputs = setup_inputs


def setup_inputs(seed=0):
    import zlib

    import numpy as np

    out = dict(_drawn_inputs(seed))
    spreads = {}
    factors = {'norm_ple': 8.0,
     'ple_gate_b': 8.0,
     'ada_b_2': 5.023,
     'norm_g_2': 4.541,
     'w2_2': 5.173,
     'a0_2': 2.76,
     'k_k_2': 74.681,
     'k_a_2': 3.061,
     'lnx_g_2': 58.431,
     'lnx_b_2': 200.0,
     'kv_norm_g_2': 8.0,
     'w_uk_2': 4.048,
     'rel_bias_2': 23.42}
    for name, (base, spread) in spreads.items():
        noise = np.random.default_rng([zlib.crc32(name.encode()), seed]).standard_normal(out[name].shape)
        drawn = base * np.exp(spread * noise) if base else spread * noise
        out[name] = __import__('jax').numpy.asarray(drawn.astype(out[name].dtype))
    for name, factor in factors.items():
        out[name] = (out[name] * factor).astype(out[name].dtype)
    return out
```

```python
import numpy as np
import concourse.bass as bass
from concourse import mybir
from concourse.alu_op_type import AluOpType as ALU

F32 = mybir.dt.float32
ACT = mybir.ActivationFunctionType
AX = mybir.AxisListType.X

P = 128
T = 1024
D = 1024
HALF = 512
KT = D // P
EPS = 1e-6

MH = 4
DV = D // MH
L = 128
NC = T // L
DK_SCALE = 128 ** -0.5
FF_GROUPS = 4

RP = 4
RL = 64
LEVELS = 6
GN_EPS = 64e-5

AH = 8
TOPK = 256
FAR = -3.0e38
TAKEN = -3.4e38
CUT = -3.2e38
DROP = -1.0e30
BIG = 1.0e30
LOWEST = -3.0e38

PARAMS = [("norm_mix", 8), ("norm_mlp", 8), ("norm_ple", 8), ("norm_final", 8), ("head_norm", 8),
          ("ple_gate_b", 8), ("c", 8), ("ada_b", 24), ("norm_g", 8), ("mu", 13), ("w0", 4), ("a0", 4),
          ("k_k", 4), ("k_a", 4), ("r_k", 4), ("lnx_g", 4), ("lnx_b", 4), ("kv_norm", 1),
          ("final_g", 8), ("b_gates", 1)]
PCOL = {}
for _n, _w in PARAMS:
    PCOL[_n] = sum(w for _, w in PARAMS[:len(PCOL)])
NPARAM = sum(w for _, w in PARAMS)

CONSTS = [("ident", 128), ("ones", 128), ("head_ones", 128), ("causal", 128), ("mask_fwd", 128),
          ("mask_bwd", 128), ("mask_ra", 128), ("levels", LEVELS * RL), ("eye2", RL)]
CCOL = {}
for _n, _w in CONSTS:
    CCOL[_n] = sum(w for _, w in CONSTS[:len(CCOL)])
NCONST = sum(w for _, w in CONSTS)
NDIST = 384

X0, XN, QK, VT, OG = 0, 8, 16, 24, 32
KTOK, HSUM = 0, 8
HID = 16
YB, YA, HN = 0, 4, 8


def constant_tile():
    c = np.zeros((P, NCONST), np.float32)
    i = np.arange(P)[:, None]
    j = np.arange(P)[None, :]

    def put(name, a):
        c[:, CCOL[name]:CCOL[name] + a.shape[1]] = a
    put("ident", (i == j).astype(np.float32))
    put("ones", np.ones((P, P), np.float32))
    put("head_ones", (i // RL == j // RL).astype(np.float32))
    put("causal", np.where(j <= i, 0.0, FAR).astype(np.float32))
    put("mask_fwd", np.where(j >= i, 0.0, BIG).astype(np.float32))
    put("mask_bwd", np.where(j <= i, 0.0, BIG).astype(np.float32))
    il, t = i % RL, np.arange(RL)[None, :]
    put("mask_ra", np.concatenate([t >= il, t > il], axis=1).astype(np.float32))
    lev = []
    for n in range(LEVELS):
        b = 1 << n
        lev.append(((il // b) % 2 == 1) & (t // b == il // b - 1))
    put("eye2", (il == t).astype(np.float32))
    put("levels", np.concatenate(lev, axis=1).astype(np.float32))
    return c


def distance_buckets():
    hot = np.zeros((32, NDIST), np.float32)
    for i in range(256):
        d = 255 - i
        if d < 16:
            b = d
        else:
            b = min(31, 16 + int(np.floor(np.log(d / 16.0) / np.log(8.0) * 16 + 1e-9)))
        hot[b, i] = 1.0
    return hot


class Steps:

    def __init__(self, eng, sem):
        self.eng, self.sem, self.n = eng, sem, 0

    def done(self, ins):
        self.n += 1
        ins.then_inc(self.sem, 1)
        self.eng.wait_ge(self.sem, self.n)


def wait_apart(eng, sem, value, passed):
    eng.wait_ge(sem, value)
    eng.sem_inc(passed, 1)


class Mem:
    pass


IN_USE = []


def new_semaphore(nc):
    def allocate(name):
        IN_USE.append(nc.alloc_semaphore(name))
        return IN_USE[-1]
    return allocate


def recycle_semaphores(nc):
    with nc.Block() as block:
        @block.gpsimd
        def _(pool):
            for s in IN_USE:
                pool.sem_clear(s)
    for s in IN_USE:
        nc.release_semaphore(s)
    IN_USE.clear()


def half(hf):
    return slice(hf * HALF, (hf + 1) * HALF)


def gemm_loads(sp, chunks, parts, wbuf, loaded, products):
    def load(n, s):
        for w, off, kt in parts:
            sp.dma_start(wbuf[:, s, off * P:(off + kt) * P], w[n]).then_inc(loaded[s], 16)
    for n in range(min(2, chunks)):
        load(n, n)
    if chunks >= 4:
        with sp.Fori(1, chunks // 2) as i:
            for s in range(2):
                sp.wait_ge(products, i * 4 + (2 * s - 2))
                load(i * 2 + s, s)
    if chunks % 2 and chunks > 2:
        n = chunks - 1
        sp.wait_ge(products, 2 * n - 2)
        load(n, 0)


def gemm_products(nc, pe, chunks, parts, rhs_of, ps, wbuf, loaded, products, emptied):
    banks = min(4, 8 // len(parts))

    def chunk(n, s, first):
        pe.wait_ge(loaded[s], first)
        for hf in range(2):
            pe.wait_ge(emptied[hf], n + 1)
            for q, (w, off, kt) in enumerate(parts):
                for k in range(kt):
                    last = nc.tensor.matmul(ps[:, q * banks + (2 * s + hf) % banks, :],
                                            wbuf[:, s, (off + k) * P:(off + k + 1) * P],
                                            rhs_of(q, k, hf), start=(k == 0), stop=(k == kt - 1))
            last.then_inc(products, 1)
    per = 16 * len(parts)
    if chunks >= 2:
        with pe.Fori(0, chunks // 2) as i:
            for s in range(2):
                chunk(i * 2 + s, s, i * per + per)
    if chunks % 2:
        chunk(chunks - 1, 0, per * (chunks // 2 + 1))


def gemm_drain(eng, hf, chunks, parts, products, emptied, take):
    banks = min(4, 8 // parts)
    eng.sem_inc(emptied[hf], banks // 2)
    if chunks >= 2:
        with eng.Fori(0, chunks // 2) as i:
            for s in range(2):
                eng.wait_ge(products, i * 4 + (2 * s + hf + 1))
                take(i * 2 + s, (2 * s + hf) % banks)
    if chunks % 2:
        n = chunks - 1
        eng.wait_ge(products, 2 * n + hf + 1)
        take(n, hf % banks)


def gemm_sems(nc, name):
    return ([new_semaphore(nc)(f"{name}_weights_loaded{s}") for s in range(2)],
            new_semaphore(nc)(f"{name}_products"),
            [new_semaphore(nc)(f"{name}_emptied{h}") for h in range(2)])


def project(nc, m, name, weights, chunks, kt, src, dst):
    loaded, products, emptied = gemm_sems(nc, name)
    parts = [(weights, 0, kt)]
    with nc.Block() as block:
        @block.sync
        def _(sp):
            gemm_loads(sp, chunks, parts, m.wbuf, loaded, products)

        @block.tensor
        def _(pe):
            gemm_products(nc, pe, chunks, parts, lambda q, k, hf: m.big[:, src + k, half(hf)],
                          m.ps, m.wbuf, loaded, products, emptied)

        @block.scalar
        def _(act):
            gemm_drain(act, 0, chunks, 1, products, emptied, lambda n, b: nc.scalar.copy(
                m.big[:, n + dst, half(0)], m.ps[:, b, :]).then_inc(emptied[0], 1))

        @block.vector
        def _(dve):
            gemm_drain(dve, 1, chunks, 1, products, emptied, lambda n, b: nc.vector.tensor_copy(
                m.big[:, n + dst, half(1)], m.ps[:, b, :]).then_inc(emptied[1], 1))


def rms_norm(nc, m, name, src, dst, gain, shift=None, store=None):
    squared = new_semaphore(nc)(f"{name}_squared")
    summed = new_semaphore(nc)(f"{name}_summed")
    variance = new_semaphore(nc)(f"{name}_variance")
    root = new_semaphore(nc)(f"{name}_root")
    steps = new_semaphore(nc)(f"{name}_steps")
    scaled = new_semaphore(nc)(f"{name}_scaled")
    shifted = new_semaphore(nc)(f"{name}_shifted")
    stored = new_semaphore(nc)(f"{name}_stored")
    with nc.Block() as block:
        @block.scalar
        def _(act):
            for n in range(2 * KT):
                hf, k = divmod(n, KT)
                if n >= 6:
                    act.wait_ge(summed, n - 5)
                nc.scalar.activation(m.tmp[:, n % 6, :], m.big[:, src + k, half(hf)],
                                     ACT.Square).then_inc(squared, 1)
            for hf in range(2):
                act.wait_ge(variance, hf + 1)
                nc.scalar.activation(m.tmp[:, 6 + hf, :], m.tmp[:, 6 + hf, :], ACT.Sqrt).then_inc(root, 1)

        @block.tensor
        def _(pe):
            for n in range(2 * KT):
                hf, k = divmod(n, KT)
                pe.wait_ge(squared, n + 1)
                nc.tensor.matmul(m.ps[:, hf, :], m.const("ones"), m.tmp[:, n % 6, :],
                                 start=(k == 0), stop=(k == KT - 1)).then_inc(summed, 1)

        @block.vector
        def _(dve):
            for hf in range(2):
                dve.wait_ge(summed, KT * (hf + 1))
                nc.vector.tensor_scalar(m.tmp[:, 6 + hf, :], m.ps[:, hf, :], 1.0 / D, EPS,
                                        ALU.mult, ALU.add).then_inc(variance, 1)
            for hf in range(2):
                dve.wait_ge(root, hf + 1)
                nc.vector.reciprocal(m.tmp[:, 6 + hf, :], m.tmp[:, 6 + hf, :]).then_inc(steps, 1)
                dve.wait_ge(steps, hf + 1)
                for k in range(KT):
                    nc.vector.scalar_tensor_tensor(m.big[:, dst + k, half(hf)], m.big[:, src + k, half(hf)],
                                                   gain(k), m.tmp[:, 6 + hf, :], ALU.mult,
                                                   ALU.mult).then_inc(scaled, 1)

        @block.gpsimd
        def _(pool):
            if shift is not None:
                for n in range(2 * KT):
                    hf, k = divmod(n, KT)
                    pool.wait_ge(scaled, n + 1)
                    nc.gpsimd.tensor_scalar(m.big[:, dst + k, half(hf)], m.big[:, dst + k, half(hf)],
                                            shift(k), 1.0, ALU.add, ALU.mult).then_inc(shifted, 1)

        @block.sync
        def _(sp):
            if store is not None:
                for n in range(2 * KT):
                    hf, k = divmod(n, KT)
                    sp.wait_ge(scaled, n + 1)
                    sp.dma_start(store[:, k, half(hf)], m.big[:, dst + k, half(hf)]).then_inc(stored, 16)
                sp.wait_ge(stored, 16 * 2 * KT)


def load_inputs(nc, m):
    loaded = new_semaphore(nc)("inputs_loaded")
    with nc.Block() as block:
        @block.sync
        def _(sp):
            sp.dma_start(m.params[:], m.d["params"]).then_inc(loaded, 16)
            sp.dma_start(m.consts[:], m.d["consts"]).then_inc(loaded, 16)
            for k in range(KT):
                sp.dma_start(m.big[:, X0 + k, :], m.d["xT"][k]).then_inc(loaded, 16)
            sp.wait_ge(loaded, 16 * (KT + 2))


def mlstm_values_and_gates(nc, m):
    wv_loaded = new_semaphore(nc)("wv_loaded")
    products = new_semaphore(nc)("v_products")
    emptied = [new_semaphore(nc)(f"v_emptied{q}") for q in range(2)]
    gate_products = new_semaphore(nc)("gate_products")
    gates_biased = new_semaphore(nc)("gates_biased")
    gates_stored = new_semaphore(nc)("gates_stored")
    wg = m.wbuf[:, 0, 0:KT * 16]
    gates = m.tmp[0:16, 0:2, :]

    with nc.Block() as block:
        @block.sync
        def _(sp):
            for n in range(2):
                sp.dma_start(m.big[:, OG + 4 * n:OG + 4 * n + 4, :],
                             m.d["wv"][n].rearrange("p (a b) -> p a b", b=T)).then_inc(wv_loaded, 16)
            sp.dma_start(wg, m.d["wgate"]).then_inc(wv_loaded, 16)
            for g in range(4):
                sp.wait_ge(gates_biased, 2)
                sp.dma_start(m.d["gates"][g].rearrange("c h t -> h c t"),
                             gates[4 * g:4 * g + 4].rearrange("h a (c t) -> h (a c) t", t=L)
                             ).then_inc(gates_stored, 16)
            sp.wait_ge(gates_stored, 64)

        @block.tensor
        def _(pe):
            pe.wait_ge(wv_loaded, 48)
            with pe.Fori(0, 2) as i:
                for tt in range(NC):
                    pe.wait_ge(emptied[tt % 2], i * 4 + (tt // 2 + 1))
                    for k in range(KT):
                        last = nc.tensor.matmul(
                            m.ps[:, tt % 4, :], m.big[:, XN + k, tt * P:(tt + 1) * P],
                            m.flat(OG, 8)[:, bass.ds(i * 4096 + k * HALF, HALF)],
                            start=(k == 0), stop=(k == KT - 1))
                    last.then_inc(products, 1)
            for hf in range(2):
                for k in range(KT):
                    last = nc.tensor.matmul(m.ps[0:16, 4 + hf, :], wg[:, k * 16:(k + 1) * 16],
                                            m.big[:, XN + k, half(hf)], start=(k == 0), stop=(k == KT - 1))
                last.then_inc(gate_products, 1)

        def drain(eng, q, copy):
            eng.sem_inc(emptied[q], 2)
            with eng.Fori(0, 2) as i:
                for tt in range(q, NC, 2):
                    eng.wait_ge(products, i * NC + (tt + 1))
                    copy(m.big[:, VT + tt, bass.ds(i * HALF, HALF)], m.ps[:, tt % 4, :]).then_inc(emptied[q], 1)

        @block.scalar
        def _(act):
            drain(act, 0, nc.scalar.copy)

        @block.vector
        def _(dve):
            drain(dve, 1, nc.vector.tensor_copy)
            for hf in range(2):
                dve.wait_ge(gate_products, hf + 1)
                nc.vector.tensor_scalar(gates[:, hf, :], m.ps[0:16, 4 + hf, :], m.par("b_gates", 0)[0:16],
                                        None, ALU.add).then_inc(gates_biased, 1)


def mlstm_output_gate(nc, m):
    passed = new_semaphore(nc)("o_passed")
    loaded, products, emptied = gemm_sems(nc, "o")
    copied = new_semaphore(nc)("o_copied")
    parts = [(m.d["wo"], 0, KT)]
    with nc.Block() as block:
        @block.sync
        def _(sp):
            gemm_loads(sp, 8, parts, m.wbuf, loaded, products)

        @block.tensor
        def _(pe):
            gemm_products(nc, pe, 8, parts, lambda q, k, hf: m.big[:, XN + k, half(hf)],
                          m.ps, m.wbuf, loaded, products, emptied)

        @block.scalar
        def _(act):
            act.sem_inc(emptied[0], 2)
            act.sem_inc(emptied[1], 2)
            with act.Fori(0, 4) as i:
                for s in range(2):
                    for hf in range(2):
                        wait_apart(act, products, i * 4 + (2 * s + hf + 1), passed)
                        nc.scalar.activation(m.big[:, i * 2 + (OG + s), half(hf)], m.ps[:, 2 * s + hf, :],
                                             ACT.Sigmoid).then_inc(emptied[hf], 1)


def mlstm_gates(nc, m):
    rows = [m.tmp[0:64, n, 0:256] for n in range(8)]
    irow, frow = rows[0][:, 0:L], rows[0][:, L:]
    lf, e1 = rows[1][:, 0:L], rows[1][:, L:]
    b, g = rows[2][:, 0:L], rows[2][:, L:]
    cm, mx = rows[3][:, 0:L], rows[3][:, L:]
    inter, em = rows[4][:, 0:L], rows[4][:, L:]
    w, zero = rows[5][:, 0:L], rows[5][:, L:]
    ends = rows[6][:, 0:2]
    mprev = rows[6][:, 2:3]
    mlast = rows[6][:, 3:4]
    nmlast = rows[6][:, 4:5]
    decay = rows[6][:, 5:6]
    carr = rows[6][:, 16:32]
    mm = rows[6][:, 32:41]
    loaded = new_semaphore(nc)("gate_rows_loaded")
    zeroed = new_semaphore(nc)("gate_zeroed")
    dstep = new_semaphore(nc)("gate_vector_steps")
    astep = new_semaphore(nc)("gate_scalar_steps")
    abs_ready = new_semaphore(nc)("gate_log_ready")
    ends_ready = new_semaphore(nc)("gate_ends_ready")
    ends_moved = new_semaphore(nc)("gate_ends_moved")
    carried = new_semaphore(nc)("gate_carried")
    mprev_moved = new_semaphore(nc)("gate_mprev_moved")
    max_ready = new_semaphore(nc)("gate_max_ready")
    exp_ready = new_semaphore(nc)("gate_exp_ready")
    scaled = new_semaphore(nc)("gate_inter_scaled")
    rows_stored = new_semaphore(nc)("gate_rows_stored")
    turned = new_semaphore(nc)("gate_columns_turned")
    ktok_used = new_semaphore(nc)("ktok_turned")
    ktok_copied = [new_semaphore(nc)(f"ktok_copied{q}") for q in range(2)]
    dirs = [(slice(0, 32), slice(None), L - 1), (slice(32, 64), slice(None, None, -1), 0)]

    with nc.Block() as block:
        @block.sync
        def _(sp):
            for d in range(2):
                sp.dma_start(irow[32 * d:32 * d + 32], m.d["gates"][2 * d].rearrange("c h t -> (c h) t")
                             ).then_inc(loaded, 16)
                sp.dma_start(frow[32 * d:32 * d + 32], m.d["gates"][2 * d + 1].rearrange("c h t -> (c h) t")
                             ).then_inc(loaded, 16)
            sp.wait_ge(ends_ready, 4)
            sp.dma_start(m.d["ends"], ends).then_inc(ends_moved, 16)
            sp.wait_ge(ends_moved, 16)
            for d in range(2):
                for q in range(2):
                    sp.dma_start(carr[32 * d:32 * d + MH, 8 * q:8 * q + 8],
                                 m.d["ends"][32 * d:32 * d + 32, q].rearrange("(c h) -> h c", h=MH),
                                 allow_slow_non_contiguous=True).then_inc(ends_moved, 16)
            sp.wait_ge(carried, 2)
            for d in range(2):
                sp.dma_start(m.d["mprev"][32 * d:32 * d + 32].rearrange("(c h) -> h c", h=MH),
                             mm[32 * d:32 * d + MH, d:d + 8],
                             allow_slow_non_contiguous=True).then_inc(mprev_moved, 16)
            sp.wait_ge(mprev_moved, 32)
            sp.dma_start(mprev, m.d["mprev"].rearrange("(r a) -> r a", a=1)).then_inc(mprev_moved, 16)
            sp.wait_ge(max_ready, 1)
            sp.dma_start(m.d["scan_rows"][0], mx).then_inc(rows_stored, 16)
            sp.wait_ge(scaled, 1)
            sp.dma_start(m.d["scan_rows"][1], inter).then_inc(rows_stored, 16)
            sp.wait_ge(exp_ready, 4)
            sp.dma_start(m.d["decay"].rearrange("(r a) -> r a", a=1), decay).then_inc(rows_stored, 16)
            sp.wait_ge(rows_stored, 48)
            sp.dma_start(m.decay_b[:], m.d["decay"].partition_broadcast(P)).then_inc(rows_stored, 16)
            sp.wait_ge(rows_stored, 64)

        @block.gpsimd
        def _(pool):
            nc.gpsimd.memset(zero, 0.0).then_inc(zeroed, 1)
            nc.gpsimd.memset(mm, 0.0).then_inc(zeroed, 1)

        @block.scalar
        def _(act):
            step = Steps(act, astep)
            act.wait_ge(loaded, 64)
            step.done(nc.scalar.activation(e1, frow, ACT.Abs))
            step.done(nc.scalar.activation(e1, e1, ACT.Exp, scale=-1.0))
            nc.scalar.activation(e1, e1, ACT.Ln, bias=1.0).then_inc(abs_ready, 1)
            act.wait_ge(max_ready, 3)
            nc.scalar.activation(inter, mx, ACT.Exp, bias=mprev, scale=-1.0).then_inc(exp_ready, 1)
            nc.scalar.activation(em, em, ACT.Exp, scale=-1.0).then_inc(exp_ready, 1)
            nc.scalar.activation(w, g, ACT.Exp, bias=nmlast).then_inc(exp_ready, 1)
            nc.scalar.activation(decay, nmlast, ACT.Exp, bias=mprev).then_inc(exp_ready, 1)
            for c in range(1, NC, 2):
                act.wait_ge(ktok_used, c + 1)
                nc.scalar.copy(m.ktok(c), m.ps[:, c % 4, :]).then_inc(ktok_copied[c % 2], 1)

        @block.vector
        def _(dve):
            step = Steps(dve, dstep)
            dve.wait_ge(loaded, 64)
            dve.wait_ge(abs_ready, 1)
            dve.wait_ge(zeroed, 2)
            step.done(nc.vector.scalar_tensor_tensor(lf, frow, 0.0, e1, ALU.min, ALU.subtract))
            for rs, ts, _ in dirs:
                step.done(nc.vector.tensor_tensor_scan(b[rs, ts], lf[rs, ts], zero[rs], 0.0, ALU.add, ALU.add))
            step.done(nc.vector.tensor_tensor(g, irow, b, ALU.subtract))
            for rs, ts, _ in dirs:
                step.done(nc.vector.tensor_tensor_scan(cm[rs, ts], g[rs, ts], g[rs, ts], LOWEST, ALU.max, ALU.max))
            for rs, _, e in dirs:
                nc.vector.tensor_copy(ends[rs, 0:1], cm[rs, e:e + 1]).then_inc(ends_ready, 1)
                nc.vector.tensor_copy(ends[rs, 1:2], b[rs, e:e + 1]).then_inc(ends_ready, 1)
            dve.wait_ge(ends_moved, 16 * 5)
            nc.vector.tensor_tensor_scan(mm[0:MH, 1:9], carr[0:MH, 0:8], carr[0:MH, 8:16], 0.0,
                                         ALU.max, ALU.add).then_inc(carried, 1)
            nc.vector.tensor_tensor_scan(mm[32:32 + MH, 7::-1], carr[32:32 + MH, 7::-1],
                                         carr[32:32 + MH, 15:7:-1], 0.0, ALU.max, ALU.add).then_inc(carried, 1)
            dve.wait_ge(mprev_moved, 48)
            nc.vector.tensor_scalar(mx, cm, mprev, None, ALU.max).then_inc(max_ready, 1)
            step.done(nc.vector.tensor_tensor(mlast, mprev, ends[:, 0:1], ALU.max))
            nc.vector.tensor_scalar(nmlast, mlast, -1.0, None, ALU.mult).then_inc(max_ready, 1)
            nc.vector.tensor_tensor(em, b, mx, ALU.add).then_inc(max_ready, 1)
            dve.wait_ge(exp_ready, 1)
            nc.vector.tensor_scalar(inter, inter, DK_SCALE, None, ALU.mult).then_inc(scaled, 1)
            for c in range(0, NC, 2):
                dve.wait_ge(ktok_used, c + 1)
                nc.vector.tensor_copy(m.ktok(c), m.ps[:, c % 4, :]).then_inc(ktok_copied[c % 2], 1)
            dve.wait_ge(turned, 3)
            nc.vector.tensor_copy(m.gcols[:], m.ps[:, 4, 0:192].rearrange("p (a b) -> p a b", a=3)
                                  ).then_inc(dstep, 1)

        @block.tensor
        def _(pe):
            for c in range(NC):
                if c >= 4:
                    pe.wait_ge(ktok_copied[c % 2], (c - 4) // 2 + 1)
                for h in range(MH):
                    last = nc.tensor.transpose(m.ps[:, c % 4, h * P:(h + 1) * P],
                                               m.big[:, QK + MH + h, c * L:(c + 1) * L], m.const("ident"))
                last.then_inc(ktok_used, 1)
            pe.wait_ge(exp_ready, 4)
            for q, r in enumerate((g, w, em)):
                nc.tensor.transpose(m.ps[:, 4, 64 * q:64 * q + 64], r, m.const("ident")[0:64, 0:64]
                                    ).then_inc(turned, 1)


def mlstm_scan(nc, m):
    units = []
    for step in range(NC):
        units += [(0, step, step), (1, NC - 1 - step, step)]
    n_units = len(units)
    mxb = [m.tmp[:, d, :] for d in range(2)]
    intb = [m.tmp[:, 2 + d, :] for d in range(2)]
    arg = [m.tmp[:, 4 + d, :] for d in range(2)]
    prob = [m.tmp[:, 6 + d, :] for d in range(2)]
    spare = m.flat(4, 4)
    wv = [spare[:, d * 1024:(d + 1) * 1024] for d in range(2)]
    qi = [spare[:, 2048 + d * 512:2048 + (d + 1) * 512] for d in range(2)]
    cst = m.wflat[:, 0:2048].rearrange("p (d h v) -> p d h v", d=2, h=MH)
    nst = m.wflat[:, 2048:2056].rearrange("p (d h) -> p d h", d=2)
    den = m.wflat[:, 2056:2060]
    nsc = m.wflat[:, 2060:2064]
    S = new_semaphore(nc)
    rows_loaded = [S(f"scan_rows_loaded{d}") for d in range(2)]
    scores_ready, arg_step, arg_ready, decay_ready = S("scores_ready"), S("arg_step"), S("arg_ready"), S("decay_ready")
    probs_ready, qi_ready, wv_ready = S("probs_ready"), S("qi_ready"), S("wv_ready")
    num_ready, state_products, h_done, state_updated = S("num_ready"), S("state_products"), S("h_done"), S("state_updated")
    zeroed, dstep = S("states_zeroed"), S("scan_vector_steps")

    def row(d, c):
        return d * 32 + c * MH

    def heads(ap, w=L):
        return ap.rearrange("p (h t) -> p h t", h=MH)

    with nc.Block() as block:
        @block.sync
        def _(sp):
            for u, (d, c, _) in enumerate(units):
                if u >= 2:
                    sp.wait_ge(arg_ready, u - 1)
                    sp.wait_ge(qi_ready, u - 1)
                for q, dst in enumerate((mxb[d], intb[d])):
                    src = m.d["scan_rows"][q, row(d, c):row(d, c) + MH].rearrange("r t -> (r t)")
                    sp.dma_start(dst, src.partition_broadcast(P)).then_inc(rows_loaded[d], 16)

        @block.gpsimd
        def _(pool):
            nc.gpsimd.memset(m.wflat[:, 0:2056], 0.0).then_inc(zeroed, 1)
            for u, (d, c, _) in enumerate(units):
                pool.wait_ge(rows_loaded[d], 32 * (u // 2 + 1))
                if u >= 2:
                    pool.wait_ge(probs_ready, u - 1)
                gcol = m.gcols[:, 0, row(d, c):row(d, c) + MH].unsqueeze(2).to_broadcast([P, MH, L])
                nc.gpsimd.tensor_tensor(heads(arg[d]), heads(mxb[d]), gcol, ALU.subtract).then_inc(arg_step, 1)
                pool.wait_ge(arg_step, u + 1)
                mask = m.const("mask_bwd" if d else "mask_fwd").unsqueeze(1).to_broadcast([P, MH, L])
                nc.gpsimd.tensor_tensor(heads(arg[d]), heads(arg[d]), mask, ALU.add).then_inc(arg_ready, 1)
                if u >= 2:
                    pool.wait_ge(num_ready, u - 1)
                nc.gpsimd.tensor_tensor(heads(qi[d]), m.big[:, QK:QK + MH, c * L:(c + 1) * L], heads(intb[d]),
                                        ALU.mult).then_inc(qi_ready, 1)

        @block.scalar
        def _(act):
            for u, (d, c, _) in enumerate(units):
                act.wait_ge(arg_ready, u + 1)
                nc.scalar.activation(arg[d], arg[d], ACT.Exp, scale=-1.0).then_inc(decay_ready, 1)
                if u >= 2:
                    act.wait_ge(state_products, u - 1)
                for h in range(MH):
                    r = row(d, c) + h
                    ins = nc.scalar.mul(wv[d][:, h * DV:(h + 1) * DV], m.big[:, VT + c, h * DV:(h + 1) * DV],
                                        m.gcols[:, 1, r:r + 1])
                ins.then_inc(wv_ready, 1)

        @block.tensor
        def _(pe):
            def scores(u):
                d, c, _ = units[u]
                if u >= 2:
                    pe.wait_ge(probs_ready, u - 1)
                for h in range(MH):
                    last = nc.tensor.matmul(m.ps[:, d, h * L:(h + 1) * L],
                                            m.big[:, QK + MH + h, c * L:(c + 1) * L],
                                            m.big[:, QK + h, c * L:(c + 1) * L], start=True, stop=True)
                last.then_inc(scores_ready, 1)

            pe.wait_ge(zeroed, 1)
            scores(0)
            for u, (d, c, _) in enumerate(units):
                if u + 1 < n_units:
                    scores(u + 1)
                pe.wait_ge(probs_ready, u + 1)
                pe.wait_ge(qi_ready, u + 1)
                if u >= 1:
                    pe.wait_ge(h_done, u)
                if u >= 2:
                    pe.wait_ge(state_updated, u - 1)
                for h in range(MH):
                    hs = slice(h * L, (h + 1) * L)
                    out = m.ps[:, 2 + h // 2, (h % 2) * DV:(h % 2 + 1) * DV]
                    nc.tensor.matmul(out, prob[d][:, hs], m.big[:, VT + c, h * DV:(h + 1) * DV], start=True, stop=False)
                    nc.tensor.matmul(out, qi[d][:, hs], cst[:, d, h, :], start=False, stop=True)
                    nc.tensor.matmul(m.ps[:, 6, h:h + 1], prob[d][:, hs], m.const("ones")[:, 0:1], start=True, stop=False)
                    last = nc.tensor.matmul(m.ps[:, 6, h:h + 1], qi[d][:, hs], nst[:, d, h:h + 1], start=False, stop=True)
                last.then_inc(num_ready, 1)
                pe.wait_ge(wv_ready, u + 1)
                if u >= 1:
                    pe.wait_ge(state_updated, u)
                for h in range(MH):
                    k = m.ktok(c)[:, h * L:(h + 1) * L]
                    r = row(d, c) + h
                    nc.tensor.matmul(m.ps[:, 4 + h // 2, (h % 2) * DV:(h % 2 + 1) * DV], k,
                                     wv[d][:, h * DV:(h + 1) * DV], start=True, stop=True)
                    last = nc.tensor.matmul(m.ps[:, 7, h:h + 1], k, m.gcols[:, 1, r:r + 1], start=True, stop=True)
                last.then_inc(state_products, 1)

        @block.vector
        def _(dve):
            step = Steps(dve, dstep)

            def probs(u):
                d, c, _ = units[u]
                dve.wait_ge(scores_ready, u + 1)
                dve.wait_ge(decay_ready, u + 1)
                nc.vector.scalar_tensor_tensor(prob[d], m.ps[:, d, :], DK_SCALE, arg[d], ALU.mult,
                                               ALU.mult).then_inc(probs_ready, 1)

            dve.wait_ge(zeroed, 1)
            probs(0)
            for u, (d, c, s) in enumerate(units):
                if u + 1 < n_units:
                    probs(u + 1)
                r = row(d, c)
                dve.wait_ge(num_ready, u + 1)
                step.done(nc.vector.tensor_scalar(den, m.ps[:, 6, 0:MH], -1.0, None, ALU.mult))
                step.done(nc.vector.tensor_tensor(den, den, m.ps[:, 6, 0:MH], ALU.max))
                step.done(nc.vector.tensor_tensor(den, den, m.gcols[:, 2, r:r + MH], ALU.max))
                step.done(nc.vector.reciprocal(den, den))
                for h in range(MH):
                    num = m.ps[:, 2 + h // 2, (h % 2) * DV:(h % 2 + 1) * DV]
                    out = m.big[:, HSUM + c, h * DV:(h + 1) * DV]
                    if s < NC // 2:
                        ins = nc.vector.tensor_scalar(out, num, den[:, h:h + 1], None, ALU.mult)
                    else:
                        ins = nc.vector.scalar_tensor_tensor(out, num, den[:, h:h + 1], out, ALU.mult, ALU.add)
                ins.then_inc(h_done, 1)
                dve.wait_ge(state_products, u + 1)
                for h in range(MH):
                    nc.vector.scalar_tensor_tensor(cst[:, d, h, :], cst[:, d, h, :], m.decay_b[:, r + h:r + h + 1],
                                                   m.ps[:, 4 + h // 2, (h % 2) * DV:(h % 2 + 1) * DV],
                                                   ALU.mult, ALU.add)
                step.done(nc.vector.tensor_tensor(nsc, nst[:, d, :], m.decay_b[:, r:r + MH], ALU.mult))
                nc.vector.tensor_tensor(nst[:, d, :], nsc, m.ps[:, 7, 0:MH], ALU.add).then_inc(state_updated, 1)


def mlstm_head_norm(nc, m):
    S = new_semaphore(nc)
    squared, steps, rooted, normed = S("head_squared"), S("head_steps"), S("head_rooted"), S("head_normed")
    turned, gated = S("head_turned"), S("head_gated")
    ss = m.wflat[:, 0:32]
    with nc.Block() as block:
        @block.scalar
        def _(act):
            for c in range(NC):
                for h in range(MH):
                    n = c * MH + h
                    if n >= 16:
                        act.wait_ge(squared, n - 15)
                    nc.scalar.activation(m.tflat[:, (n % 16) * DV:(n % 16 + 1) * DV], m.big[:, HSUM + c, h * DV:(h + 1) * DV], ACT.Square,
                                         accum_out=ss[:, c * MH + h:c * MH + h + 1]).then_inc(squared, 1)
            act.wait_ge(steps, 1)
            nc.scalar.activation(ss, ss, ACT.Sqrt).then_inc(rooted, 1)

        @block.vector
        def _(dve):
            dve.wait_ge(squared, NC * MH)
            nc.vector.tensor_scalar(ss, ss, 1.0 / DV, EPS, ALU.mult, ALU.add).then_inc(steps, 1)
            dve.wait_ge(rooted, 1)
            nc.vector.reciprocal(ss, ss).then_inc(steps, 1)
            dve.wait_ge(steps, 2)
            for c in range(NC):
                hc = m.big[:, HSUM + c, :].rearrange("p (h v) -> p h v", h=MH)
                nc.vector.tensor_tensor(hc, hc, ss[:, c * MH:(c + 1) * MH].unsqueeze(2).to_broadcast([P, MH, DV]),
                                        ALU.mult).then_inc(normed, 1)
            for n in range(2 * KT):
                hf, f = divmod(n, KT)
                dve.wait_ge(turned, n + 1)
                nc.vector.scalar_tensor_tensor(m.big[:, QK + f, half(hf)], m.ps[:, n % 4, :], m.par("head_norm", f),
                                               m.big[:, OG + f, half(hf)], ALU.mult, ALU.mult).then_inc(gated, 1)

        @block.tensor
        def _(pe):
            for n in range(2 * KT):
                hf, f = divmod(n, KT)
                pe.wait_ge(normed, 4 * hf + 4)
                if n >= 4:
                    pe.wait_ge(gated, n - 3)
                for q in range(4):
                    last = nc.tensor.transpose(m.ps[:, n % 4, q * P:(q + 1) * P],
                                               m.big[:, HSUM + 4 * hf + q, f * P:(f + 1) * P], m.const("ident"))
                last.then_inc(turned, 1)


def mlstm_out(nc, m):
    loaded, products, emptied = gemm_sems(nc, "w_out")
    x_loaded = new_semaphore(nc)("x_loaded_again")
    parts = [(m.d["w_out"], 0, KT)]
    with nc.Block() as block:
        @block.sync
        def _(sp):
            for k in range(KT):
                sp.dma_start(m.big[:, VT + k, :], m.d["xT"][k]).then_inc(x_loaded, 16)
            gemm_loads(sp, 8, parts, m.wbuf, loaded, products)

        @block.tensor
        def _(pe):
            gemm_products(nc, pe, 8, parts, lambda q, k, hf: m.big[:, QK + k, half(hf)],
                          m.ps, m.wbuf, loaded, products, emptied)

        @block.vector
        def _(dve):
            dve.wait_ge(x_loaded, 16 * KT)
            for hf in range(2):
                dve.sem_inc(emptied[hf], 2)
            with dve.Fori(0, 4) as i:
                for s in range(2):
                    for hf in range(2):
                        dve.wait_ge(products, i * 4 + (2 * s + hf + 1))
                        nc.vector.tensor_tensor(m.big[:, i * 2 + (X0 + s), half(hf)], m.ps[:, 2 * s + hf, :],
                                                m.big[:, i * 2 + (VT + s), half(hf)],
                                                ALU.add).then_inc(emptied[hf], 1)


def mlp(nc, m):
    S = new_semaphore(nc)
    passed = S("mlp_passed")
    loaded = [S(f"mlp_weights_loaded{s}") for s in range(2)]
    products = S("mlp_products")
    hid_emptied = [S(f"mlp_hidden_emptied{h}") for h in range(2)]
    hid_ready = [S(f"mlp_hidden_ready{h}") for h in range(2)]
    relu_step = [S(f"mlp_relu{h}") for h in range(2)]
    down_emptied = [S(f"mlp_down_emptied{h}") for h in range(2)]
    parts = [(m.d["w_mlp"], 0, KT)]
    G = 2 * KT

    with nc.Block() as block:
        @block.sync
        def _(sp):
            gemm_loads(sp, FF_GROUPS * G, parts, m.wbuf, loaded, products)

        @block.tensor
        def _(pe):
            with pe.Fori(0, FF_GROUPS) as g:
                for hf in range(2):
                    wait_apart(pe, down_emptied[hf], g * KT + 2, passed)
                with pe.Fori(0, KT // 2) as i:
                    for s in range(2):
                        pe.wait_ge(loaded[s], g * (16 * KT) + i * 16 + 16)
                        for hf in range(2):
                            pe.wait_ge(hid_emptied[hf], g * KT + i * 2 + (s + 1))
                            for k in range(KT):
                                last = nc.tensor.matmul(m.ps[:, 2 * s + hf, :], m.wbuf[:, s, k * P:(k + 1) * P],
                                                        m.big[:, XN + k, half(hf)], start=(k == 0), stop=(k == KT - 1))
                            last.then_inc(products, 1)
                for hf in range(2):
                    wait_apart(pe, hid_ready[hf], g * KT + KT, passed)
                with pe.Fori(0, KT // 2) as i:
                    for s in range(2):
                        pe.wait_ge(loaded[s], g * (16 * KT) + i * 16 + (16 + 8 * KT))
                        for hf in range(2):
                            pe.wait_ge(down_emptied[hf], g * KT + i * 2 + (s + 1))
                            for k in range(KT):
                                last = nc.tensor.matmul(m.ps[:, 2 * s + hf, :], m.wbuf[:, s, k * P:(k + 1) * P],
                                                        m.big[:, HID + k, half(hf)], start=(k == 0), stop=(k == KT - 1))
                            last.then_inc(products, 1)

        def hidden(eng, hf, g, relu, square):
            with eng.Fori(0, KT // 2) as i:
                for s in range(2):
                    h = m.big[:, i * 2 + (HID + s), half(hf)]
                    wait_apart(eng, products, g * (2 * G) + i * 4 + (2 * s + hf + 1), passed)
                    relu(h, m.ps[:, 2 * s + hf, :]).then_inc(hid_emptied[hf], 1)
                    wait_apart(eng, hid_emptied[hf], g * KT + i * 2 + (s + 3), passed)
                    square(h).then_inc(hid_ready[hf], 1)

        @block.scalar
        def _(act):
            act.sem_inc(hid_emptied[0], 2)
            with act.Fori(0, FF_GROUPS) as g:
                hidden(act, 0, g, lambda h, ps: nc.scalar.activation(h, ps, ACT.Relu),
                       lambda h: nc.scalar.activation(h, h, ACT.Square))

        @block.vector
        def _(dve):
            dve.sem_inc(hid_emptied[1], 2)
            for hf in range(2):
                dve.sem_inc(down_emptied[hf], 2)
            with dve.Fori(0, FF_GROUPS) as g:
                hidden(dve, 1, g, lambda h, ps: nc.vector.tensor_scalar(h, ps, 0.0, None, ALU.max),
                       lambda h: nc.vector.tensor_tensor(h, h, h, ALU.mult))
                with dve.Fori(0, KT // 2) as i:
                    for s in range(2):
                        for hf in range(2):
                            h = m.big[:, i * 2 + (X0 + s), half(hf)]
                            dve.wait_ge(products, g * (2 * G) + i * 4 + (G + 2 * s + hf + 1))
                            nc.vector.tensor_tensor(h, m.ps[:, 2 * s + hf, :], h, ALU.add
                                                    ).then_inc(down_emptied[hf], 1)


def ple(nc, m):
    loaded, products, emptied = gemm_sems(nc, "ple")
    p_loaded = new_semaphore(nc)("p_loaded")
    gate_ready = new_semaphore(nc)("ple_gate_ready")
    gated = new_semaphore(nc)("ple_gated")
    passed = new_semaphore(nc)("ple_passed")
    parts = [(m.d["w_pgate"], 0, KT), (m.d["w_ple"], KT, 2)]
    with nc.Block() as block:
        @block.sync
        def _(sp):
            for k in range(2):
                sp.dma_start(m.big[:, VT + k, :], m.d["pT"][k]).then_inc(p_loaded, 16)
            gemm_loads(sp, 8, parts, m.wbuf, loaded, products)

        @block.tensor
        def _(pe):
            pe.wait_ge(p_loaded, 32)
            gemm_products(nc, pe, 8, parts, lambda q, k, hf: m.big[:, (VT if q else XN) + k, half(hf)],
                          m.ps, m.wbuf, loaded, products, emptied)

        @block.scalar
        def _(act):
            act.sem_inc(gated, 4)
            with act.Fori(0, 4) as i:
                for s in range(2):
                    for hf in range(2):
                        u = 2 * s + hf
                        wait_apart(act, products, i * 4 + (u + 1), passed)
                        wait_apart(act, gated, i * 4 + (u + 1), passed)
                        nc.scalar.activation(m.tmp[:, u, :], m.ps[:, u, :], ACT.Sigmoid,
                                             bias=m.par_at("ple_gate_b", i * 2 + s)).then_inc(gate_ready, 1)

        @block.vector
        def _(dve):
            for hf in range(2):
                dve.sem_inc(emptied[hf], 2)
            with dve.Fori(0, 4) as i:
                for s in range(2):
                    for hf in range(2):
                        u = 2 * s + hf
                        h = m.big[:, i * 2 + (X0 + s), half(hf)]
                        dve.wait_ge(gate_ready, i * 4 + (u + 1))
                        nc.vector.tensor_tensor(m.tmp[:, u, :], m.tmp[:, u, :], m.ps[:, 4 + u, :], ALU.mult
                                                ).then_inc(emptied[hf], 1)
                        dve.wait_ge(emptied[hf], i * 2 + (s + 3))
                        nc.vector.tensor_tensor(h, h, m.tmp[:, u, :], ALU.add).then_inc(gated, 1)


def modulation(nc, m):
    S = new_semaphore(nc)
    loaded = [S(f"ada_loaded{s}") for s in range(2)]
    silu_step, silu_ready, products, steps = S("silu_step"), S("silu_ready"), S("ada_products"), S("ada_steps")
    with nc.Block() as block:
        @block.sync
        def _(sp):
            for n in range(8):
                if n >= 2:
                    sp.wait_ge(products, n - 1)
                sp.dma_start(m.wbuf[:, n % 2, :].rearrange("p (a b) -> p a b", a=3),
                             m.d["w_ada"][3 * n:3 * n + 3].rearrange("n p k -> p n k")).then_inc(loaded[n % 2], 16)

        @block.scalar
        def _(act):
            nc.scalar.activation(m.cact[:], m.pars("c"), ACT.Sigmoid).then_inc(silu_step, 1)

        @block.tensor
        def _(pe):
            pe.wait_ge(silu_ready, 1)
            for n in range(8):
                pe.wait_ge(loaded[n % 2], 16 * (n // 2 + 1))
                for q in range(3):
                    for k in range(KT):
                        o = 3 * n + q
                        last = nc.tensor.matmul(m.ps[:, 0, o:o + 1], m.wbuf[:, n % 2, (q * KT + k) * P:(q * KT + k + 1) * P],
                                                m.cact[:, k:k + 1], start=(k == 0), stop=(k == KT - 1))
                last.then_inc(products, 1)

        @block.vector
        def _(dve):
            step = Steps(dve, steps)
            dve.wait_ge(silu_step, 1)
            nc.vector.tensor_tensor(m.cact[:], m.cact[:], m.pars("c"), ALU.mult).then_inc(silu_ready, 1)
            dve.wait_ge(products, 8)
            step.done(nc.vector.tensor_tensor(m.mod[:], m.ps[:, 0, 0:24], m.pars("ada_b"), ALU.add))
            step.done(nc.vector.scalar_tensor_tensor(m.gain2[:], m.mod[:, 8:16], 1.0, m.pars("norm_g"),
                                                     ALU.add, ALU.mult))


QA, QI, CKV, KW, LT, LK, KD, BW, QABS = 16, 20, 24, 25, 26, 27, 28, 30, 32


def latents(nc, m):
    S = new_semaphore(nc)
    loaded, kd_loaded, squared, summed, variance = S("att_loaded"), S("kd_loaded"), S("ckv_squared"), S("ckv_summed"), S("ckv_var")
    root, steps, lat_ready, turned, bias_ready = S("ckv_root"), S("ckv_steps"), S("lat_ready"), S("lat_turned"), S("bias_ready")
    bias_copied, bias_stored = S("bias_copied"), S("bias_stored")
    hot = m.tmp[0:32, 6, 0:NDIST]
    relb = m.tmp[0:32, 7, 0:AH]
    brow = m.tmp[0:AH, 5, 0:NDIST]
    with nc.Block() as block:
        @block.sync
        def _(sp):
            sp.dma_start(hot, m.d["hot"]).then_inc(loaded, 16)
            sp.dma_start(relb, m.d["rel_bias"]).then_inc(loaded, 16)
            sp.dma_start(m.relfar[:], m.d["rel_bias"][31].partition_broadcast(P)).then_inc(loaded, 16)
            sp.dma_start(m.big[:, 4, 0:512].rearrange("p (a c) -> p a c", a=4), m.d["w_ukT"]).then_inc(loaded, 16)
            sp.dma_start(m.big[:, 4, 512:1024], m.d["w_uv"]).then_inc(loaded, 16)
            sp.dma_start(m.big[0:64, KD, :], m.big[0:64, KW, :]).then_inc(kd_loaded, 16)
            sp.dma_start(m.big[64:128, KD, :], m.big[0:64, KW, :]).then_inc(kd_loaded, 16)
            sp.wait_ge(bias_copied, 1)
            sp.dma_start(m.d["bias_rows"], brow).then_inc(bias_stored, 16)
            sp.wait_ge(bias_stored, 16)
            sp.dma_start(m.d["bias_copies"], m.d["bias_rows"].unsqueeze(1).to_broadcast([AH, P, NDIST])
                         ).then_inc(bias_stored, 16)
            sp.wait_ge(bias_stored, 32)
            for h in range(AH):
                src = m.d["bias_copies"][h]
                sp.dma_start(m.flat(BW, 2)[:, h * 256:(h + 1) * 256],
                             bass.AP(src.tensor, h * P * NDIST + 127, [[NDIST - 1, P], [1, 256]])).then_inc(bias_stored, 16)
            sp.wait_ge(bias_stored, 16 * (AH + 2))
            sp.wait_ge(kd_loaded, 32)
            sp.wait_ge(loaded, 80)

        @block.scalar
        def _(act):
            for hf in range(2):
                nc.scalar.activation(m.tmp[:, hf, :], m.big[:, CKV, half(hf)], ACT.Square).then_inc(squared, 1)
            act.wait_ge(bias_ready, 1)
            nc.scalar.copy(brow, m.ps[0:AH, 6, 0:NDIST]).then_inc(bias_copied, 1)
            for hf in range(2):
                act.wait_ge(variance, hf + 1)
                nc.scalar.activation(m.tmp[:, 2 + hf, :], m.tmp[:, 2 + hf, :], ACT.Sqrt).then_inc(root, 1)

        @block.tensor
        def _(pe):
            for hf in range(2):
                pe.wait_ge(squared, hf + 1)
                nc.tensor.matmul(m.ps[:, hf, :], m.const("ones"), m.tmp[:, hf, :], start=True, stop=True).then_inc(summed, 1)
            pe.wait_ge(loaded, 80)
            nc.tensor.matmul(m.ps[0:AH, 6, 0:NDIST], relb, hot, start=True, stop=True).then_inc(bias_ready, 1)
            for src, b0 in ((KW, 4), (LT, 2)):
                if src == LT:
                    pe.wait_ge(lat_ready, 2)
                for t in range(8):
                    last = nc.tensor.transpose(m.ps[:, b0 + t // 4, (t % 4) * P:(t % 4 + 1) * P],
                                               m.big[:, src, t * P:(t + 1) * P], m.const("ident"))
                last.then_inc(turned, 1)

        @block.vector
        def _(dve):
            for hf in range(2):
                dve.wait_ge(summed, hf + 1)
                nc.vector.tensor_scalar(m.tmp[:, 2 + hf, :], m.ps[:, hf, :], 1.0 / P, EPS, ALU.mult, ALU.add).then_inc(variance, 1)
            for hf in range(2):
                dve.wait_ge(root, hf + 1)
                nc.vector.reciprocal(m.tmp[:, 2 + hf, :], m.tmp[:, 2 + hf, :]).then_inc(steps, 1)
                dve.wait_ge(steps, hf + 1)
                nc.vector.scalar_tensor_tensor(m.big[:, LT, half(hf)], m.big[:, CKV, half(hf)], m.par("kv_norm", 0),
                                               m.tmp[:, 2 + hf, :], ALU.mult, ALU.mult).then_inc(lat_ready, 1)
            dve.wait_ge(turned, 1)
            for q in range(2):
                nc.vector.tensor_copy(m.wi[:, 4 * q:4 * q + 4, :],
                                      m.ps[:, 4 + q, :].rearrange("p (a b) -> p a b", a=4)[:, :, 64:64 + AH])
            dve.wait_ge(turned, 2)
            for q in range(2):
                nc.vector.tensor_copy(m.big[:, LK, half(q)], m.ps[:, 2 + q, :])


def absorbed_queries(nc, m):
    S = new_semaphore(nc)
    products, emptied = S("qabs_products"), [S(f"qabs_emptied{q}") for q in range(2)]
    N = 2 * AH

    def drain(eng, q, scale):
        for n in range(q, N, 2):
            h, hf = divmod(n, 2)
            eng.wait_ge(products, n + 1)
            scale(m.big[:, QABS + h, half(hf)], m.ps[:, n % 8, :]).then_inc(emptied[q], 1)

    with nc.Block() as block:
        @block.tensor
        def _(pe):
            for n in range(N):
                h, hf = divmod(n, 2)
                rows = slice(64 * (h % 2), 64 * (h % 2) + 64)
                if n >= 8:
                    pe.wait_ge(emptied[n % 2], (n - 8) // 2 + 1)
                nc.tensor.matmul(m.ps[:, n % 8, :], m.big[rows, 4, (h // 2) * P:(h // 2 + 1) * P],
                                 m.big[rows, QA + h // 2, half(hf)], start=True, stop=True).then_inc(products, 1)

        @block.scalar
        def _(act):
            drain(act, 0, lambda o, i: nc.scalar.mul(o, i, 0.125))

        @block.vector
        def _(dve):
            drain(dve, 1, lambda o, i: nc.vector.tensor_scalar(o, i, 0.125, None, ALU.mult))


def sparse_attention(nc, m):
    S = new_semaphore(nc)
    idx_ready, relu_done, relu_used, acc_step = S("idx_ready"), S("relu_done"), S("relu_used"), S("acc_step")
    topk_step, sel_ready, biased = S("topk_step"), S("sel_ready"), S("bias_masked")
    scores_ready, logits_done, max_ready, exp_ready = S("att_scores"), S("att_logits"), S("att_max"), S("att_exp")
    turned, pt0, pt1, pv_ready, olat_ready = S("att_turned"), S("att_pt0"), S("att_pt1"), S("att_pv"), S("att_olat")
    o_done, recip_step, o_scaled, o_turned, y_done = S("att_o"), S("att_recip"), S("att_oscaled"), S("att_oturned"), S("att_y")
    work, sel = m.tflat[:, 0:1024], m.tflat[:, 1024:2048]
    bsel = m.tflat[:, 2048:4096].rearrange("p (h j) -> p h j", h=AH)
    bwin = m.flat(BW, 2).rearrange("p (h j) -> p h j", h=AH)
    s = [m.wflat[:, q * 1024:(q + 1) * 1024] for q in range(2)]
    pt = [m.wflat[:, 2048 + q * 1024:2048 + (q + 1) * 1024] for q in range(2)]
    olat = [m.wflat[:, 4096 + q * 128:4096 + (q + 1) * 128] for q in range(2)]
    otok = m.wflat[:, 4352:4864]
    nmax = m.wflat[:, 4864:4872]
    sums = m.wflat[:, 4872:4880]
    recip = m.wflat[:, 4880:4888]
    top8 = m.wflat[:, 4888:4896]
    bank_set = [m.psflat[:, q * 1024:(q + 1) * 1024] for q in range(2)]
    NB = T // P
    ROUNDS = TOPK // 8

    with nc.Block() as block:
        @block.tensor
        def _(pe):
            def pieces(n):
                return [(a, min(a + HALF, n)) for a in range(0, n, HALF)]

            def scores(b, h):
                n, hd = P * (b + 1), AH * b + h
                if hd >= 2:
                    pe.wait_ge(logits_done, hd - 1)
                if b >= 2 and h < 2:
                    pe.wait_ge(relu_done, AH * (b - 1))
                for a, e in pieces(n):
                    last = nc.tensor.matmul(bank_set[h % 2][:, a:e], m.big[:, QABS + h, b * P:(b + 1) * P],
                                            m.big[:, LT, a:e], start=True, stop=True)
                last.then_inc(scores_ready, 1)

            def heads_out(b, h):
                hd = AH * b + h
                pe.wait_ge(olat_ready, hd + 1)
                if h == 0 and b >= 1:
                    pe.wait_ge(o_scaled, b)
                nc.tensor.matmul(m.ps[:, 7, h * 64:(h + 1) * 64], olat[h % 2], m.big[:, 4, 512 + h * 64:512 + (h + 1) * 64],
                                 start=True, stop=True).then_inc(o_done, 1)

            for b in range(NB):
                n = P * (b + 1)
                if b >= 2:
                    for h in range(AH):
                        rows = slice(64 * (h % 2), 64 * (h % 2) + 64)
                        if h < 2:
                            pe.wait_ge(logits_done, AH * b)
                        else:
                            pe.wait_ge(relu_done, AH * (b - 2) + h - 1)
                        for a, e in pieces(n):
                            last = nc.tensor.matmul(bank_set[h % 2][:, a:e], m.big[rows, QI + h // 2, b * P:(b + 1) * P],
                                                    m.big[rows, KD, a:e], start=True, stop=True)
                        last.then_inc(idx_ready, 1)
                scores(b, 0)
                for h in range(AH):
                    hd = AH * b + h
                    if h + 1 < AH:
                        scores(b, h + 1)
                    pe.wait_ge(exp_ready, hd + 1)
                    if hd >= 1:
                        pe.wait_ge(pt0, hd)
                    if b >= 4 and hd > 32:
                        pe.wait_ge(pt1, hd - 32)
                    for kb in range(b + 1):
                        last = nc.tensor.transpose(m.ps[:, 4 + kb // 4, (kb % 4) * P:(kb % 4 + 1) * P],
                                                   s[h % 2][:, kb * P:(kb + 1) * P], m.const("ident"))
                    last.then_inc(turned, 1)
                    if h >= 1:
                        heads_out(b, h - 1)
                    pe.wait_ge(pt0, hd + 1)
                    if b >= 4:
                        pe.wait_ge(pt1, hd - 31)
                    if hd >= 1:
                        pe.wait_ge(olat_ready, hd)
                    if h == 0 and b >= 1:
                        pe.wait_ge(y_done, b)
                    for kb in range(b + 1):
                        last = nc.tensor.matmul(m.ps[:, 6, 0:P], m.big[:, LK, kb * P:(kb + 1) * P],
                                                pt[h % 2][:, kb * P:(kb + 1) * P], start=(kb == 0), stop=(kb == b))
                    last.then_inc(pv_ready, 1)
                heads_out(b, AH - 1)
                pe.wait_ge(o_scaled, b + 1)
                for q in range(4):
                    last = nc.tensor.transpose(m.ps[:, 6, q * P:(q + 1) * P], otok[:, q * P:(q + 1) * P], m.const("ident"))
                last.then_inc(o_turned, 1)

        @block.scalar
        def _(act):
            for b in range(NB):
                n = P * (b + 1)
                if b >= 2:
                    for h in range(AH):
                        i = AH * (b - 2) + h
                        act.wait_ge(idx_ready, i + 1)
                        if h < 2:
                            act.wait_ge(turned, AH * b)
                        else:
                            act.wait_ge(relu_used, i - 1)
                        nc.scalar.activation(s[h % 2][:, 0:n], bank_set[h % 2][:, 0:n], ACT.Relu).then_inc(relu_done, 1)

                def exp(h):
                    hd = AH * b + h
                    act.wait_ge(max_ready, hd + 1)
                    nc.scalar.activation(s[h % 2][:, 0:n], s[h % 2][:, 0:n], ACT.Exp, bias=nmax[:, h:h + 1],
                                         accum_out=sums[:, h:h + 1]).then_inc(exp_ready, 1)
                exp(0)
                for h in range(AH):
                    hd = AH * b + h
                    act.wait_ge(turned, hd + 1)
                    if hd >= 2:
                        act.wait_ge(pv_ready, hd - 1)
                    w = min(n, HALF)
                    nc.scalar.copy(pt[h % 2][:, 0:w], m.ps[:, 4, 0:w]).then_inc(pt0, 1)
                    if h + 1 < AH:
                        exp(h + 1)
                    act.wait_ge(pv_ready, hd + 1)
                    if hd >= 2:
                        act.wait_ge(o_done, hd - 1)
                    nc.scalar.copy(olat[h % 2], m.ps[:, 6, 0:P]).then_inc(olat_ready, 1)
                act.wait_ge(o_turned, b + 1)
                nc.scalar.copy(m.big[:, YB:YB + 4, b * P:(b + 1) * P],
                               m.ps[:, 6, :].rearrange("p (a t) -> p a t", a=4)).then_inc(y_done, 1)

        @block.gpsimd
        def _(pool):
            for b in range(NB):
                n, w = P * (b + 1), min(256, P * (b + 1))
                pool.wait_ge(sel_ready, b + 1)
                nc.gpsimd.tensor_tensor(bsel[:, :, 256 - w:], bwin[:, :, 256 - w:],
                                        sel[:, n - w:n].unsqueeze(1).to_broadcast([P, AH, w]), ALU.add).then_inc(biased, 1)

        @block.vector
        def _(dve):
            acc = Steps(dve, acc_step)
            rec = Steps(dve, recip_step)
            for b in range(NB):
                n, w = P * (b + 1), min(256, P * (b + 1))
                if b >= 2:
                    for h in range(AH):
                        dve.wait_ge(relu_done, AH * (b - 2) + h + 1)
                        wi = m.wi[:, b, h:h + 1]
                        if h == 0:
                            ins = nc.vector.tensor_scalar(work[:, 0:n], s[0][:, 0:n], wi, None, ALU.mult)
                        else:
                            ins = nc.vector.scalar_tensor_tensor(work[:, 0:n], s[h % 2][:, 0:n], wi, work[:, 0:n],
                                                                 ALU.mult, ALU.add)
                        ins.then_inc(relu_used, 1)
                        dve.wait_ge(relu_used, AH * (b - 2) + h + 1)
                    acc.done(nc.vector.tensor_tensor(work[:, n - P:n], work[:, n - P:n], m.const("causal"), ALU.add))
                    before = 2 * ROUNDS * (b - 2)
                    for r in range(ROUNDS):
                        nc.vector.max(top8, work[:, 0:n]).then_inc(topk_step, 1)
                        dve.wait_ge(topk_step, before + 2 * r + 1)
                        nc.vector.match_replace(work[:, 0:n], top8, work[:, 0:n], TAKEN).then_inc(topk_step, 1)
                        dve.wait_ge(topk_step, before + 2 * r + 2)
                    nc.vector.tensor_scalar(sel[:, 0:n], work[:, 0:n], CUT, DROP, ALU.is_gt, ALU.mult).then_inc(sel_ready, 1)
                else:
                    if b == 1:
                        acc.done(nc.vector.memset(sel[:, 0:P], 0.0))
                    nc.vector.tensor_scalar(sel[:, n - P:n], m.const("causal"), -1.0, DROP, ALU.is_lt, ALU.mult).then_inc(sel_ready, 1)
                dve.wait_ge(sel_ready, b + 1)
                dve.wait_ge(biased, b + 1)

                def logits(h):
                    hd = AH * b + h
                    dve.wait_ge(scores_ready, hd + 1)
                    if hd >= 2:
                        dve.wait_ge(turned, hd - 1)
                    if n > w:
                        acc.done(nc.vector.scalar_tensor_tensor(s[h % 2][:, 0:n - w], bank_set[h % 2][:, 0:n - w],
                                                                m.relfar[:, h:h + 1], sel[:, 0:n - w], ALU.add, ALU.add))
                    nc.vector.tensor_tensor(s[h % 2][:, n - w:n], bank_set[h % 2][:, n - w:n], bsel[:, h, 256 - w:],
                                            ALU.add).then_inc(logits_done, 1)
                    dve.wait_ge(logits_done, hd + 1)
                    nc.vector.tensor_reduce(nmax[:, h:h + 1], s[h % 2][:, 0:n], AX, ALU.max, negate=True).then_inc(max_ready, 1)
                logits(0)
                for h in range(AH):
                    hd = AH * b + h
                    if h + 1 < AH:
                        logits(h + 1)
                    if b >= 4:
                        dve.wait_ge(turned, hd + 1)
                        dve.wait_ge(pv_ready, hd - 1)
                        nc.vector.tensor_copy(pt[h % 2][:, HALF:n], m.ps[:, 5, 0:n - HALF]).then_inc(pt1, 1)
                dve.wait_ge(exp_ready, AH * (b + 1))
                rec.done(nc.vector.reciprocal(recip, sums))
                dve.wait_ge(o_done, AH * (b + 1))
                if b >= 1:
                    dve.wait_ge(o_turned, b)
                nc.vector.tensor_tensor(otok.rearrange("p (h d) -> p h d", h=AH),
                                        m.ps[:, 7, :].rearrange("p (h d) -> p h d", h=AH),
                                        recip.unsqueeze(2).to_broadcast([P, AH, 64]), ALU.mult).then_inc(o_scaled, 1)


RR, RK, RV, RC, RA, RB = 16, 20, 24, 28, 32, 36
LORA = 28


def shift_tokens(nc, m):
    S = new_semaphore(nc)
    differed, shifted = S("shift_differed"), S("shifted")
    tanh_done = S("lora_tanh")
    with nc.Block() as block:
        @block.gpsimd
        def _(pool):
            for n in range(13):
                if n >= 4:
                    pool.wait_ge(shifted, n - 3)
                p, t = m.big[:, RR + n, :], m.tflat[:, (n % 4) * 1024:(n % 4 + 1) * 1024]
                nc.gpsimd.tensor_tensor(t[:, 1:], p[:, 0:T - 1], p[:, 1:], ALU.subtract)
                nc.gpsimd.tensor_scalar(t[:, 0:1], p[:, 0:1], -1.0, 0.0, ALU.mult, ALU.add).then_inc(differed, 1)

        @block.vector
        def _(dve):
            for n in range(13):
                dve.wait_ge(differed, n + 1)
                p, t = m.big[:, RR + n, :], m.tflat[:, (n % 4) * 1024:(n % 4 + 1) * 1024]
                nc.vector.scalar_tensor_tensor(p, t, m.par("mu", n), p, ALU.mult, ALU.add).then_inc(shifted, 1)

        @block.scalar
        def _(act):
            act.wait_ge(shifted, 13)
            nc.scalar.activation(m.big[0:64, LORA, :], m.big[0:64, LORA, :], ACT.Tanh).then_inc(tanh_done, 1)


def rwkv_lora(nc, m):
    S = new_semaphore(nc)
    loaded, products, emptied = S("lora_loaded"), S("lora_products"), S("lora_emptied")
    lora_w = m.tflat[:, 0:512]
    with nc.Block() as block:
        @block.sync
        def _(sp):
            sp.dma_start(lora_w, m.d["w_lora"]).then_inc(loaded, 16)

        @block.tensor
        def _(pe):
            pe.wait_ge(loaded, 16)
            for n in range(4 * RP):
                p, q, hf = n // 4, (n // 2) % 2, n % 2
                rows = slice(64 * q, 64 * q + 64)
                if n >= 8:
                    pe.wait_ge(emptied, n - 7)
                nc.tensor.matmul(m.ps[:, n % 8, :], lora_w[rows, p * P:(p + 1) * P], m.big[rows, LORA, half(hf)],
                                 start=True, stop=True).then_inc(products, 1)

        @block.scalar
        def _(act):
            for n in range(4 * RP):
                p, q, hf = n // 4, (n // 2) % 2, n % 2
                act.wait_ge(products, n + 1)
                nc.scalar.activation(m.big[:, (RB if q else RA) + p, half(hf)], m.ps[:, n % 8, :], ACT.Sigmoid,
                                     bias=m.par("a0" if q else "w0", p)).then_inc(emptied, 1)


def rwkv_keys(nc, m):
    S = new_semaphore(nc)
    kk_raw, squared, summed, clamped, rooted = S("kk_raw"), S("kk_squared"), S("kk_summed"), S("kk_clamped"), S("kk_rooted")
    steps, scale_step, k_scaled = S("kk_steps"), S("k_scale_step"), S("k_scaled")
    kk = m.wflat[:, 0:4096].rearrange("p (a t) -> p a t", a=RP)
    N = 2 * RP
    with nc.Block() as block:
        @block.vector
        def _(dve):
            step = Steps(dve, steps)
            for p in range(RP):
                nc.vector.tensor_scalar(kk[:, p, :], m.big[:, RK + p, :], m.par("k_k", p), None, ALU.mult).then_inc(kk_raw, 1)
            for n in range(N):
                dve.wait_ge(summed, n + 1)
                nc.vector.tensor_scalar(m.tmp[:, n, :], m.ps[:, n, :], 1e-24, None, ALU.max).then_inc(clamped, 1)
            for n in range(N):
                p, hf = divmod(n, 2)
                dve.wait_ge(rooted, n + 1)
                step.done(nc.vector.reciprocal(m.tmp[:, n, :], m.tmp[:, n, :]))
                step.done(nc.vector.tensor_tensor(kk[:, p, half(hf)], kk[:, p, half(hf)], m.tmp[:, n, :], ALU.mult))
            dve.wait_ge(k_scaled, RP)
            for p in range(RP):
                nc.vector.tensor_tensor(m.big[:, RB + p, :], m.big[:, RB + p, :], kk[:, p, :], ALU.mult)

        @block.gpsimd
        def _(pool):
            for p in range(RP):
                t = m.big[:, RC + p, :]
                nc.gpsimd.tensor_scalar(t, m.big[:, RB + p, :], -1.0, m.par("k_a", p), ALU.add, ALU.mult).then_inc(scale_step, 1)
                pool.wait_ge(scale_step, 3 * p + 1)
                nc.gpsimd.tensor_scalar(t, t, 1.0, 1.0, ALU.add, ALU.mult).then_inc(scale_step, 1)
                pool.wait_ge(scale_step, 3 * p + 2)
                pool.wait_ge(kk_raw, RP)
                nc.gpsimd.tensor_tensor(m.big[:, RK + p, :], m.big[:, RK + p, :], t, ALU.mult).then_inc(k_scaled, 1)
                pool.sem_inc(scale_step, 1)

        @block.scalar
        def _(act):
            for n in range(N):
                p, hf = divmod(n, 2)
                act.wait_ge(kk_raw, p + 1)
                nc.scalar.activation(m.tmp[:, n, :], kk[:, p, half(hf)], ACT.Square).then_inc(squared, 1)
            for n in range(N):
                act.wait_ge(clamped, n + 1)
                nc.scalar.activation(m.tmp[:, n, :], m.tmp[:, n, :], ACT.Sqrt).then_inc(rooted, 1)

        @block.tensor
        def _(pe):
            for n in range(N):
                pe.wait_ge(squared, n + 1)
                nc.tensor.matmul(m.ps[:, n, :], m.const("head_ones"), m.tmp[:, n, :], start=True, stop=True).then_inc(summed, 1)


def rwkv_bonus(nc, m):
    S = new_semaphore(nc)
    ready, summed, weighted, stored = S("bonus_ready"), S("bonus_summed"), S("bonus_weighted"), S("bonus_stored")
    N = 2 * RP
    with nc.Block() as block:
        @block.vector
        def _(dve):
            for n in range(N):
                p, hf = divmod(n, 2)
                nc.vector.scalar_tensor_tensor(m.tmp[:, n, :], m.big[:, RR + p, half(hf)], m.par("r_k", p),
                                               m.big[:, RK + p, half(hf)], ALU.mult, ALU.mult).then_inc(ready, 1)
            for n in range(N):
                p, hf = divmod(n, 2)
                dve.wait_ge(summed, n + 1)
                nc.vector.tensor_tensor(m.tmp[:, n, :], m.ps[:, n, :], m.big[:, RV + p, half(hf)], ALU.mult
                                        ).then_inc(weighted, 1)

        @block.tensor
        def _(pe):
            for n in range(N):
                pe.wait_ge(ready, n + 1)
                nc.tensor.matmul(m.ps[:, n, :], m.const("head_ones"), m.tmp[:, n, :], start=True, stop=True).then_inc(summed, 1)

        @block.sync
        def _(sp):
            for n in range(N):
                sp.wait_ge(weighted, n + 1)
                sp.dma_start(m.d["bonus"][n], m.tmp[:, n, :]).then_inc(stored, 16)
            sp.wait_ge(stored, 16 * N)


def rwkv_scale(nc, m):
    S = new_semaphore(nc)
    steps, zeroed, summed, before_ready = S("cum_steps"), S("reset_ready"), S("cum_ready"), S("cum_before_ready")
    exps = S("decay_exps")
    scaled_r = S("r_scaled")
    kk = m.wflat[:, 0:4096].rearrange("p (a t) -> p a t", a=RP)
    keep = m.wflat[:, 4096:5120]
    up = m.tflat[:].rearrange("p (a t) -> p a t", a=RP)
    with nc.Block() as block:
        @block.vector
        def _(dve):
            step = Steps(dve, steps)
            step.done(nc.vector.memset(keep, 1.0))
            step.done(nc.vector.memset(keep[:, 0:T:RL], 0.0))
            for p in range(RP):
                lw, cum = m.big[:, RA + p, :], m.big[:, RC + p, :]
                step.done(nc.vector.tensor_scalar(lw, lw, -float(np.exp(-0.5)), None, ALU.mult))
                nc.vector.tensor_tensor_scan(cum, keep, lw, 0.0, ALU.mult, ALU.add).then_inc(summed, 1)
                dve.wait_ge(summed, p + 1)
                nc.vector.tensor_tensor(lw, cum, lw, ALU.subtract).then_inc(before_ready, 1)
            for p in range(RP):
                lw, cum = m.big[:, RA + p, :], m.big[:, RC + p, :]
                dve.wait_ge(exps, 3 * p + 3)
                nc.vector.scalar_tensor_tensor(lw, lw, -1.0, kk[:, p, :], ALU.mult, ALU.mult)
                nc.vector.tensor_tensor(m.big[:, RK + p, :], m.big[:, RK + p, :], cum, ALU.mult)
                nc.vector.tensor_tensor(m.big[:, RB + p, :], m.big[:, RB + p, :], cum, ALU.mult)

        @block.scalar
        def _(act):
            for p in range(RP):
                lw, cum = m.big[:, RA + p, :], m.big[:, RC + p, :]
                act.wait_ge(before_ready, p + 1)
                nc.scalar.activation(lw, lw, ACT.Exp).then_inc(exps, 1)
                nc.scalar.activation(up[:, p, :], cum, ACT.Exp).then_inc(exps, 1)
                nc.scalar.activation(cum, cum, ACT.Exp, scale=-1.0).then_inc(exps, 1)

        @block.gpsimd
        def _(pool):
            for p in range(RP):
                pool.wait_ge(exps, 3 * p + 3)
                nc.gpsimd.tensor_tensor(m.big[:, RR + p, :], m.big[:, RR + p, :], up[:, p, :], ALU.mult)
                nc.gpsimd.tensor_copy(m.pl[:, p, :], up[:, p, RL - 1:T:RL]).then_inc(scaled_r, 1)


def rwkv_scan(nc, m):
    S = new_semaphore(nc)
    turned, tok_copied = S("tok_turned"), S("tok_copied")
    mats, mats_masked = S("chunk_products"), S("chunk_products_masked")
    eyes, y1, y1_masked, ty, t_grown = S("inverse_eyes"), S("inverse_y1"), S("inverse_y1_masked"), S("inverse_ty"), S("inverse_grown")
    g_ready, g_copied, uv_ready, uv_copied = S("g_ready"), S("g_copied"), S("uv_ready"), S("uv_copied")
    u_ready, u_added, y_ready, y_copied, y_added = S("u_ready"), S("u_added"), S("y_ready"), S("y_copied"), S("y_added")
    s_ready, s_added, s_scaled = S("s_ready"), S("s_added"), S("s_scaled")
    w, t = m.wflat, m.tflat

    def heads(ap):
        return ap.rearrange("p (a b c) -> p a b c", a=RP, b=2)
    tok = [w[:, q * 512:(q + 1) * 512] for q in range(4)]
    bt, kt_, at, vt = [heads(x) for x in tok]
    mb = w[:, 2048:3072].rearrange("p (h a x) -> p h a x", h=2, a=RP)
    mk = w[:, 3072:4096].rearrange("p (h a x) -> p h a x", h=2, a=RP)
    inv, invt, y1s = w[:, 4096:4608], w[:, 4608:5120], w[:, 5120:5632]
    g_s, uv, u = t[:, 0:512], t[:, 512:1024], t[:, 1024:1536]
    wt = t[:, 1536:2048].rearrange("p (q a x) -> p q a x", q=2, a=RP)
    st = t[:, 2048:2304].rearrange("p (a v) -> p a v", a=RP)
    NPAIR = NC

    def tile64(q):
        return slice(64 * q, 64 * q + 64)

    def hx(ap, p, hh):
        return heads(ap)[:, p, hh, :]

    with nc.Block() as block:
        @block.tensor
        def _(pe):
            for i in range(NPAIR):
                tt = slice(i * P, (i + 1) * P)
                if i:
                    pe.wait_ge(y_added, 2 * i)
                    pe.wait_ge(s_scaled, 2 * i)
                for q, g in enumerate((RB, RK, RA, RV)):
                    for p in range(RP):
                        last = nc.tensor.transpose(m.ps[:, q, p * P:(p + 1) * P], m.big[:, g + p, tt], m.const("ident"))
                    last.then_inc(turned, 1)
                for q, g in enumerate((RB, RK)):
                    for hh in range(2):
                        for p in range(RP):
                            for par in range(2):
                                cols = slice(i * P + RL * par, i * P + RL * par + RL)
                                last = nc.tensor.matmul(m.ps[tile64(par), 4 + 2 * q + hh, p * P:(p + 1) * P],
                                                        m.big[tile64(hh), g + p, cols],
                                                        m.ra[tile64(hh), :, p, cols],
                                                        start=True, stop=True)
                    last.then_inc(mats, 1)
                pe.wait_ge(eyes, 2 * i + 3)
                pe.wait_ge(mats_masked, 4 * (i + 1))
                pe.wait_ge(tok_copied, 4 * (i + 1))
                for l in range(LEVELS):
                    n = LEVELS * i + l
                    if l:
                        pe.wait_ge(t_grown, 2 * n)
                    for p in range(RP):
                        for hh in range(2):
                            for par in range(2):
                                r = tile64(par)
                                last = nc.tensor.matmul(m.ps[r, 0, (2 * p + hh) * 64:(2 * p + hh + 1) * 64],
                                                        mb[r, hh, p, 64:128], hx(inv, p, hh)[r], start=True, stop=True)
                    last.then_inc(y1, 1)
                    pe.wait_ge(y1_masked, n + 1)
                    for q, (a, b) in enumerate(((invt, y1s), (y1s, invt))):
                        for p in range(RP):
                            for hh in range(2):
                                for par in range(2):
                                    r = tile64(par)
                                    last = nc.tensor.matmul(m.ps[r, 1 + q, (2 * p + hh) * 64:(2 * p + hh + 1) * 64],
                                                            hx(a, p, hh)[r], hx(b, p, hh)[r], start=True, stop=True)
                        last.then_inc(ty, 1)
                pe.wait_ge(t_grown, 2 * LEVELS * (i + 1))
                for p in range(RP):
                    for hh in range(2):
                        for par in range(2):
                            r = tile64(par)
                            last = nc.tensor.matmul(m.ps[r, 3, (2 * p + hh) * 64:(2 * p + hh + 1) * 64],
                                                    mk[r, hh, p, 64:128], vt[r, p, hh, :], start=True, stop=True)
                last.then_inc(g_ready, 1)
                for par in range(2):
                    for p in range(RP):
                        for hh in range(2):
                            r = tile64(par)
                            last = nc.tensor.matmul(m.ps[tile64(hh), 5 + par, p * 64:(p + 1) * 64],
                                                    at[r, p, hh, :], hx(invt, p, hh)[r], start=True, stop=True)
                last.then_inc(g_ready, 1)
                pe.wait_ge(g_copied, 3 * i + 1)
                for p in range(RP):
                    for hh in range(2):
                        for par in range(2):
                            r = tile64(par)
                            last = nc.tensor.matmul(m.ps[r, 4, (2 * p + hh) * 64:(2 * p + hh + 1) * 64],
                                                    hx(invt, p, hh)[r], hx(g_s, p, hh)[r], start=True, stop=True)
                last.then_inc(uv_ready, 1)
                pe.wait_ge(g_copied, 3 * i + 3)
                for par in range(2):
                    c = 2 * i + par
                    cols = slice(i * P + RL * par, i * P + RL * par + RL)
                    r = tile64(par)
                    if c:
                        pe.wait_ge(s_scaled, c)
                    else:
                        pe.wait_ge(eyes, 1)
                    for hh in range(2):
                        for p in range(RP):
                            last = nc.tensor.matmul(m.ps[r, 0 + hh, p * 64:(p + 1) * 64], wt[tile64(hh), par, p, :],
                                                    st[tile64(hh), p, :], start=True, stop=True)
                    last.then_inc(u_ready, 1)
                    if par:
                        pe.wait_ge(y_added, c)
                    for p in range(RP):
                        for hh in range(2):
                            last = nc.tensor.matmul(m.ps[tile64(hh), 2, p * 64:(p + 1) * 64], st[tile64(hh), p, :],
                                                    m.big[tile64(hh), RR + p, cols], start=True, stop=True)
                    last.then_inc(y_ready, 1)
                    pe.wait_ge(u_added, 2 * c + 2)
                    for p in range(RP):
                        for hh in range(2):
                            out = m.ps[tile64(hh), 7, p * 64:(p + 1) * 64]
                            nc.tensor.matmul(out, bt[r, p, hh, :], hx(u, p, hh)[r], start=True, stop=False)
                            last = nc.tensor.matmul(out, kt_[r, p, hh, :], vt[r, p, hh, :], start=False, stop=True)
                    last.then_inc(s_ready, 1)
                    for p in range(RP):
                        for hh in range(2):
                            out = m.ps[tile64(hh), 3, p * 64:(p + 1) * 64]
                            nc.tensor.matmul(out, hx(u, p, hh)[r], mb[r, hh, p, 0:64], start=True, stop=False)
                            last = nc.tensor.matmul(out, vt[r, p, hh, :], mk[r, hh, p, 0:64], start=False, stop=True)
                    last.then_inc(y_ready, 1)

        @block.gpsimd
        def _(pool):
            eye = m.const("eye2").unsqueeze(1).to_broadcast([P, 2 * RP, RL])
            for i in range(NPAIR):
                if i:
                    pool.wait_ge(g_ready, 2 * i)
                    pool.wait_ge(uv_ready, i)
                if i == 0:
                    nc.gpsimd.memset(t[:, 2048:2304], 0.0).then_inc(eyes, 1)
                for x in (inv, invt):
                    nc.gpsimd.tensor_copy(x.rearrange("p (a b) -> p a b", b=RL), eye).then_inc(eyes, 1)

        @block.scalar
        def _(act):
            for i in range(NPAIR):
                for q in range(4):
                    act.wait_ge(turned, 4 * i + q + 1)
                    nc.scalar.copy(tok[q], m.ps[:, q, :]).then_inc(tok_copied, 1)
                act.wait_ge(g_ready, 2 * i + 1)
                nc.scalar.copy(g_s, m.ps[:, 3, :]).then_inc(g_copied, 1)
                act.wait_ge(g_ready, 2 * i + 2)
                for par in range(2):
                    nc.scalar.copy(wt[:, par, :, :], m.ps[:, 5 + par, 0:256].rearrange("p (a x) -> p a x", a=RP)
                                   ).then_inc(g_copied, 1)
                act.wait_ge(uv_ready, i + 1)
                nc.scalar.copy(uv, m.ps[:, 4, :]).then_inc(uv_copied, 1)
                for par in range(2):
                    c = 2 * i + par
                    cols = slice(i * P + RL * par, i * P + RL * par + RL)
                    act.wait_ge(y_ready, 2 * c + 1)
                    nc.scalar.copy(m.big[:, RC:RC + 4, cols], m.ps[:, 2, 0:256].rearrange("p (a x) -> p a x", a=RP)
                                   ).then_inc(y_copied, 1)

        @block.vector
        def _(dve):
            ra = m.const("mask_ra").unsqueeze(1).to_broadcast([P, RP, P])
            for i in range(NPAIR):
                for q, dst in enumerate((mb, mk)):
                    dve.wait_ge(mats, 2 * i + q + 1)
                    for hh in range(2):
                        nc.vector.tensor_tensor(dst[:, hh], m.ps[:, 4 + 2 * q + hh, :].rearrange("p (a x) -> p a x", a=RP),
                                                ra, ALU.mult).then_inc(mats_masked, 1)
                dve.wait_ge(eyes, 2 * i + 3)
                for l in range(LEVELS):
                    n = LEVELS * i + l
                    lv = m.const("levels")[:, l * RL:(l + 1) * RL].unsqueeze(1).to_broadcast([P, 2 * RP, RL])
                    dve.wait_ge(y1, n + 1)
                    nc.vector.tensor_tensor(y1s.rearrange("p (a b) -> p a b", b=RL),
                                            m.ps[:, 0, :].rearrange("p (a b) -> p a b", b=RL), lv, ALU.mult
                                            ).then_inc(y1_masked, 1)
                    for q, x in enumerate((inv, invt)):
                        dve.wait_ge(ty, 2 * n + 2)
                        nc.vector.tensor_tensor(x, x, m.ps[:, 1 + q, :], ALU.add).then_inc(t_grown, 1)
                for par in range(2):
                    c = 2 * i + par
                    r = tile64(par)
                    cols = slice(i * P + RL * par, i * P + RL * par + RL)
                    dve.wait_ge(uv_copied, i + 1)
                    dve.wait_ge(u_ready, c + 1)
                    for hh in range(2):
                        nc.vector.tensor_tensor(heads(u)[r, :, hh, :], m.ps[r, hh, 0:256].rearrange("p (a x) -> p a x", a=RP),
                                                heads(uv)[r, :, hh, :], ALU.add).then_inc(u_added, 1)
                    dve.wait_ge(s_ready, c + 1)
                    nc.vector.tensor_tensor(st, st, m.ps[:, 7, 0:256].rearrange("p (a x) -> p a x", a=RP), ALU.add
                                            ).then_inc(s_added, 1)
                    dve.wait_ge(s_added, c + 1)
                    dve.wait_ge(y_ready, 2 * c + 1)
                    nc.vector.tensor_tensor(st, st, m.pl[:, :, c:c + 1].to_broadcast([P, RP, RL]), ALU.mult
                                            ).then_inc(s_scaled, 1)
                    dve.wait_ge(y_ready, 2 * c + 2)
                    dve.wait_ge(y_copied, c + 1)
                    y = m.big[:, RC:RC + 4, cols]
                    nc.vector.tensor_tensor(y, y, m.ps[:, 3, 0:256].rearrange("p (a x) -> p a x", a=RP), ALU.add
                                            ).then_inc(y_added, 1)


def rwkv_group_norm(nc, m):
    S = new_semaphore(nc)
    loaded, meaned, centred, squared, summed, var, rooted = [S("gn_" + x) for x in
                                                             ("bonus_loaded", "mean", "centred", "squared", "summed", "var", "rooted")]
    steps, normed, biased, done = S("gn_steps"), S("gn_normed"), S("gn_biased"), S("gn_done")
    N = 2 * RP
    unit = [(divmod(n, 2)) for n in range(N)]
    sq = [m.wflat[:, n * 512:(n + 1) * 512] for n in range(N)]
    with nc.Block() as block:
        @block.sync
        def _(sp):
            for n, (p, hf) in enumerate(unit):
                sp.dma_start(m.big[:, RA + p, half(hf)], m.d["bonus"][n]).then_inc(loaded, 16)

        @block.tensor
        def _(pe):
            for n, (p, hf) in enumerate(unit):
                nc.tensor.matmul(m.ps[:, n, :], m.const("head_ones"), m.big[:, RC + p, half(hf)],
                                 start=True, stop=True).then_inc(meaned, 1)
            for n in range(N):
                pe.wait_ge(squared, n + 1)
                nc.tensor.matmul(m.ps[:, n, :], m.const("head_ones"), sq[n], start=True, stop=True).then_inc(summed, 1)

        @block.scalar
        def _(act):
            for n, (p, hf) in enumerate(unit):
                act.wait_ge(centred, n + 1)
                nc.scalar.activation(sq[n], m.big[:, RC + p, half(hf)], ACT.Square).then_inc(squared, 1)
            for n in range(N):
                act.wait_ge(var, n + 1)
                nc.scalar.activation(m.tmp[:, n, :], m.tmp[:, n, :], ACT.Sqrt).then_inc(rooted, 1)
            for n, (p, hf) in enumerate(unit):
                act.wait_ge(normed, n + 1)
                nc.scalar.activation(m.big[:, YA + p, half(hf)], m.big[:, RC + p, half(hf)], ACT.Identity,
                                     bias=m.par("lnx_b", p), scale=m.par("lnx_g", p)).then_inc(biased, 1)

        @block.vector
        def _(dve):
            step = Steps(dve, steps)
            for n, (p, hf) in enumerate(unit):
                y = m.big[:, RC + p, half(hf)]
                dve.wait_ge(meaned, n + 1)
                nc.vector.scalar_tensor_tensor(y, m.ps[:, n, :], -1.0 / RL, y, ALU.mult, ALU.add).then_inc(centred, 1)
            for n in range(N):
                dve.wait_ge(summed, n + 1)
                nc.vector.tensor_scalar(m.tmp[:, n, :], m.ps[:, n, :], 1.0 / RL, GN_EPS, ALU.mult, ALU.add).then_inc(var, 1)
            for n, (p, hf) in enumerate(unit):
                y = m.big[:, RC + p, half(hf)]
                dve.wait_ge(rooted, n + 1)
                step.done(nc.vector.reciprocal(m.tmp[:, n, :], m.tmp[:, n, :]))
                dve.wait_ge(squared, n + 1)
                nc.vector.tensor_tensor(y, y, m.tmp[:, n, :], ALU.mult).then_inc(normed, 1)

        @block.gpsimd
        def _(pool):
            pool.wait_ge(loaded, 16 * N)
            for n, (p, hf) in enumerate(unit):
                y = m.big[:, YA + p, half(hf)]
                pool.wait_ge(biased, n + 1)
                nc.gpsimd.tensor_tensor(y, y, m.big[:, RA + p, half(hf)], ALU.add).then_inc(done, 1)


def branch_gates(nc, m):
    loaded, products, emptied = gemm_sems(nc, "z")
    silu_ready, gated = new_semaphore(nc)("z_silu_ready"), new_semaphore(nc)("z_gated")
    parts = [(m.d["w_z"], 0, KT)]
    with nc.Block() as block:
        @block.sync
        def _(sp):
            gemm_loads(sp, 8, parts, m.wbuf, loaded, products)

        @block.tensor
        def _(pe):
            gemm_products(nc, pe, 8, parts, lambda q, k, hf: m.big[:, HN + k, half(hf)],
                          m.ps, m.wbuf, loaded, products, emptied)

        @block.scalar
        def _(act):
            for hf in range(2):
                act.sem_inc(emptied[hf], 2)
            act.sem_inc(gated, 4)
            with act.Fori(0, 4) as i:
                for s in range(2):
                    for hf in range(2):
                        u = 2 * s + hf
                        act.wait_ge(products, i * 4 + (u + 1))
                        act.wait_ge(gated, i * 4 + (u + 1))
                        nc.scalar.activation(m.tmp[:, u, :], m.ps[:, u, :], ACT.Silu).then_inc(emptied[hf], 1)

        @block.vector
        def _(dve):
            with dve.Fori(0, 4) as i:
                for s in range(2):
                    for hf in range(2):
                        u = 2 * s + hf
                        y = m.big[:, i * 2 + (YB + s), half(hf)]
                        dve.wait_ge(emptied[hf], i * 2 + (s + 3))
                        nc.vector.tensor_tensor(y, y, m.tmp[:, u, :], ALU.mult).then_inc(gated, 1)


MG, RES = 16, 24


def merge(nc, m):
    loaded, products, emptied = gemm_sems(nc, "merge")
    gates_ready, added, prod = [new_semaphore(nc)("merge_" + x) for x in ("gates_ready", "added", "weighted")]
    parts = [(m.d["w_ga"], 0, KT), (m.d["w_gb"], 8, KT), (m.d["w_pa"], 16, 4), (m.d["w_pb"], 20, 4)]
    src = [HN, HN, YA, YB]
    with nc.Block() as block:
        @block.sync
        def _(sp):
            gemm_loads(sp, 8, parts, m.wbuf, loaded, products)

        @block.tensor
        def _(pe):
            gemm_products(nc, pe, 8, parts, lambda q, k, hf: m.big[:, src[q] + k, half(hf)],
                          m.ps, m.wbuf, loaded, products, emptied)

        @block.scalar
        def _(act):
            act.sem_inc(added, 2)
            with act.Fori(0, 4) as i:
                for s in range(2):
                    for hf in range(2):
                        u = 2 * s + hf
                        act.wait_ge(products, i * 4 + (u + 1))
                        act.wait_ge(added, i * 4 + (u + 1))
                        for q in range(2):
                            nc.scalar.activation(m.tmp[:, 4 * hf + q, :], m.ps[:, 2 * q + hf, :], ACT.Sigmoid
                                                 ).then_inc(gates_ready, 1)

        @block.vector
        def _(dve):
            for hf in range(2):
                dve.sem_inc(emptied[hf], 1)
            with dve.Fori(0, 4) as i:
                for s in range(2):
                    for hf in range(2):
                        u = 2 * s + hf
                        dve.wait_ge(gates_ready, i * 8 + (2 * u + 2))
                        nc.vector.tensor_tensor(m.tmp[:, 4 * hf, :], m.tmp[:, 4 * hf, :], m.ps[:, 4 + hf, :], ALU.mult
                                                ).then_inc(prod, 1)
                        nc.vector.tensor_tensor(m.tmp[:, 4 * hf + 1, :], m.tmp[:, 4 * hf + 1, :], m.ps[:, 6 + hf, :],
                                                ALU.mult).then_inc(emptied[hf], 1)

        @block.gpsimd
        def _(pool):
            with pool.Fori(0, 4) as i:
                for s in range(2):
                    for hf in range(2):
                        pool.wait_ge(emptied[hf], i * 2 + (s + 2))
                        nc.gpsimd.tensor_tensor(m.big[:, i * 2 + (MG + s), half(hf)], m.tmp[:, 4 * hf, :],
                                                m.tmp[:, 4 * hf + 1, :], ALU.add).then_inc(added, 1)


def output(nc, m):
    loaded, products, emptied = gemm_sems(nc, "w_o")
    x_loaded = new_semaphore(nc)("residual_loaded")
    parts = [(m.d["w_o"], 0, KT)]
    with nc.Block() as block:
        @block.sync
        def _(sp):
            for k in range(KT):
                sp.dma_start(m.big[:, RES + k, :], m.d["residual"][k]).then_inc(x_loaded, 16)
            gemm_loads(sp, 8, parts, m.wbuf, loaded, products)

        @block.tensor
        def _(pe):
            gemm_products(nc, pe, 8, parts, lambda q, k, hf: m.big[:, MG + k, half(hf)],
                          m.ps, m.wbuf, loaded, products, emptied)

        @block.vector
        def _(dve):
            dve.wait_ge(x_loaded, 16 * KT)
            for hf in range(2):
                dve.sem_inc(emptied[hf], 2)
            with dve.Fori(0, 4) as i:
                for s in range(2):
                    for hf in range(2):
                        dve.wait_ge(products, i * 4 + (2 * s + hf + 1))
                        nc.vector.scalar_tensor_tensor(
                            m.big[:, i * 2 + (X0 + s), half(hf)], m.ps[:, 2 * s + hf, :],
                            m.mod[:, bass.ds(i * 2 + (16 + s), 1)], m.big[:, i * 2 + (RES + s), half(hf)],
                            ALU.mult, ALU.add).then_inc(emptied[hf], 1)


INPUTS = [("xT", (KT, P, T)), ("pT", (2, P, T)), ("params", (P, NPARAM)), ("consts", (P, NCONST)),
          ("hot", (32, NDIST)), ("wqk", (8, P, 1024)), ("wv", (2, P, 4096)), ("wo", (8, P, 1024)),
          ("wgate", (P, KT * 16)), ("w_out", (8, P, 1024)), ("w_mlp", (64, P, 1024)),
          ("w_pgate", (8, P, 1024)), ("w_ple", (8, P, 256)), ("w_ada", (24, P, 1024)),
          ("w_att", (10, P, 1024)), ("w_rwkv", (13, P, 1024)), ("w_z", (8, P, 1024)),
          ("w_ga", (8, P, 1024)), ("w_gb", (8, P, 1024)), ("w_pa", (8, P, 512)), ("w_pb", (8, P, 512)),
          ("w_o", (8, P, 1024)), ("w_ukT", (P, 4, P)), ("w_uv", (P, 512)), ("w_lora", (P, 512)),
          ("rel_bias", (32, AH))]
SCRATCH = [("gates", (4, NC, MH, L)), ("ends", (64, 2)), ("mprev", (64,)), ("scan_rows", (2, 64, L)),
           ("decay", (64,)), ("bias_rows", (AH, NDIST)), ("bias_copies", (AH, P, NDIST)), ("bonus", (8, P, HALF)), ("residual", (KT, P, T))]


def build(nc, stop=None):
    m = Mem()
    m.d = {}
    for name, shape in INPUTS:
        m.d[name] = nc.dram_tensor(name, list(shape), F32, kind="ExternalInput").ap()
    for name, shape in SCRATCH:
        m.d[name] = nc.dram_tensor("scratch_" + name, list(shape), F32).ap()
    out = nc.dram_tensor("out", [KT, P, T], F32, kind="ExternalOutput").ap()

    def sb(name, shape):
        return nc.alloc_sbuf_tensor(name, shape, F32)
    m.big = sb("big", [P, 40, T])
    m.wbuf = sb("wbuf", [P, 2, 24 * P])
    m.tmp = sb("tmp", [P, 8, HALF])
    m.params = sb("par", [P, NPARAM])
    m.consts = sb("con", [P, NCONST])
    m.gcols = sb("gcols", [P, 3, 64])
    m.decay_b = sb("decay_b", [P, 64])
    m.mod, m.gain2, m.cact = sb("mod", [P, 24]), sb("gain2", [P, 8]), sb("cact", [P, 8])
    m.relfar, m.wi = sb("relfar", [P, AH]), sb("wi", [P, 8, AH])
    m.pl = sb("pl", [P, RP, 16])
    m.ps = nc.alloc_psum_tensor("ps", [P, 8, HALF], F32)
    m.wflat = m.wbuf[:].rearrange("p a b -> p (a b)")
    m.tflat = m.tmp[:].rearrange("p a b -> p (a b)")
    m.psflat = m.ps[:].rearrange("p a b -> p (a b)")
    m.ra = m.big[:].rearrange("p (g a) t -> p g a t", a=4)[:, RR // 4:RA // 4 + 1:(RA - RR) // 4]

    m.flat = lambda c, n: m.big[:, c:c + n, :].rearrange("p a b -> p (a b)")
    m.ktok = lambda c: m.flat(KTOK, 4)[:, c * 512:(c + 1) * 512]
    m.const = lambda name: m.consts[:, CCOL[name]:CCOL[name] + dict(CONSTS)[name]]
    m.par = lambda name, k: m.params[:, PCOL[name] + k:PCOL[name] + k + 1]
    m.par_at = lambda name, i: m.params[:, bass.ds(i + PCOL[name], 1)]
    m.pars = lambda name: m.params[:, PCOL[name]:PCOL[name] + dict(PARAMS)[name]]

    def by_chunk(a):
        return a.rearrange("k p t -> p k t")

    stages = [
        ("load", lambda: load_inputs(nc, m)),
        ("norm_mix", lambda: rms_norm(nc, m, "norm_mix", X0, XN, lambda k: m.par("norm_mix", k))),
        ("qk", lambda: project(nc, m, "qk", m.d["wqk"], 8, KT, XN, QK)),
        ("vg", lambda: mlstm_values_and_gates(nc, m)),
        ("o", lambda: mlstm_output_gate(nc, m)),
        ("gates", lambda: mlstm_gates(nc, m)),
        ("scan", lambda: mlstm_scan(nc, m)),
        ("head_norm", lambda: mlstm_head_norm(nc, m)),
        ("w_out", lambda: mlstm_out(nc, m)),
        ("norm_mlp", lambda: rms_norm(nc, m, "norm_mlp", X0, XN, lambda k: m.par("norm_mlp", k))),
        ("mlp", lambda: mlp(nc, m)),
        ("norm_ple", lambda: rms_norm(nc, m, "norm_ple", X0, XN, lambda k: m.par("norm_ple", k))),
        ("ple", lambda: ple(nc, m)),
        ("norm_final", lambda: rms_norm(nc, m, "norm_final", X0, X0, lambda k: m.par("norm_final", k),
                                        store=by_chunk(m.d["residual"]))),
        ("modulation", lambda: modulation(nc, m)),
        ("norm_in", lambda: rms_norm(nc, m, "norm_in", X0, HN, lambda k: m.gain2[:, k:k + 1],
                                     shift=lambda k: m.mod[:, k:k + 1])),
        ("att_in", lambda: project(nc, m, "att", m.d["w_att"], 10, KT, HN, QA)),
        ("latents", lambda: latents(nc, m)),
        ("qabs", lambda: absorbed_queries(nc, m)),
        ("attention", lambda: sparse_attention(nc, m)),
        ("rwkv_in", lambda: project(nc, m, "rwkv", m.d["w_rwkv"], 13, KT, HN, RR)),
        ("shift", lambda: shift_tokens(nc, m)),
        ("lora", lambda: rwkv_lora(nc, m)),
        ("keys", lambda: rwkv_keys(nc, m)),
        ("bonus", lambda: rwkv_bonus(nc, m)),
        ("scale", lambda: rwkv_scale(nc, m)),
        ("rscan", lambda: rwkv_scan(nc, m)),
        ("gn", lambda: rwkv_group_norm(nc, m)),
        ("z", lambda: branch_gates(nc, m)),
        ("merge", lambda: merge(nc, m)),
        ("w_o", lambda: output(nc, m)),
        ("final", lambda: rms_norm(nc, m, "final", X0, X0, lambda k: m.par("final_g", k), store=by_chunk(out))),
    ]
    IN_USE.clear()
    for name, stage in stages:
        stage()
        if name in ("ple", "qabs", "gn"):
            recycle_semaphores(nc)
        if name == stop:
            break


def layout(inp):
    def a(name):
        x = np.asarray(inp[name])
        return x

    def chunked(w):
        k, n = w.shape
        return np.ascontiguousarray(w.reshape(k // P, P, n // P, P).transpose(2, 1, 0, 3).reshape(n // P, P, k))

    def cols(v):
        return np.ascontiguousarray(v.reshape(-1, P).T)

    o = {"xT": np.ascontiguousarray(a("x")[0].T).reshape(KT, P, T),
         "pT": np.ascontiguousarray(a("p")[0, 0].T).reshape(2, P, T), "consts": constant_tile(),
         "hot": distance_buckets()}
    src = {"norm_mix": "norm_mix", "norm_mlp": "norm_mlp", "norm_ple": "norm_ple", "norm_final": "norm_final",
           "head_norm": "mlstm_head_norm", "ple_gate_b": "ple_gate_b", "c": "c_2", "ada_b": "ada_b_2",
           "norm_g": "norm_g_2", "mu": "shift_mu_2", "w0": "w0_2", "a0": "a0_2", "k_k": "k_k_2", "k_a": "k_a_2",
           "r_k": "r_k_2", "lnx_g": "lnx_g_2", "lnx_b": "lnx_b_2", "kv_norm": "kv_norm_g_2", "final_g": "final_g_2"}
    par = np.zeros((P, NPARAM), np.float32)
    for name, s in src.items():
        c = cols(a(s).reshape(-1))
        par[:, PCOL[name]:PCOL[name] + c.shape[1]] = c
    par[0:16, PCOL["b_gates"]] = a("mlstm_b_gates").reshape(-1)
    o["params"] = par
    w = a("mlstm_w_in")[0]
    o["wqk"] = chunked(w[:, 0:1024])
    o["wv"] = np.ascontiguousarray(w[:, 1024:2048].reshape(KT, P, 2, HALF).transpose(2, 1, 0, 3).reshape(2, P, 4096))
    o["wo"] = chunked(w[:, 2048:3072])
    o["wgate"] = np.ascontiguousarray(w[:, 3072:3088].reshape(KT, P, 16).transpose(1, 0, 2).reshape(P, KT * 16))
    o["w_out"] = chunked(a("mlstm_w_out")[0])
    w1, w2 = chunked(a("mlp_w1")[0]), a("mlp_w2")[0]
    o["w_mlp"] = np.concatenate([x for g in range(FF_GROUPS)
                                 for x in (w1[8 * g:8 * g + 8], chunked(w2[1024 * g:1024 * g + 1024]))])
    o["w_pgate"], o["w_ple"] = chunked(a("ple_gate_w")[0]), chunked(a("ple_w")[0])
    o["w_ada"] = chunked(a("ada_w_2")[0])
    w = a("w_in_2")[0]
    kw = np.zeros((D, P), np.float32)
    kw[:, 0:72] = w[:, 3840:3912]
    o["w_att"] = chunked(np.concatenate([w[:, 2176:2688], w[:, 3328:3840], w[:, 2688:2816], kw], axis=1))
    o["w_rwkv"] = chunked(w[:, 0:1664])
    o["w_z"] = chunked(np.concatenate([w[:, 2816:3328], w[:, 1664:2176]], axis=1))
    o["w_ga"], o["w_gb"] = chunked(w[:, 3912:4936]), chunked(w[:, 4936:5960])
    o["w_pa"], o["w_pb"], o["w_o"] = chunked(a("w_pa_2")[0]), chunked(a("w_pb_2")[0]), chunked(a("w_o_2")[0])
    o["w_ukT"] = np.ascontiguousarray(a("w_uk_2")[0].reshape(P, 4, 2, 64).transpose(2, 3, 1, 0).reshape(P, 4, P))
    o["w_uv"] = np.ascontiguousarray(a("w_uv_2")[0].reshape(P, 512))
    o["w_lora"] = np.concatenate([a("w2_2")[0], a("a2_2")[0]], axis=0)
    o["rel_bias"] = np.ascontiguousarray(a("rel_bias_2"))
    return o


def kernel(**inputs):
    import concourse.bacc as bacc
    from concourse.bass_utils import run_bass_kernel_spmd
    nc = bacc.Bacc("TRN2", target_bir_lowering=False, num_devices=1)
    build(nc)
    r = run_bass_kernel_spmd(nc, [layout(inputs)], core_ids=[0])
    return np.ascontiguousarray(r.results[0]["out"].reshape(D, T).T).reshape(1, T, D)
```

```python
import numpy as np
import concourse.bass as bass
from concourse import mybir
from concourse.alu_op_type import AluOpType as ALU

F32 = mybir.dt.float32
F32R = mybir.dt.float32r
ACT = mybir.ActivationFunctionType
AX = mybir.AxisListType.X

P = 128
T = 1024
D = 1024
HALF = 512
KT = D // P
EPS = 1e-6

MH = 4
DV = D // MH
L = 128
NC = T // L
DK_SCALE = 128 ** -0.5
FF_GROUPS = 4

RP = 4
RL = 64
LEVELS = 6
GN_EPS = 64e-5

AH = 8
TOPK = 256
FAR = -3.0e38
TAKEN = -3.4e38
CUT = -3.2e38
DROP = -1.0e30
BIG = 1.0e30
LOWEST = -3.0e38

PARAMS = [("norm_mix", 8), ("norm_mlp", 8), ("norm_ple", 8), ("norm_final", 8), ("head_norm", 8),
          ("ple_gate_b", 8), ("c", 8), ("ada_b", 24), ("norm_g", 8), ("mu", 13), ("w0", 4), ("a0", 4),
          ("k_k", 4), ("k_a", 4), ("r_k", 4), ("lnx_g", 4), ("lnx_b", 4), ("kv_norm", 1),
          ("final_g", 8), ("b_gates", 1)]
PCOL = {}
for _n, _w in PARAMS:
    PCOL[_n] = sum(w for _, w in PARAMS[:len(PCOL)])
NPARAM = sum(w for _, w in PARAMS)

CONSTS = [("ident", 128), ("ones", 128), ("head_ones", 128), ("causal", 128), ("mask_fwd", 128),
          ("mask_bwd", 128), ("mask_ra", 128), ("levels", LEVELS * RL), ("level0t", RL),
          ("eye2", RL)]
CCOL = {}
for _n, _w in CONSTS:
    CCOL[_n] = sum(w for _, w in CONSTS[:len(CCOL)])
NCONST = sum(w for _, w in CONSTS)
NDIST = 384

XIN, XH, XL = 16, 0, 8
QK, VF, OG = 16, 24, 32
VT, HSUM, KTOK, SPARE = 0, 8, 24, 28
GH, GL = 16, 24
X0, NH, NL, HH, HL = 0, 8, 16, 24, 32
XAGAIN, PH, PL_ = 8, 26, 24
ADA = list(range(24, 32)) + list(range(8, 24))
QA, QI, CKV, KW, LT, LK, KD, WUK, BW, QABS, YB = 24, 28, 32, 33, 34, 35, 36, 37, 38, 0, 28
SCORES, SCORE_LAST, HN_UNITS = 24, 32, 37
RR, RA, RK, RV, RC, RB, LORA, YA = 0, 4, 8, 12, 16, 20, 16, 24
RWKV_CHUNKS = [g + k for g in (RR, RK, RV) for k in range(4)] + [LORA]
Z, GA, GB = 0, 8, 16
YL, YH, ML, MH_, OUT, RES = 24, 32, 0, 8, 16, 24


def constant_tile():
    c = np.zeros((P, NCONST), np.float32)
    i = np.arange(P)[:, None]
    j = np.arange(P)[None, :]

    def put(name, a):
        c[:, CCOL[name]:CCOL[name] + a.shape[1]] = a
    put("ident", (i == j).astype(np.float32))
    put("ones", np.ones((P, P), np.float32))
    put("head_ones", (i // RL == j // RL).astype(np.float32))
    put("causal", np.where(j <= i, 0.0, FAR).astype(np.float32))
    put("mask_fwd", np.where(j >= i, 0.0, BIG).astype(np.float32))
    put("mask_bwd", np.where(j <= i, 0.0, BIG).astype(np.float32))
    il, t = i % RL, np.arange(RL)[None, :]
    put("mask_ra", np.concatenate([t >= il, t > il], axis=1).astype(np.float32))
    lev = []
    for n in range(LEVELS):
        b = 1 << n
        lev.append(((il // b) % 2 == 1) & (t // b == il // b - 1))
    put("eye2", (il == t).astype(np.float32))
    put("level0t", ((t % 2 == 1) & (il == t - 1)).astype(np.float32))
    put("levels", np.concatenate(lev, axis=1).astype(np.float32))
    return c


def distance_buckets():
    hot = np.zeros((32, NDIST), np.float32)
    for i in range(256):
        d = 255 - i
        if d < 16:
            b = d
        else:
            b = min(31, 16 + int(np.floor(np.log(d / 16.0) / np.log(8.0) * 16 + 1e-9)))
        hot[b, i] = 1.0
    return hot


class Steps:

    def __init__(self, eng, sem):
        self.eng, self.sem, self.n = eng, sem, 0

    def done(self, ins):
        self.n += 1
        ins.then_inc(self.sem, 1)
        self.eng.wait_ge(self.sem, self.n)


def wait_apart(eng, sem, value, passed):
    eng.wait_ge(sem, value)
    eng.sem_inc(passed, 1)


class Mem:
    pass


IN_USE = []


def new_semaphore(nc):
    def allocate(name):
        IN_USE.append(nc.alloc_semaphore(name))
        return IN_USE[-1]
    return allocate


def recycle_semaphores(nc):
    with nc.Block() as block:
        @block.gpsimd
        def _(pool):
            for s in IN_USE:
                pool.sem_clear(s)
    for s in IN_USE:
        nc.release_semaphore(s)
    IN_USE.clear()


def half(hf):
    return slice(hf * HALF, (hf + 1) * HALF)


class Stream:
    def __init__(self, nc, m, name):
        S = new_semaphore(nc)
        self.nc, self.m = nc, m
        self.loaded = [S(f"{name}_weights_loaded{q}") for q in range(2)]
        self.hi_ready = S(f"{name}_weights_hi")
        self.lo_ready = S(f"{name}_weights_lo")
        self.products = S(f"{name}_products")
        self.emptied = [S(f"{name}_emptied{q}") for q in range(2)]
        self.passed = S(f"{name}_passed")

    def loads(self, sp, weights, units, others=None):
        m = self.m

        def load(n, s):
            sp.dma_start(m.w_raw[:, s, :], weights[n]).then_inc(self.loaded[s], 16)
        for n in range(2):
            load(n, n)
        if others is not None:
            others()
        with sp.Fori(1, units // 2) as i:
            for s in range(2):
                sp.wait_ge(self.lo_ready, i * 2 + (s - 1))
                load(i * 2 + s, s)
        if units % 2:
            sp.wait_ge(self.lo_ready, units - 2)
            load(units - 1, 0)

    def hi(self, act, n, s):
        act.wait_ge(self.loaded[s], (n - s) * 8 + 16)
        act.wait_ge(self.products, n * 2)
        self.nc.scalar.copy(self.m.w_hi[:, s, :], self.m.w_raw[:, s, :]).then_inc(self.hi_ready, 1)

    def his(self, act, units):
        act.wait_ge(self.loaded[0], 16)
        self.nc.scalar.copy(self.m.w_hi[:, 0, :], self.m.w_raw[:, 0, :]).then_inc(self.hi_ready, 1)
        with act.Fori(0, (units - 1) // 2) as i:
            self.hi(act, i * 2 + 1, 1)
            self.hi(act, i * 2 + 2, 0)
        if units % 2 == 0:
            self.hi(act, units - 1, 1)

    def los(self, pool, units):
        m = self.m

        def lo(n, s):
            pool.wait_ge(self.hi_ready, n + 1)
            self.nc.gpsimd.tensor_tensor(m.w_lo[:, s, :], m.w_raw[:, s, :], m.w_hi[:, s, :].bitcast(F32),
                                         ALU.subtract).then_inc(self.lo_ready, 1)
        with pool.Fori(0, units // 2) as i:
            for s in range(2):
                lo(i * 2 + s, s)
        if units % 2:
            lo(units - 1, 0)

    def half_products(self, pe, n, s, hf, tiles):
        m, nc = self.m, self.nc
        for k, (bank, xh, xl, first, final) in enumerate(tiles):
            w = slice(k * P, (k + 1) * P)
            out = m.ps[:, bank, :]
            nc.tensor.matmul(out, m.w_hi[:, s, w], m.rounded(xh, half(hf)), start=first, stop=False)
            nc.tensor.matmul(out, m.w_hi[:, s, w], m.rounded(xl, half(hf)), start=False, stop=False)
            last = nc.tensor.matmul(out, m.w_lo[:, s, w], m.rounded(xh, half(hf)), start=False, stop=final)
        last.then_inc(self.products, 1)

    def multiply(self, pe, units, hi, lo):
        def unit(n, s):
            pe.wait_ge(self.lo_ready, n + 1)
            for hf in range(2):
                pe.wait_ge(self.emptied[hf], n + 1)
                self.half_products(pe, n, s, hf, [(2 * s + hf, hi + k, lo + k, k == 0, k == KT - 1) for k in range(KT)])
        pe.sem_inc(self.products, 2)
        with pe.Fori(0, units // 2) as i:
            for s in range(2):
                unit(i * 2 + s, s)
        if units % 2:
            unit(units - 1, 0)

    def drain(self, eng, hf, units, take, credit=2, per_unit=None):
        eng.sem_inc(self.emptied[hf], credit)

        def one(n, s):
            eng.wait_ge(self.products, n * 2 + (hf + 3))
            take(n, 2 * s + hf)
        with eng.Fori(0, units // 2) as i:
            for s in range(2):
                one(i * 2 + s, s)
        if units % 2:
            one(units - 1, 0)


def project(nc, m, name, weights, units, hi, lo, dst):
    st = Stream(nc, m, name)
    with nc.Block() as block:
        @block.sync
        def _(sp):
            st.loads(sp, weights, units)

        @block.scalar
        def _(act):
            st.his(act, units)

        @block.gpsimd
        def _(pool):
            st.los(pool, units)

        @block.tensor
        def _(pe):
            st.multiply(pe, units, hi, lo)

        @block.vector
        def _(dve):
            for hf in range(2):
                dve.sem_inc(st.emptied[hf], 2)

            def take(n, s):
                for hf in range(2):
                    dve.wait_ge(st.products, n * 2 + (hf + 3))
                    to = m.chunk(dst + n, half(hf)) if isinstance(n, int) else m.chunk(dst, half(hf), plus=n)
                    nc.vector.tensor_copy(to, m.ps[:, 2 * s + hf, :]).then_inc(st.emptied[hf], 1)
            with dve.Fori(0, KT // 2) as i:
                for s in range(2):
                    take(i * 2 + s, s)
            for n in range(KT, units):
                take(n, n % 2)


def rms_norm(nc, m, name, src, gain, dst=None, hi=None, lo=None, shift=None, store=None, ahead=None, products=None):
    S = new_semaphore(nc)
    squared, summed, variance, root, steps, scaled, hi_done, lo_done, stored = [
        S(f"{name}_{x}") for x in ("squared", "summed", "variance", "root", "steps", "scaled", "hi", "lo", "stored")]
    to = lo if dst is None else dst
    units = [divmod(n, KT) for n in range(2 * KT)]
    with nc.Block() as block:
        @block.scalar
        def _(act):
            for n, (hf, k) in enumerate(units):
                if n >= 6:
                    act.wait_ge(summed, n - 5)
                nc.scalar.activation(m.tmp[:, n % 6, :], m.chunk(src + k, half(hf)),
                                     ACT.Square).then_inc(squared, 1)
            for hf in range(2):
                act.wait_ge(variance, hf + 1)
                nc.scalar.activation(m.tmp[:, 6 + hf, :], m.tmp[:, 6 + hf, :], ACT.Sqrt).then_inc(root, 1)
            if hi is not None:
                for n, (hf, k) in enumerate(units):
                    act.wait_ge(scaled, n + 1)
                    nc.scalar.copy(m.rounded(hi + k, half(hf)), m.chunk(lo + k, half(hf))).then_inc(hi_done, 1)

        @block.tensor
        def _(pe):
            for n, (hf, k) in enumerate(units):
                pe.wait_ge(squared, n + 1)
                nc.tensor.matmul(m.ps[:, hf, :], m.const("ones"), m.tmp[:, n % 6, :],
                                 start=(k == 0), stop=(k == KT - 1)).then_inc(summed, 1)
            if products is not None:
                products(pe)

        @block.vector
        def _(dve):
            def var(hf):
                dve.wait_ge(summed, KT * (hf + 1))
                nc.vector.tensor_scalar(m.tmp[:, 6 + hf, :], m.ps[:, hf, :], 1.0 / D, EPS,
                                        ALU.mult, ALU.add).then_inc(variance, 1)
            var(0)
            for hf in range(2):
                dve.wait_ge(root, hf + 1)
                nc.vector.reciprocal(m.tmp[:, 6 + hf, :], m.tmp[:, 6 + hf, :]).then_inc(steps, 1)
                dve.wait_ge(steps, (1 + KT * (shift is not None)) * hf + 1)
                for k in range(KT):
                    y = m.chunk(to + k, half(hf))
                    ins = nc.vector.scalar_tensor_tensor(y, m.chunk(src + k, half(hf)),
                                                         gain(k), m.tmp[:, 6 + hf, :], ALU.mult, ALU.mult)
                    if shift is not None:
                        ins.then_inc(steps, 1)
                        dve.wait_ge(steps, (1 + KT) * hf + 2 + k)
                        ins = nc.vector.tensor_scalar(y, y, shift(k), None, ALU.add)
                    ins.then_inc(scaled, 1)
                    if hf == 0 and k == KT - 1:
                        var(1)
            if hi is not None:
                for n, (hf, k) in enumerate(units):
                    if hf == 1 and k % 2:
                        dve.wait_ge(hi_done, n + 1)
                        nc.vector.tensor_tensor(m.rounded(lo + k, half(hf)), m.chunk(lo + k, half(hf)),
                                                m.rounded(hi + k, half(hf)).bitcast(F32), ALU.subtract)

        @block.gpsimd
        def _(pool):
            if hi is not None:
                for n, (hf, k) in enumerate(units):
                    if hf == 1 and k % 2:
                        continue
                    pool.wait_ge(hi_done, n + 1)
                    nc.gpsimd.tensor_tensor(m.rounded(lo + k, half(hf)), m.chunk(lo + k, half(hf)),
                                            m.rounded(hi + k, half(hf)).bitcast(F32), ALU.subtract).then_inc(lo_done, 1)

        @block.sync
        def _(sp):
            if ahead is not None:
                ahead(sp)
            if store is not None:
                for n, (hf, k) in enumerate(units):
                    sp.wait_ge(scaled, n + 1)
                    sp.dma_start(store[:, k, half(hf)], m.chunk(to + k, half(hf))).then_inc(stored, 16)
                sp.wait_ge(stored, 16 * 2 * KT)


def load_inputs(nc, m):
    loaded = new_semaphore(nc)("inputs_loaded")
    sigmoid_ready, silu_ready = new_semaphore(nc)("sigmoid_ready"), new_semaphore(nc)("silu_ready")
    with nc.Block() as block:
        @block.sync
        def _(sp):
            sp.dma_start(m.params[:], m.d["params"]).then_inc(loaded, 16)
            sp.dma_start(m.consts[:], m.d["consts"]).then_inc(loaded, 16)
            for k in range(KT):
                sp.dma_start(m.chunk(XIN + k), m.d["xT"][k]).then_inc(loaded, 16)
            sp.wait_ge(loaded, 16 * (KT + 2))

        @block.scalar
        def _(act):
            act.wait_ge(loaded, 16 * (KT + 2))
            nc.scalar.activation(m.cact[:], m.pars("c"), ACT.Sigmoid).then_inc(sigmoid_ready, 1)

        @block.vector
        def _(dve):
            dve.wait_ge(sigmoid_ready, 1)
            nc.vector.tensor_tensor(m.cact[:], m.cact[:], m.pars("c"), ALU.mult).then_inc(silu_ready, 1)


def mlstm_inputs(nc, m):
    st = Stream(nc, m, "in")
    gates_stored, zero = new_semaphore(nc)("gates_stored"), new_semaphore(nc)("gates_biased")
    U = 25
    gates = m.tmp[0:16, 0:2, :]
    with nc.Block() as block:
        @block.sync
        def _(sp):
            st.loads(sp, m.d["w_in"], U)
            sp.wait_ge(zero, 2)
            for g in range(4):
                sp.dma_start(m.d["gates"][g].rearrange("c h t -> h c t"),
                             gates[4 * g:4 * g + 4].rearrange("h a (c t) -> h (a c) t", t=L)
                             ).then_inc(gates_stored, 16)
            sp.wait_ge(gates_stored, 64)

        @block.gpsimd
        def _(pool):
            st.los(pool, U)

        @block.tensor
        def _(pe):
            st.multiply(pe, U, XH, XL)

        @block.scalar
        def _(act):
            st.his(act, 17)
            def gate(n, s):
                for hf in range(2):
                    wait_apart(act, st.products, n * 2 + (hf + 3), st.passed)
                    nc.scalar.activation(m.chunk(OG, half(hf), plus=n - 17), m.ps[:, 2 * s + hf, :],
                                         ACT.Sigmoid).then_inc(st.emptied[hf], 1)
            st.hi(act, 17, 1)
            for hf in range(2):
                act.wait_ge(st.emptied[hf], 19)
            with act.Fori(0, 3) as i:
                for s in (0, 1):
                    st.hi(act, i * 2 + (18 + s), s)
                    gate(i * 2 + (17 + s), 1 - s)
            st.hi(act, 24, 0)
            gate(23, 1)
            gate(24, 0)

        @block.vector
        def _(dve):
            for hf in range(2):
                dve.sem_inc(st.emptied[hf], 2)
            for g, to in enumerate((QK, VF)):
                with dve.Fori(0, KT // 2) as i:
                    for s in range(2):
                        for hf in range(2):
                            dve.wait_ge(st.products, i * 4 + (16 * g + 2 * s + hf + 3))
                            nc.vector.tensor_copy(m.chunk(to, half(hf), plus=i * 2 + s), m.ps[:, 2 * s + hf, :]
                                                  ).then_inc(st.emptied[hf], 1)
            for hf in range(2):
                dve.wait_ge(st.products, 32 + hf + 3)
                nc.vector.tensor_scalar(gates[:, hf, :], m.ps[0:16, hf, :], m.par("b_gates", 0)[0:16],
                                        None, ALU.add).then_inc(zero, 1)
                dve.wait_ge(zero, hf + 1)
                dve.sem_inc(st.emptied[hf], 1)


def values_by_token(nc, m):
    S = new_semaphore(nc)
    turned, copied = S("values_turned"), [S(f"values_copied{q}") for q in range(2)]

    def drain(eng, q, copy):
        for n in range(q, 16, 2):
            c, f = divmod(n, 2)
            eng.wait_ge(turned, n + 1)
            copy(m.chunk(VT + c, slice(f * HALF, (f + 1) * HALF)), m.ps[:, n % 8, :]).then_inc(copied[q], 1)

    with nc.Block() as block:
        @block.tensor
        def _(pe):
            for n in range(16):
                c, f = divmod(n, 2)
                if n >= 8:
                    pe.wait_ge(copied[n % 2], (n - 8) // 2 + 1)
                for j in range(4):
                    last = nc.tensor.transpose(m.ps[:, n % 8, j * P:(j + 1) * P],
                                               m.chunk(VF + 4 * f + j, slice(c * P, (c + 1) * P)), m.const("ident"))
                last.then_inc(turned, 1)

        @block.scalar
        def _(act):
            drain(act, 0, nc.scalar.copy)

        @block.vector
        def _(dve):
            drain(dve, 1, nc.vector.tensor_copy)


def mlstm_gates(nc, m):
    rows = [m.tmp[0:64, n, 0:256] for n in range(8)]
    irow, frow = rows[0][:, 0:L], rows[0][:, L:]
    lf, e1 = rows[1][:, 0:L], rows[1][:, L:]
    b, g = rows[2][:, 0:L], rows[2][:, L:]
    cm, mx = rows[3][:, 0:L], rows[3][:, L:]
    inter, em = rows[4][:, 0:L], rows[4][:, L:]
    w, zero = rows[5][:, 0:L], rows[5][:, L:]
    ends = rows[6][:, 0:2]
    mprev = rows[6][:, 2:3]
    mlast = rows[6][:, 3:4]
    nmlast = rows[6][:, 4:5]
    decay = rows[6][:, 5:6]
    carr = rows[6][:, 16:32]
    mm = rows[6][:, 32:41]
    loaded = new_semaphore(nc)("gate_rows_loaded")
    zeroed = new_semaphore(nc)("gate_zeroed")
    dstep = new_semaphore(nc)("gate_vector_steps")
    astep = new_semaphore(nc)("gate_scalar_steps")
    abs_ready = new_semaphore(nc)("gate_log_ready")
    ends_ready = new_semaphore(nc)("gate_ends_ready")
    ends_moved = new_semaphore(nc)("gate_ends_moved")
    carried = new_semaphore(nc)("gate_carried")
    mprev_moved = new_semaphore(nc)("gate_mprev_moved")
    max_ready = new_semaphore(nc)("gate_max_ready")
    exp_ready = new_semaphore(nc)("gate_exp_ready")
    scaled = new_semaphore(nc)("gate_inter_scaled")
    rows_stored = new_semaphore(nc)("gate_rows_stored")
    turned = new_semaphore(nc)("gate_columns_turned")
    ktok_used = new_semaphore(nc)("ktok_turned")
    ktok_copied = [new_semaphore(nc)(f"ktok_copied{q}") for q in range(2)]
    dirs = [(slice(0, 32), slice(None), L - 1), (slice(32, 64), slice(None, None, -1), 0)]

    with nc.Block() as block:
        @block.sync
        def _(sp):
            for d in range(2):
                sp.dma_start(irow[32 * d:32 * d + 32], m.d["gates"][2 * d].rearrange("c h t -> (c h) t")
                             ).then_inc(loaded, 16)
                sp.dma_start(frow[32 * d:32 * d + 32], m.d["gates"][2 * d + 1].rearrange("c h t -> (c h) t")
                             ).then_inc(loaded, 16)
            sp.wait_ge(ends_ready, 4)
            sp.dma_start(m.d["ends"], ends).then_inc(ends_moved, 16)
            sp.wait_ge(ends_moved, 16)
            for d in range(2):
                for q in range(2):
                    sp.dma_start(carr[32 * d:32 * d + MH, 8 * q:8 * q + 8],
                                 m.d["ends"][32 * d:32 * d + 32, q].rearrange("(c h) -> h c", h=MH),
                                 allow_slow_non_contiguous=True).then_inc(ends_moved, 16)
            sp.wait_ge(carried, 2)
            for d in range(2):
                sp.dma_start(m.d["mprev"][32 * d:32 * d + 32].rearrange("(c h) -> h c", h=MH),
                             mm[32 * d:32 * d + MH, d:d + 8],
                             allow_slow_non_contiguous=True).then_inc(mprev_moved, 16)
            sp.wait_ge(mprev_moved, 32)
            sp.dma_start(mprev, m.d["mprev"].rearrange("(r a) -> r a", a=1)).then_inc(mprev_moved, 16)
            sp.wait_ge(max_ready, 1)
            sp.dma_start(m.d["scan_rows"][0], mx).then_inc(rows_stored, 16)
            sp.wait_ge(scaled, 1)
            sp.dma_start(m.d["scan_rows"][1], inter).then_inc(rows_stored, 16)
            sp.wait_ge(exp_ready, 4)
            sp.dma_start(m.d["decay"].rearrange("(r a) -> r a", a=1), decay).then_inc(rows_stored, 16)
            sp.wait_ge(rows_stored, 48)
            sp.dma_start(m.decay_b[:], m.d["decay"].partition_broadcast(P)).then_inc(rows_stored, 16)
            sp.wait_ge(rows_stored, 64)

        @block.gpsimd
        def _(pool):
            nc.gpsimd.memset(zero, 0.0).then_inc(zeroed, 1)
            nc.gpsimd.memset(mm, 0.0).then_inc(zeroed, 1)

        @block.scalar
        def _(act):
            step = Steps(act, astep)
            act.wait_ge(loaded, 64)
            step.done(nc.scalar.activation(e1, frow, ACT.Abs))
            step.done(nc.scalar.activation(e1, e1, ACT.Exp, scale=-1.0))
            nc.scalar.activation(e1, e1, ACT.Ln, bias=1.0).then_inc(abs_ready, 1)
            act.wait_ge(max_ready, 3)
            nc.scalar.activation(inter, mx, ACT.Exp, bias=mprev, scale=-1.0).then_inc(exp_ready, 1)
            nc.scalar.activation(em, em, ACT.Exp, scale=-1.0).then_inc(exp_ready, 1)
            nc.scalar.activation(w, g, ACT.Exp, bias=nmlast).then_inc(exp_ready, 1)
            nc.scalar.activation(decay, nmlast, ACT.Exp, bias=mprev).then_inc(exp_ready, 1)
            for c in range(1, NC, 2):
                act.wait_ge(ktok_used, c + 1)
                nc.scalar.copy(m.ktok(c), m.ps[:, c % 4, :]).then_inc(ktok_copied[c % 2], 1)

        @block.vector
        def _(dve):
            step = Steps(dve, dstep)
            dve.wait_ge(loaded, 64)
            dve.wait_ge(abs_ready, 1)
            dve.wait_ge(zeroed, 2)
            step.done(nc.vector.scalar_tensor_tensor(lf, frow, 0.0, e1, ALU.min, ALU.subtract))
            for rs, ts, _ in dirs:
                step.done(nc.vector.tensor_tensor_scan(b[rs, ts], lf[rs, ts], zero[rs], 0.0, ALU.add, ALU.add))
            step.done(nc.vector.tensor_tensor(g, irow, b, ALU.subtract))
            for rs, ts, _ in dirs:
                step.done(nc.vector.tensor_tensor_scan(cm[rs, ts], g[rs, ts], g[rs, ts], LOWEST, ALU.max, ALU.max))
            for rs, _, e in dirs:
                nc.vector.tensor_copy(ends[rs, 0:1], cm[rs, e:e + 1]).then_inc(ends_ready, 1)
                nc.vector.tensor_copy(ends[rs, 1:2], b[rs, e:e + 1]).then_inc(ends_ready, 1)
            dve.wait_ge(ends_moved, 16 * 5)
            nc.vector.tensor_tensor_scan(mm[0:MH, 1:9], carr[0:MH, 0:8], carr[0:MH, 8:16], 0.0,
                                         ALU.max, ALU.add).then_inc(carried, 1)
            nc.vector.tensor_tensor_scan(mm[32:32 + MH, 7::-1], carr[32:32 + MH, 7::-1],
                                         carr[32:32 + MH, 15:7:-1], 0.0, ALU.max, ALU.add).then_inc(carried, 1)
            dve.wait_ge(mprev_moved, 48)
            nc.vector.tensor_scalar(mx, cm, mprev, None, ALU.max).then_inc(max_ready, 1)
            step.done(nc.vector.tensor_tensor(mlast, mprev, ends[:, 0:1], ALU.max))
            nc.vector.tensor_scalar(nmlast, mlast, -1.0, None, ALU.mult).then_inc(max_ready, 1)
            nc.vector.tensor_tensor(em, b, mx, ALU.add).then_inc(max_ready, 1)
            dve.wait_ge(exp_ready, 1)
            nc.vector.tensor_scalar(inter, inter, DK_SCALE, None, ALU.mult).then_inc(scaled, 1)
            for c in range(0, NC, 2):
                dve.wait_ge(ktok_used, c + 1)
                nc.vector.tensor_copy(m.ktok(c), m.ps[:, c % 4, :]).then_inc(ktok_copied[c % 2], 1)
            dve.wait_ge(turned, 3)
            nc.vector.tensor_copy(m.gcols[:], m.ps[:, 4, 0:192].rearrange("p (a b) -> p a b", a=3)
                                  ).then_inc(dstep, 1)

        @block.tensor
        def _(pe):
            for c in range(NC):
                if c >= 4:
                    pe.wait_ge(ktok_copied[c % 2], (c - 4) // 2 + 1)
                for h in range(MH):
                    last = nc.tensor.transpose(m.ps[:, c % 4, h * P:(h + 1) * P],
                                               m.chunk(QK + MH + h, slice(c * L, (c + 1) * L)), m.const("ident"))
                last.then_inc(ktok_used, 1)
            pe.wait_ge(exp_ready, 4)
            for q, r in enumerate((g, w, em)):
                nc.tensor.transpose(m.ps[:, 4, 64 * q:64 * q + 64], r, m.const("ident")[0:64, 0:64]
                                    ).then_inc(turned, 1)


def mlstm_scan(nc, m):
    units = []
    for step in range(NC):
        units += [(0, step, step), (1, NC - 1 - step, step)]
    n_units = len(units)
    mxb = [m.tmp[:, d, :] for d in range(2)]
    intb = [m.tmp[:, 2 + d, :] for d in range(2)]
    arg = [m.tmp[:, 4 + d, :] for d in range(2)]
    prob = [m.tmp[:, 6 + d, :] for d in range(2)]
    spare = m.flat(SPARE, 4)
    wv = [spare[:, d * 1024:(d + 1) * 1024] for d in range(2)]
    qi = [spare[:, 2048 + d * 512:2048 + (d + 1) * 512] for d in range(2)]
    cst = m.wflat[:, 0:2048].rearrange("p (d h v) -> p d h v", d=2, h=MH)
    nst = m.wflat[:, 2048:2056].rearrange("p (d h) -> p d h", d=2)
    den = m.wflat[:, 2056:2060]
    nsc = m.wflat[:, 2060:2064]
    S = new_semaphore(nc)
    rows_loaded = [S(f"scan_rows_loaded{d}") for d in range(2)]
    scores_ready, arg_step, arg_ready, decay_ready = S("scores_ready"), S("arg_step"), S("arg_ready"), S("decay_ready")
    probs_ready, qi_ready, wv_ready = S("probs_ready"), S("qi_ready"), S("wv_ready")
    num_ready, state_products, h_done, state_updated = S("num_ready"), S("state_products"), S("h_done"), S("state_updated")
    zeroed, dstep = S("states_zeroed"), S("scan_vector_steps")

    def row(d, c):
        return d * 32 + c * MH

    def heads(ap, w=L):
        return ap.rearrange("p (h t) -> p h t", h=MH)

    with nc.Block() as block:
        @block.sync
        def _(sp):
            for u, (d, c, _) in enumerate(units):
                if u >= 2:
                    sp.wait_ge(arg_ready, u - 1)
                    sp.wait_ge(qi_ready, u - 1)
                for q, dst in enumerate((mxb[d], intb[d])):
                    src = m.d["scan_rows"][q, row(d, c):row(d, c) + MH].rearrange("r t -> (r t)")
                    sp.dma_start(dst, src.partition_broadcast(P)).then_inc(rows_loaded[d], 16)

        @block.gpsimd
        def _(pool):
            nc.gpsimd.memset(m.wflat[:, 0:2056], 0.0).then_inc(zeroed, 1)
            for u, (d, c, _) in enumerate(units):
                pool.wait_ge(rows_loaded[d], 32 * (u // 2 + 1))
                if u >= 2:
                    pool.wait_ge(probs_ready, u - 1)
                gcol = m.gcols[:, 0, row(d, c):row(d, c) + MH].unsqueeze(2).to_broadcast([P, MH, L])
                nc.gpsimd.tensor_tensor(heads(arg[d]), heads(mxb[d]), gcol, ALU.subtract).then_inc(arg_step, 1)
                pool.wait_ge(arg_step, u + 1)
                mask = m.const("mask_bwd" if d else "mask_fwd").unsqueeze(1).to_broadcast([P, MH, L])
                nc.gpsimd.tensor_tensor(heads(arg[d]), heads(arg[d]), mask, ALU.add).then_inc(arg_ready, 1)
                if u >= 2:
                    pool.wait_ge(num_ready, u - 1)
                nc.gpsimd.tensor_tensor(heads(qi[d]), m.chunk(QK, slice(c * L, (c + 1) * L), n=MH), heads(intb[d]),
                                        ALU.mult).then_inc(qi_ready, 1)

        @block.scalar
        def _(act):
            for u, (d, c, _) in enumerate(units):
                act.wait_ge(arg_ready, u + 1)
                nc.scalar.activation(arg[d], arg[d], ACT.Exp, scale=-1.0).then_inc(decay_ready, 1)
                if u >= 2:
                    act.wait_ge(state_products, u - 1)
                for h in range(MH):
                    r = row(d, c) + h
                    ins = nc.scalar.mul(wv[d][:, h * DV:(h + 1) * DV], m.chunk(VT + c, slice(h * DV, (h + 1) * DV)),
                                        m.gcols[:, 1, r:r + 1])
                ins.then_inc(wv_ready, 1)

        @block.tensor
        def _(pe):
            def scores(u):
                d, c, _ = units[u]
                if u >= 2:
                    pe.wait_ge(probs_ready, u - 1)
                for h in range(MH):
                    last = nc.tensor.matmul(m.ps[:, d, h * L:(h + 1) * L],
                                            m.chunk(QK + MH + h, slice(c * L, (c + 1) * L)),
                                            m.chunk(QK + h, slice(c * L, (c + 1) * L)), start=True, stop=True)
                last.then_inc(scores_ready, 1)

            pe.wait_ge(zeroed, 1)
            scores(0)
            for u, (d, c, _) in enumerate(units):
                if u + 1 < n_units:
                    scores(u + 1)
                pe.wait_ge(probs_ready, u + 1)
                pe.wait_ge(qi_ready, u + 1)
                if u >= 1:
                    pe.wait_ge(h_done, u)
                if u >= 2:
                    pe.wait_ge(state_updated, u - 1)
                for h in range(MH):
                    hs = slice(h * L, (h + 1) * L)
                    out = m.ps[:, 2 + h // 2, (h % 2) * DV:(h % 2 + 1) * DV]
                    nc.tensor.matmul(out, prob[d][:, hs], m.chunk(VT + c, slice(h * DV, (h + 1) * DV)), start=True, stop=False)
                    nc.tensor.matmul(out, qi[d][:, hs], cst[:, d, h, :], start=False, stop=True)
                    nc.tensor.matmul(m.ps[:, 6, h:h + 1], prob[d][:, hs], m.const("ones")[:, 0:1], start=True, stop=False)
                    last = nc.tensor.matmul(m.ps[:, 6, h:h + 1], qi[d][:, hs], nst[:, d, h:h + 1], start=False, stop=True)
                last.then_inc(num_ready, 1)
                pe.wait_ge(wv_ready, u + 1)
                if u >= 1:
                    pe.wait_ge(state_updated, u)
                for h in range(MH):
                    k = m.ktok(c)[:, h * L:(h + 1) * L]
                    r = row(d, c) + h
                    nc.tensor.matmul(m.ps[:, 4 + h // 2, (h % 2) * DV:(h % 2 + 1) * DV], k,
                                     wv[d][:, h * DV:(h + 1) * DV], start=True, stop=True)
                    last = nc.tensor.matmul(m.ps[:, 7, h:h + 1], k, m.gcols[:, 1, r:r + 1], start=True, stop=True)
                last.then_inc(state_products, 1)

        @block.vector
        def _(dve):
            step = Steps(dve, dstep)

            def probs(u):
                d, c, _ = units[u]
                dve.wait_ge(scores_ready, u + 1)
                dve.wait_ge(decay_ready, u + 1)
                nc.vector.scalar_tensor_tensor(prob[d], m.ps[:, d, :], DK_SCALE, arg[d], ALU.mult,
                                               ALU.mult).then_inc(probs_ready, 1)

            dve.wait_ge(zeroed, 1)
            probs(0)
            for u, (d, c, s) in enumerate(units):
                if u + 1 < n_units:
                    probs(u + 1)
                r = row(d, c)
                dve.wait_ge(num_ready, u + 1)
                step.done(nc.vector.tensor_scalar(den, m.ps[:, 6, 0:MH], -1.0, None, ALU.mult))
                step.done(nc.vector.tensor_tensor(den, den, m.ps[:, 6, 0:MH], ALU.max))
                step.done(nc.vector.tensor_tensor(den, den, m.gcols[:, 2, r:r + MH], ALU.max))
                step.done(nc.vector.reciprocal(den, den))
                for h in range(MH):
                    num = m.ps[:, 2 + h // 2, (h % 2) * DV:(h % 2 + 1) * DV]
                    out = m.chunk(HSUM + c, slice(h * DV, (h + 1) * DV))
                    if s < NC // 2:
                        ins = nc.vector.tensor_scalar(out, num, den[:, h:h + 1], None, ALU.mult)
                    else:
                        ins = nc.vector.scalar_tensor_tensor(out, num, den[:, h:h + 1], out, ALU.mult, ALU.add)
                ins.then_inc(h_done, 1)
                dve.wait_ge(state_products, u + 1)
                for h in range(MH):
                    nc.vector.scalar_tensor_tensor(cst[:, d, h, :], cst[:, d, h, :], m.decay_b[:, r + h:r + h + 1],
                                                   m.ps[:, 4 + h // 2, (h % 2) * DV:(h % 2 + 1) * DV],
                                                   ALU.mult, ALU.add)
                step.done(nc.vector.tensor_tensor(nsc, nst[:, d, :], m.decay_b[:, r:r + MH], ALU.mult))
                nc.vector.tensor_tensor(nst[:, d, :], nsc, m.ps[:, 7, 0:MH], ALU.add).then_inc(state_updated, 1)


def mlstm_head_norm(nc, m):
    S = new_semaphore(nc)
    squared, steps, rooted, normed = S("head_squared"), S("head_steps"), S("head_rooted"), S("head_normed")
    turned, gated, hi_done, lo_done = S("head_turned"), S("head_gated"), S("head_hi"), S("head_lo")
    ss = m.wflat[:, 0:32]
    with nc.Block() as block:
        @block.scalar
        def _(act):
            for c in range(NC):
                for h in range(MH):
                    n = c * MH + h
                    if n >= 16:
                        act.wait_ge(squared, n - 15)
                    nc.scalar.activation(m.tflat[:, (n % 16) * DV:(n % 16 + 1) * DV], m.chunk(HSUM + c, slice(h * DV, (h + 1) * DV)), ACT.Square,
                                         accum_out=ss[:, c * MH + h:c * MH + h + 1]).then_inc(squared, 1)
            act.wait_ge(steps, 1)
            nc.scalar.activation(ss, ss, ACT.Sqrt).then_inc(rooted, 1)
            for n in range(2 * KT):
                hf, f = divmod(n, KT)
                act.wait_ge(gated, n + 1)
                nc.scalar.copy(m.rounded(GH + f, half(hf)), m.chunk(GL + f, half(hf))).then_inc(hi_done, 1)

        @block.gpsimd
        def _(pool):
            for n in range(2 * KT):
                hf, f = divmod(n, KT)
                if hf == 1 and f % 2:
                    continue
                pool.wait_ge(hi_done, n + 1)
                nc.gpsimd.tensor_tensor(m.rounded(GL + f, half(hf)), m.chunk(GL + f, half(hf)),
                                        m.rounded(GH + f, half(hf)).bitcast(F32), ALU.subtract).then_inc(lo_done, 1)

        @block.vector
        def _(dve):
            dve.wait_ge(squared, NC * MH)
            nc.vector.tensor_scalar(ss, ss, 1.0 / DV, EPS, ALU.mult, ALU.add).then_inc(steps, 1)
            dve.wait_ge(rooted, 1)
            nc.vector.reciprocal(ss, ss).then_inc(steps, 1)
            dve.wait_ge(steps, 2)
            for c in range(NC):
                hc = m.chunk(HSUM + c).rearrange("p (h v) -> p h v", h=MH)
                nc.vector.tensor_tensor(hc, hc, ss[:, c * MH:(c + 1) * MH].unsqueeze(2).to_broadcast([P, MH, DV]),
                                        ALU.mult).then_inc(normed, 1)
            for n in range(2 * KT):
                hf, f = divmod(n, KT)
                dve.wait_ge(turned, n + 1)
                nc.vector.scalar_tensor_tensor(m.chunk(GL + f, half(hf)), m.ps[:, n % 4, :], m.par("head_norm", f),
                                               m.chunk(OG + f, half(hf)), ALU.mult, ALU.mult).then_inc(gated, 1)
            for f in range(1, KT, 2):
                dve.wait_ge(hi_done, KT + f + 1)
                nc.vector.tensor_tensor(m.rounded(GL + f, half(1)), m.chunk(GL + f, half(1)),
                                        m.rounded(GH + f, half(1)).bitcast(F32), ALU.subtract)

        @block.tensor
        def _(pe):
            for n in range(2 * KT):
                hf, f = divmod(n, KT)
                pe.wait_ge(normed, 4 * hf + 4)
                if n >= 4:
                    pe.wait_ge(gated, n - 3)
                for q in range(4):
                    last = nc.tensor.transpose(m.ps[:, n % 4, q * P:(q + 1) * P],
                                               m.chunk(HSUM + 4 * hf + q, slice(f * P, (f + 1) * P)), m.const("ident"))
                last.then_inc(turned, 1)


def add_projection(nc, m, name, weights, hi, lo, residual, at, dst, gate=None):
    st = Stream(nc, m, name)
    x_loaded = new_semaphore(nc)(f"{name}_residual_loaded")
    with nc.Block() as block:
        @block.sync
        def _(sp):
            def load_residual():
                for k in range(KT):
                    sp.dma_start(m.chunk(at + k), residual[k]).then_inc(x_loaded, 16)
            st.loads(sp, weights, KT, load_residual)

        @block.scalar
        def _(act):
            st.his(act, KT)

        @block.gpsimd
        def _(pool):
            st.los(pool, KT)

        @block.tensor
        def _(pe):
            st.multiply(pe, KT, hi, lo)

        @block.vector
        def _(dve):
            dve.wait_ge(x_loaded, 16 * KT)
            for hf in range(2):
                dve.sem_inc(st.emptied[hf], 2)
            with dve.Fori(0, KT // 2) as i:
                for s in range(2):
                    for hf in range(2):
                        dve.wait_ge(st.products, i * 4 + (2 * s + hf + 3))
                        out, x = [m.chunk(c, half(hf), plus=i * 2 + s) for c in (dst, at)]
                        if gate is None:
                            ins = nc.vector.tensor_tensor(out, m.ps[:, 2 * s + hf, :], x, ALU.add)
                        else:
                            ins = nc.vector.scalar_tensor_tensor(out, m.ps[:, 2 * s + hf, :], gate(i * 2 + s), x,
                                                                 ALU.mult, ALU.add)
                        ins.then_inc(st.emptied[hf], 1)


def mlp(nc, m):
    S = new_semaphore(nc)
    st = Stream(nc, m, "mlp")
    relu_ready, sq_ready, hid_hi, hid_lo = S("mlp_relu"), S("mlp_square"), S("mlp_hidden_hi"), S("mlp_hidden_lo")
    hid_emptied = [S(f"mlp_hidden_emptied{h}") for h in range(2)]
    down_emptied = [S(f"mlp_down_emptied{h}") for h in range(2)]
    U = 2 * KT * FF_GROUPS
    G = 2 * KT

    with nc.Block() as block:
        @block.sync
        def _(sp):
            st.loads(sp, m.d["w_mlp"], U)

        @block.tensor
        def _(pe):
            def unit(n, q, s, emptied, at, hi, lo):
                pe.wait_ge(st.lo_ready, n + 1)
                for hf in range(2):
                    pe.wait_ge(emptied[hf], q + 1)
                    st.half_products(pe, n, s, hf, [(2 * s + hf, hi + k, lo + k, k == 0, k == KT - 1) for k in range(KT)])
            pe.sem_inc(st.products, 2)
            with pe.Fori(0, FF_GROUPS) as g:
                for hf in range(2):
                    wait_apart(pe, down_emptied[hf], g * KT + 2, st.passed)
                with pe.Fori(0, KT // 2) as i:
                    for s in range(2):
                        unit(g * G + i * 2 + s, g * KT + i * 2 + s, s, hid_emptied, 0, NH, NL)
                wait_apart(pe, hid_lo, g * G + G, st.passed)
                with pe.Fori(0, KT // 2) as i:
                    for s in range(2):
                        unit(g * G + i * 2 + (s + KT), g * KT + i * 2 + s, s, down_emptied, 0, HH, HL)

        @block.scalar
        def _(act):
            for hf in range(2):
                act.sem_inc(hid_emptied[hf], 2)

            def relu(g, q, s):
                for hf in range(2):
                    wait_apart(act, st.products, g * (2 * G) + q * 2 + (hf + 3), st.passed)
                    nc.scalar.activation(m.chunk(HL, half(hf), plus=q), m.ps[:, 2 * s + hf, :], ACT.Relu
                                         ).then_inc(hid_emptied[hf], 1)
            act.wait_ge(st.loaded[0], 16)
            nc.scalar.copy(m.w_hi[:, 0, :], m.w_raw[:, 0, :]).then_inc(st.hi_ready, 1)
            with act.Fori(0, FF_GROUPS - 1) as g:
                with act.Fori(0, KT // 2) as i:
                    for s in range(2):
                        st.hi(act, g * G + i * 2 + (s + 1), 1 - s)
                        relu(g, i * 2 + s, s)
                with act.Fori(0, KT // 2) as i:
                    for s in range(2):
                        st.hi(act, g * G + i * 2 + (s + 1 + KT), 1 - s)
            g = FF_GROUPS - 1
            with act.Fori(0, KT // 2) as i:
                for s in range(2):
                    st.hi(act, i * 2 + (g * G + s + 1), 1 - s)
                    relu(g, i * 2 + s, s)
            with act.Fori(0, KT // 2 - 1) as i:
                for s in range(2):
                    st.hi(act, i * 2 + (g * G + s + 1 + KT), 1 - s)
            st.hi(act, U - 1, 1)

        @block.vector
        def _(dve):
            for hf in range(2):
                dve.sem_inc(down_emptied[hf], 2)
            with dve.Fori(0, FF_GROUPS) as g:
                with dve.Fori(0, KT // 2) as i:
                    for s in range(2):
                        for hf in range(2):
                            h = m.chunk(HL, half(hf), plus=i * 2 + s)
                            dve.wait_ge(hid_emptied[hf], g * KT + i * 2 + (s + 3))
                            nc.vector.tensor_tensor(h, h, h, ALU.mult).then_inc(sq_ready, 1)
                            dve.wait_ge(sq_ready, g * G + i * 4 + (2 * s + hf + 1))
                            nc.vector.tensor_copy(m.rounded(HH, half(hf), plus=i * 2 + s), h).then_inc(hid_hi, 1)
                with dve.Fori(0, KT // 2) as i:
                    for s in range(2):
                        for hf in range(2):
                            h = m.chunk(X0, half(hf), plus=i * 2 + s)
                            dve.wait_ge(st.products, g * (2 * G) + i * 4 + (G + 2 * s + hf + 3))
                            nc.vector.tensor_tensor(h, m.ps[:, 2 * s + hf, :], h, ALU.add
                                                    ).then_inc(down_emptied[hf], 1)

        @block.gpsimd
        def _(pool):
            def lo(n, s):
                pool.wait_ge(st.hi_ready, n + 1)
                nc.gpsimd.tensor_tensor(m.w_lo[:, s, :], m.w_raw[:, s, :], m.w_hi[:, s, :].bitcast(F32),
                                        ALU.subtract).then_inc(st.lo_ready, 1)

            def hidden_lo(pool, before, q):
                for hf in range(2):
                    pool.wait_ge(hid_hi, before + (hf + 1))
                    nc.gpsimd.tensor_tensor(m.rounded(HL, half(hf), plus=q), m.chunk(HL, half(hf), plus=q),
                                            m.rounded(HH, half(hf), plus=q).bitcast(F32), ALU.subtract).then_inc(hid_lo, 1)
            lo(0, 0)
            with pool.Fori(0, FF_GROUPS - 1) as g:
                with pool.Fori(0, KT // 2) as i:
                    for s in range(2):
                        lo(g * G + i * 2 + (s + 1), 1 - s)
                        hidden_lo(pool, g * G + i * 4 + 2 * s, i * 2 + s)
                with pool.Fori(0, KT // 2) as i:
                    for s in range(2):
                        lo(g * G + i * 2 + (s + 1 + KT), 1 - s)
            g = FF_GROUPS - 1
            with pool.Fori(0, KT // 2) as i:
                for s in range(2):
                    lo(i * 2 + (g * G + s + 1), 1 - s)
                    hidden_lo(pool, i * 4 + (g * G + 2 * s), i * 2 + s)
            with pool.Fori(0, KT // 2 - 1) as i:
                for s in range(2):
                    lo(i * 2 + (g * G + s + 1 + KT), 1 - s)
            lo(U - 1, 1)


def ple(nc, m):
    S = new_semaphore(nc)
    st = Stream(nc, m, "ple")
    ada_loaded = S("ada_first_loaded")
    p_loaded, p_hi, p_lo = S("p_loaded"), S("p_hi"), S("p_lo")
    w_loaded, w_hi, w_lo = S("ple_w_loaded"), S("ple_w_hi"), S("ple_w_lo")
    pe_products, pe_copied = S("p_products"), [S(f"p_copied{q}") for q in range(2)]
    gate_ready, gated, add_step = S("ple_gate_ready"), S("ple_gated"), S("ple_weighted")
    wr, wh, wl = 28, 30, 28
    PP = 32
    with nc.Block() as block:
        @block.sync
        def _(sp):
            for k in range(2):
                sp.dma_start(m.chunk(PL_ + k), m.d["pT"][k]).then_inc(p_loaded, 16)
                sp.dma_start(m.chunk(wr + k).rearrange("p (n j) -> p n j", n=KT),
                             m.d["w_ple"].rearrange("n p (k j) -> k p n j", k=2)[k]).then_inc(p_loaded, 16)

        @block.scalar
        def _(act):
            act.wait_ge(p_loaded, 64)
            nc.scalar.copy(m.rounded(PH, n=2), m.chunk(PL_, n=2)).then_inc(p_hi, 1)
            nc.scalar.copy(m.rounded(wh, n=2), m.chunk(wr, n=2)).then_inc(p_hi, 1)
            for n in range(0, 16, 2):
                act.wait_ge(pe_products, n + 1)
                nc.scalar.copy(m.chunk(PP + n // 2, half(0)), m.ps[:, n % 8, :]).then_inc(pe_copied[0], 1)

        @block.gpsimd
        def _(pool):
            pool.wait_ge(p_hi, 1)
            nc.gpsimd.tensor_tensor(m.rounded(PL_, n=2), m.chunk(PL_, n=2), m.rounded(PH, n=2).bitcast(F32),
                                    ALU.subtract).then_inc(p_lo, 1)

        @block.vector
        def _(dve):
            dve.wait_ge(p_hi, 2)
            nc.vector.tensor_tensor(m.rounded(wl, n=2), m.chunk(wr, n=2), m.rounded(wh, n=2).bitcast(F32),
                                    ALU.subtract).then_inc(p_lo, 1)
            for n in range(1, 16, 2):
                dve.wait_ge(pe_products, n + 1)
                nc.vector.tensor_copy(m.chunk(PP + n // 2, half(1)), m.ps[:, n % 8, :]).then_inc(pe_copied[1], 1)

        @block.tensor
        def _(pe):
            pe.wait_ge(p_lo, 2)
            for n in range(16):
                c, hf = divmod(n, 2)
                w = slice(c * P, (c + 1) * P)
                if n >= 8:
                    pe.wait_ge(pe_copied[hf], (n - 8) // 2 + 1)
                for k in range(2):
                    out = m.ps[:, n % 8, :]
                    nc.tensor.matmul(out, m.rounded(wh + k, w), m.rounded(PH + k, half(hf)), start=(k == 0), stop=False)
                    nc.tensor.matmul(out, m.rounded(wh + k, w), m.rounded(PL_ + k, half(hf)), start=False, stop=False)
                    last = nc.tensor.matmul(out, m.rounded(wl + k, w), m.rounded(PH + k, half(hf)), start=False, stop=(k == 1))
                last.then_inc(pe_products, 1)

    with nc.Block() as block:
        @block.sync
        def _(sp):
            def load_modulation():
                for n in range(KT):
                    sp.dma_start(m.chunk(ADA[n]), m.d["w_ada"][n]).then_inc(ada_loaded, 16)
            st.loads(sp, m.d["w_pgate"], KT, load_modulation)
            sp.wait_ge(ada_loaded, 16 * KT)

        @block.gpsimd
        def _(pool):
            st.los(pool, KT)

        @block.tensor
        def _(pe):
            st.multiply(pe, KT, NH, NL)

        @block.scalar
        def _(act):
            for hf in range(2):
                act.sem_inc(st.emptied[hf], 2)
            act.sem_inc(gated, 4)

            def gate(n, s):
                for hf in range(2):
                    wait_apart(act, gated, n * 2 + (hf + 1), st.passed)
                    wait_apart(act, st.products, n * 2 + (hf + 3), st.passed)
                    nc.scalar.activation(m.tmp[:, 2 * s + hf, :], m.ps[:, 2 * s + hf, :], ACT.Sigmoid,
                                         bias=m.par_at("ple_gate_b", n)).then_inc(st.emptied[hf], 1)
            act.wait_ge(st.loaded[0], 16)
            nc.scalar.copy(m.w_hi[:, 0, :], m.w_raw[:, 0, :]).then_inc(st.hi_ready, 1)
            with act.Fori(0, 3) as i:
                for s in range(2):
                    st.hi(act, i * 2 + (s + 1), 1 - s)
                    gate(i * 2 + s, s)
            st.hi(act, 7, 1)
            for n in (6, 7):
                gate(n, n % 2)

        @block.vector
        def _(dve):
            with dve.Fori(0, 4) as i:
                for s in range(2):
                    for hf in range(2):
                        u = 2 * s + hf
                        h = m.chunk(X0, half(hf), plus=i * 2 + s)
                        dve.wait_ge(st.emptied[hf], i * 2 + (s + 3))
                        nc.vector.tensor_tensor(m.tmp[:, u, :], m.tmp[:, u, :], m.chunk(PP, half(hf), plus=i * 2 + s),
                                                ALU.mult).then_inc(add_step, 1)
                        dve.wait_ge(add_step, i * 4 + (u + 1))
                        nc.vector.tensor_tensor(h, h, m.tmp[:, u, :], ALU.add).then_inc(gated, 1)


def load_modulation_ahead(nc, m):
    m.ada_loaded = new_semaphore(nc)("ada_loaded")

    def ahead(sp):
        for n in range(KT, 3 * KT):
            sp.dma_start(m.chunk(ADA[n]), m.d["w_ada"][n]).then_inc(m.ada_loaded, 16)
    return ahead


def modulation_products(nc, m, units):
    for n in units:
        for k in range(KT):
            last = nc.tensor.matmul(m.ps[0:1, 2 + n // 4, (n % 4) * P:(n % 4 + 1) * P], m.cact[:, k:k + 1],
                                    m.chunk(ADA[n], slice(k * P, (k + 1) * P)), start=(k == 0), stop=(k == KT - 1))
    return last


def modulation(nc, m):
    S = new_semaphore(nc)
    products, copied, moved, turned, steps = S("ada_products"), S("ada_row_copied"), S("ada_row_moved"), S("ada_turned"), S("ada_steps")
    row, rows = m.tflat[0:1, 0:3 * D], m.tflat[0:3 * KT, 3 * D:3 * D + P]
    with nc.Block() as block:
        @block.tensor
        def _(pe):
            pe.wait_ge(m.ada_loaded, 16 * 2 * KT)
            for q in range(2, 6):
                modulation_products(nc, m, range(4 * q, 4 * q + 4)).then_inc(products, 1)
            pe.wait_ge(moved, 16)
            nc.tensor.transpose(m.ps[:, 0, 0:3 * KT], rows, m.const("ident")[0:3 * KT, 0:3 * KT]).then_inc(turned, 1)

        @block.sync
        def _(sp):
            sp.wait_ge(copied, 6)
            sp.dma_start(rows, row).then_inc(moved, 16)

        @block.vector
        def _(dve):
            for q in range(6):
                if q >= 2:
                    dve.wait_ge(products, q - 1)
                nc.vector.tensor_copy(row[:, q * HALF:(q + 1) * HALF], m.ps[0:1, 2 + q, :]).then_inc(copied, 1)
            step = Steps(dve, steps)
            dve.wait_ge(turned, 1)
            step.done(nc.vector.tensor_tensor(m.mod[:], m.ps[:, 0, 0:3 * KT], m.pars("ada_b"), ALU.add))
            step.done(nc.vector.scalar_tensor_tensor(m.gain2[:], m.mod[:, 8:16], 1.0, m.pars("norm_g"),
                                                     ALU.add, ALU.mult))


def latents(nc, m):
    S = new_semaphore(nc)
    loaded, kd_loaded, squared, summed, variance = S("att_loaded"), S("kd_loaded"), S("ckv_squared"), S("ckv_summed"), S("ckv_var")
    root, steps, lat_ready, turned, bias_ready = S("ckv_root"), S("ckv_steps"), S("lat_ready"), S("lat_turned"), S("bias_ready")
    bias_copied, bias_stored = S("bias_copied"), S("bias_stored")
    hot = m.tmp[0:32, 6, 0:NDIST]
    relb = m.tmp[0:32, 7, 0:AH]
    brow = m.tmp[0:AH, 5, 0:NDIST]
    with nc.Block() as block:
        @block.sync
        def _(sp):
            sp.dma_start(hot, m.d["hot"]).then_inc(loaded, 16)
            sp.dma_start(relb, m.d["rel_bias"]).then_inc(loaded, 16)
            sp.dma_start(m.relfar[:], m.d["rel_bias"][31].partition_broadcast(P)).then_inc(loaded, 16)
            sp.dma_start(m.chunk(WUK, slice(0, 512)).rearrange("p (a c) -> p a c", a=4), m.d["w_ukT"]).then_inc(loaded, 16)
            sp.dma_start(m.chunk(WUK, slice(512, 1024)), m.d["w_uv"]).then_inc(loaded, 16)
            sp.dma_start(m.chunk(KD, rows=slice(0, 64)), m.chunk(KW, rows=slice(0, 64))).then_inc(kd_loaded, 16)
            sp.dma_start(m.chunk(KD, rows=slice(64, 128)), m.chunk(KW, rows=slice(0, 64))).then_inc(kd_loaded, 16)
            sp.wait_ge(bias_copied, 1)
            sp.dma_start(m.d["bias_rows"], brow).then_inc(bias_stored, 16)
            sp.wait_ge(bias_stored, 16)
            sp.dma_start(m.d["bias_copies"], m.d["bias_rows"].unsqueeze(1).to_broadcast([AH, P, NDIST])
                         ).then_inc(bias_stored, 16)
            sp.wait_ge(bias_stored, 32)
            for h in range(AH):
                src = m.d["bias_copies"][h]
                sp.dma_start(m.flat(BW, 2)[:, h * 256:(h + 1) * 256],
                             bass.AP(src.tensor, h * P * NDIST + 127, [[NDIST - 1, P], [1, 256]])).then_inc(bias_stored, 16)
            sp.wait_ge(bias_stored, 16 * (AH + 2))
            sp.wait_ge(kd_loaded, 32)
            sp.wait_ge(loaded, 80)

        @block.scalar
        def _(act):
            for hf in range(2):
                nc.scalar.activation(m.tmp[:, hf, :], m.chunk(CKV, half(hf)), ACT.Square).then_inc(squared, 1)
            act.wait_ge(bias_ready, 1)
            nc.scalar.copy(brow, m.ps[0:AH, 6, 0:NDIST]).then_inc(bias_copied, 1)
            for hf in range(2):
                act.wait_ge(variance, hf + 1)
                nc.scalar.activation(m.tmp[:, 2 + hf, :], m.tmp[:, 2 + hf, :], ACT.Sqrt).then_inc(root, 1)

        @block.tensor
        def _(pe):
            for hf in range(2):
                pe.wait_ge(squared, hf + 1)
                nc.tensor.matmul(m.ps[:, hf, :], m.const("ones"), m.tmp[:, hf, :], start=True, stop=True).then_inc(summed, 1)
            pe.wait_ge(loaded, 80)
            nc.tensor.matmul(m.ps[0:AH, 6, 0:NDIST], relb, hot, start=True, stop=True).then_inc(bias_ready, 1)
            for src, b0 in ((KW, 4), (LT, 2)):
                if src == LT:
                    pe.wait_ge(lat_ready, 2)
                for t in range(8):
                    last = nc.tensor.transpose(m.ps[:, b0 + t // 4, (t % 4) * P:(t % 4 + 1) * P],
                                               m.chunk(src, slice(t * P, (t + 1) * P)), m.const("ident"))
                last.then_inc(turned, 1)

        @block.vector
        def _(dve):
            for hf in range(2):
                dve.wait_ge(summed, hf + 1)
                nc.vector.tensor_scalar(m.tmp[:, 2 + hf, :], m.ps[:, hf, :], 1.0 / P, EPS, ALU.mult, ALU.add).then_inc(variance, 1)
            for hf in range(2):
                dve.wait_ge(root, hf + 1)
                nc.vector.reciprocal(m.tmp[:, 2 + hf, :], m.tmp[:, 2 + hf, :]).then_inc(steps, 1)
                dve.wait_ge(steps, hf + 1)
                nc.vector.scalar_tensor_tensor(m.chunk(LT, half(hf)), m.chunk(CKV, half(hf)), m.par("kv_norm", 0),
                                               m.tmp[:, 2 + hf, :], ALU.mult, ALU.mult).then_inc(lat_ready, 1)
            dve.wait_ge(turned, 1)
            for q in range(2):
                nc.vector.tensor_copy(m.wi[:, 4 * q:4 * q + 4, :],
                                      m.ps[:, 4 + q, :].rearrange("p (a b) -> p a b", a=4)[:, :, 64:64 + AH])
            dve.wait_ge(turned, 2)
            for q in range(2):
                nc.vector.tensor_copy(m.chunk(LK, half(q)), m.ps[:, 2 + q, :])


def absorbed_queries(nc, m):
    S = new_semaphore(nc)
    products, emptied = S("qabs_products"), [S(f"qabs_emptied{q}") for q in range(2)]
    zeroed, padded = S("qabs_zeroed"), S("qabs_padded")
    weights = [m.tflat[:, 512 * q:512 * q + 512] for q in range(2)]
    N = 2 * AH

    def drain(eng, q, scale):
        for n in range(q, N, 2):
            h, hf = divmod(n, 2)
            eng.wait_ge(products, n + 1)
            scale(m.chunk(QABS + h, half(hf)), m.ps[:, n % 8, :]).then_inc(emptied[q], 1)

    with nc.Block() as block:
        @block.tensor
        def _(pe):
            for n in range(N):
                h, hf = divmod(n, 2)
                if n == 0:
                    pe.wait_ge(padded, 2)
                if n >= 8:
                    pe.wait_ge(emptied[n % 2], (n - 8) // 2 + 1)
                nc.tensor.matmul(m.ps[:, n % 8, :], weights[h % 2][:, (h // 2) * P:(h // 2 + 1) * P],
                                 m.chunk(QA + h // 2, half(hf)), start=True, stop=True).then_inc(products, 1)

        @block.scalar
        def _(act):
            drain(act, 0, lambda o, i: nc.scalar.mul(o, i, 0.125))

        @block.vector
        def _(dve):
            nc.vector.memset(m.tflat[:, 0:1024], 0.0).then_inc(zeroed, 1)
            dve.wait_ge(zeroed, 1)
            for q in range(2):
                r = slice(64 * q, 64 * q + 64)
                nc.vector.tensor_copy(weights[q][r], m.chunk(WUK, slice(0, 512), rows=r)).then_inc(padded, 1)
            drain(dve, 1, lambda o, i: nc.vector.tensor_scalar(o, i, 0.125, None, ALU.mult))


def score_rows(m, b):
    n = P * (b + 1)
    if b == T // P - 1:
        return m.chunk(SCORE_LAST)
    at = sum(P * (c + 1) for c in range(2, b))
    return m.flat(SCORES, 4)[:, at:at + n]


def index_scores(nc, m):
    S = new_semaphore(nc)
    idx_ready, relu_done, relu_used, masked = S("idx_ready"), S("relu_done"), S("relu_used"), S("idx_masked")
    s = [m.wflat[:, q * 1024:(q + 1) * 1024] for q in range(4)]
    keys_ready = S("idx_keys_ready")
    keys = [m.chunk(KD), m.tflat[:, 0:1024]]
    units = [(b, h) for b in range(2, T // P) for h in range(AH)]
    with nc.Block() as block:
        @block.tensor
        def _(pe):
            for i, (b, h) in enumerate(units):
                n = P * (b + 1)
                if i == 0:
                    pe.wait_ge(keys_ready, 3)
                if i >= 4:
                    pe.wait_ge(relu_done, i - 3)
                for a in range(0, n, HALF):
                    e = min(a + HALF, n)
                    last = nc.tensor.matmul(m.psflat[:, (i % 4) * 1024 + a:(i % 4) * 1024 + e],
                                            m.chunk(QI + h // 2, slice(b * P, (b + 1) * P)), keys[h % 2][:, a:e],
                                            start=True, stop=True)
                last.then_inc(idx_ready, 1)

        @block.scalar
        def _(act):
            for i, (b, h) in enumerate(units):
                n = P * (b + 1)
                act.wait_ge(idx_ready, i + 1)
                if i >= 4:
                    act.wait_ge(relu_used, i - 3)
                nc.scalar.activation(s[i % 4][:, 0:n], m.psflat[:, (i % 4) * 1024:(i % 4) * 1024 + n], ACT.Relu
                                     ).then_inc(relu_done, 1)

        @block.vector
        def _(dve):
            nc.vector.memset(keys[1][0:64], 0.0).then_inc(keys_ready, 1)
            nc.vector.tensor_copy(keys[1][64:128], m.chunk(KD, rows=slice(64, 128))).then_inc(keys_ready, 1)
            dve.wait_ge(keys_ready, 2)
            nc.vector.memset(m.chunk(KD, rows=slice(64, 128)), 0.0).then_inc(keys_ready, 1)
            for i, (b, h) in enumerate(units):
                n = P * (b + 1)
                acc, wi = score_rows(m, b), m.wi[:, b, h:h + 1]
                dve.wait_ge(relu_done, i + 1)
                if h == 0:
                    ins = nc.vector.tensor_scalar(acc, s[i % 4][:, 0:n], wi, None, ALU.mult)
                else:
                    dve.wait_ge(relu_used, i)
                    ins = nc.vector.scalar_tensor_tensor(acc, s[i % 4][:, 0:n], wi, acc, ALU.mult, ALU.add)
                ins.then_inc(relu_used, 1)
                if h == AH - 1:
                    dve.wait_ge(relu_used, i + 1)
                    nc.vector.tensor_tensor(acc[:, n - P:n], acc[:, n - P:n], m.const("causal"), ALU.add).then_inc(masked, 1)


def select_and_project(nc, m):
    S = new_semaphore(nc)
    st = Stream(nc, m, "hn")
    topk_step, selected = S("topk_step"), S("selected")
    stored = [S(f"hn_stored{u}") for u in range(4)]
    top8 = m.gcols[:, 0, 0:8]
    ROUNDS = TOPK // 8
    with nc.Block() as block:
        @block.sync
        def _(sp):
            st.loads(sp, m.d["w_hn"], HN_UNITS)

        @block.gpsimd
        def _(pool):
            st.los(pool, HN_UNITS)

        @block.tensor
        def _(pe):
            st.multiply(pe, HN_UNITS, NH, NL)

        @block.scalar
        def _(act):
            for hf in range(2):
                act.sem_inc(st.emptied[hf], 2)
            for u in range(4):
                act.sem_inc(stored[u], 16)

            def drain(n, s, func):
                for hf in range(2):
                    u = 2 * s + hf
                    wait_apart(act, st.products, n * 2 + (hf + 3), st.passed)
                    wait_apart(act, stored[u], (n - s) * 8 + 16, st.passed)
                    nc.scalar.activation(m.tmp[:, u, :], m.ps[:, u, :], func).then_inc(st.emptied[hf], 1)
                for hf in range(2):
                    act.wait_ge(st.emptied[hf], n + 3)
                    act.dma_start(m.d["hn_out"][n, hf], m.tmp[:, 2 * s + hf, :]).then_inc(stored[2 * s + hf], 16)

            def run(first, count, func):
                s0 = first % 2
                with act.Fori(0, count // 2) as i:
                    for d in range(2):
                        st.hi(act, i * 2 + (first + d + 1), (s0 + d + 1) % 2)
                        drain(i * 2 + (first + d), (s0 + d) % 2, func)
            act.wait_ge(st.loaded[0], 16)
            nc.scalar.copy(m.w_hi[:, 0, :], m.w_raw[:, 0, :]).then_inc(st.hi_ready, 1)
            run(0, 12, ACT.Identity)
            st.hi(act, 13, 1)
            drain(12, 0, ACT.Identity)
            run(13, 8, ACT.Silu)
            run(21, 14, ACT.Sigmoid)
            st.hi(act, 36, 0)
            drain(35, 1, ACT.Sigmoid)
            drain(36, 0, ACT.Sigmoid)
            for u in range(4):
                act.wait_ge(stored[u], 16 + 16 * ((HN_UNITS + 1 - u // 2) // 2))

        @block.vector
        def _(dve):
            done = 0
            for b in range(2, T // P):
                x = score_rows(m, b)
                for r in range(ROUNDS):
                    if r:
                        dve.wait_ge(topk_step, done)
                    nc.vector.max(top8, x).then_inc(topk_step, 1)
                    dve.wait_ge(topk_step, done + 1)
                    nc.vector.match_replace(x, top8, x, TAKEN).then_inc(topk_step, 1)
                    done += 2
                dve.wait_ge(topk_step, done)
                nc.vector.tensor_scalar(x, x, CUT, DROP, ALU.is_gt, ALU.mult).then_inc(selected, 1)


def load_recurrence_input(sp, m, k, loaded):
    sp.dma_start(m.chunk(RWKV_CHUNKS[k]).rearrange("p (h t) -> p h t", h=2),
                 m.d["hn_out"][k].rearrange("h p t -> p h t")).then_inc(loaded, 16)


def sparse_attention(nc, m):
    S = new_semaphore(nc)
    rwkv_loaded = S("rwkv_loaded")
    sel_ready, biased, acc_step = S("sel_ready"), S("bias_masked"), S("far_logits")
    scores_ready, logits_done, max_ready, exp_ready = S("att_scores"), S("att_logits"), S("att_max"), S("att_exp")
    turned, pt0, pt1, pv_ready, olat_ready = S("att_turned"), S("att_pt0"), S("att_pt1"), S("att_pv"), S("att_olat")
    o_done, recip_step, o_scaled, o_turned, y_done = S("att_o"), S("att_recip"), S("att_oscaled"), S("att_oturned"), S("att_y")
    sel0 = m.wflat[:, 1152:1408]
    bsel = [m.tflat[:, 2048 * q:2048 * q + 2048].rearrange("p (h j) -> p h j", h=AH) for q in range(2)]
    bwin = m.flat(BW, 2).rearrange("p (h j) -> p h j", h=AH)
    s = [m.chunk(LORA + 1 + q) for q in range(3)]
    pt = [m.chunk(LORA + 4 + q) for q in range(3)]
    olat = [m.wflat[:, q * 128:(q + 1) * 128] for q in range(2)]
    otok = m.wflat[:, 512:1024]
    nmax, sums = [m.wflat[:, 1024 + 16 * q:1024 + 16 * q + 8] for q in range(2)], [m.wflat[:, 1064 + 16 * q:1064 + 16 * q + 8] for q in range(2)]
    recip = m.wflat[:, 1120:1128]
    bank_set = [m.psflat[:, q * 1024:(q + 1) * 1024] for q in range(2)]
    NB = T // P
    units = [(b, h) for b in range(NB) for h in range(AH)]
    wide = [0]
    for b, h in units:
        wide.append(wide[-1] + (b >= 4))

    with nc.Block() as block:
        @block.sync
        def _(sp):
            for k in range(4, 13):
                load_recurrence_input(sp, m, k, rwkv_loaded)
            sp.wait_ge(rwkv_loaded, 16 * 9)

        @block.tensor
        def _(pe):
            def scores(u):
                b, h = units[u]
                n = P * (b + 1)
                if u >= 2:
                    pe.wait_ge(logits_done, u - 1)
                for a in range(0, n, HALF):
                    e = min(a + HALF, n)
                    last = nc.tensor.matmul(bank_set[u % 2][:, a:e], m.chunk(QABS + h, slice(b * P, (b + 1) * P)),
                                            m.chunk(LT, slice(a, e)), start=True, stop=True)
                last.then_inc(scores_ready, 1)

            def turn(u):
                b, h = units[u]
                pe.wait_ge(exp_ready, u + 1)
                if u:
                    pe.wait_ge(pt0, u)
                if b >= 4 and wide[u]:
                    pe.wait_ge(pt1, wide[u])
                for kb in range(b + 1):
                    last = nc.tensor.transpose(m.ps[:, 4 + kb // 4, (kb % 4) * P:(kb % 4 + 1) * P],
                                               s[u % 3][:, kb * P:(kb + 1) * P], m.const("ident"))
                last.then_inc(turned, 1)

            def values(u):
                b, h = units[u]
                pe.wait_ge(pt0, u + 1)
                if b >= 4:
                    pe.wait_ge(pt1, wide[u + 1])
                if u:
                    pe.wait_ge(olat_ready, u)
                if h == 1 and b:
                    pe.wait_ge(y_done, b)
                for kb in range(b + 1):
                    last = nc.tensor.matmul(m.ps[:, 6, 0:P], m.chunk(LK, slice(kb * P, (kb + 1) * P)),
                                            pt[u % 3][:, kb * P:(kb + 1) * P], start=(kb == 0), stop=(kb == b))
                last.then_inc(pv_ready, 1)

            def output(u):
                b, h = units[u]
                pe.wait_ge(olat_ready, u + 1)
                if h == 0 and b:
                    pe.wait_ge(o_scaled, b)
                nc.tensor.matmul(m.ps[:, 7, h * 64:(h + 1) * 64], olat[u % 2], m.chunk(WUK, slice(512 + h * 64, 512 + (h + 1) * 64)),
                                 start=True, stop=True).then_inc(o_done, 1)

            def turn_outputs(b):
                pe.wait_ge(o_scaled, b + 1)
                pe.wait_ge(olat_ready, min(AH * (b + 1) + 1, len(units)))
                for q in range(4):
                    last = nc.tensor.transpose(m.ps[:, 6, q * P:(q + 1) * P], otok[:, q * P:(q + 1) * P], m.const("ident"))
                last.then_inc(o_turned, 1)

            N = len(units)
            scores(0)
            for u in range(N + 3):
                if u + 1 < N:
                    scores(u + 1)
                if u < N:
                    turn(u)
                if u >= 3 and units[u - 3][1] == AH - 1:
                    turn_outputs(units[u - 3][0])
                if 1 <= u <= N:
                    values(u - 1)
                if 2 <= u < N + 2:
                    output(u - 2)

        @block.scalar
        def _(act):
            def exp(u):
                b, h = units[u]
                n = P * (b + 1)
                act.wait_ge(max_ready, u + 1)
                nc.scalar.activation(s[u % 3][:, 0:n], s[u % 3][:, 0:n], ACT.Exp, bias=nmax[b % 2][:, h:h + 1],
                                     accum_out=sums[b % 2][:, h:h + 1]).then_inc(exp_ready, 1)

            def take_output(u):
                act.wait_ge(pv_ready, u + 1)
                if u >= 2:
                    act.wait_ge(o_done, u - 1)
                nc.scalar.copy(olat[u % 2], m.ps[:, 6, 0:P]).then_inc(olat_ready, 1)

            def take_block(b):
                act.wait_ge(o_turned, b + 1)
                nc.scalar.copy(m.chunk(YB, slice(b * P, (b + 1) * P), n=4),
                               m.ps[:, 6, :].rearrange("p (a t) -> p a t", a=4)).then_inc(y_done, 1)
            exp(0)
            for u, (b, h) in enumerate(units):
                act.wait_ge(turned, u + 1)
                if u >= 3:
                    act.wait_ge(pv_ready, u - 2)
                w = min(P * (b + 1), HALF)
                nc.scalar.copy(pt[u % 3][:, 0:w], m.ps[:, 4, 0:w]).then_inc(pt0, 1)
                if u >= 3 and units[u - 3][1] == AH - 1:
                    take_block(units[u - 3][0])
                if u >= 1:
                    take_output(u - 1)
                if u + 1 < len(units):
                    exp(u + 1)
            take_output(len(units) - 1)
            take_block(NB - 1)

        @block.gpsimd
        def _(pool):
            for b in range(NB):
                n, w = P * (b + 1), min(256, P * (b + 1))
                if b < 2:
                    pool.wait_ge(sel_ready, 1)
                    sel = sel0[:, 256 - n:]
                else:
                    sel = score_rows(m, b)
                    pool.wait_ge(logits_done, AH * (b - 1))
                nc.gpsimd.tensor_tensor(bsel[b % 2][:, :, 256 - w:], bwin[:, :, 256 - w:],
                                        sel[:, n - w:n].unsqueeze(1).to_broadcast([P, AH, w]), ALU.add).then_inc(biased, 1)

        @block.vector
        def _(dve):
            acc = Steps(dve, acc_step)
            rec = Steps(dve, recip_step)
            nc.vector.memset(sel0[:, 0:P], 0.0)
            nc.vector.tensor_scalar(sel0[:, P:2 * P], m.const("causal"), -1.0, DROP, ALU.is_lt, ALU.mult).then_inc(sel_ready, 1)

            def logits(u):
                b, h = units[u]
                n, w = P * (b + 1), min(256, P * (b + 1))
                if h == 0:
                    dve.wait_ge(biased, b + 1)
                dve.wait_ge(scores_ready, u + 1)
                if u >= 3:
                    dve.wait_ge(turned, u - 2)
                x, sc = s[u % 3], bank_set[u % 2]
                if n > w:
                    nc.vector.scalar_tensor_tensor(x[:, 0:n - w], sc[:, 0:n - w], m.relfar[:, h:h + 1],
                                                   score_rows(m, b)[:, 0:n - w], ALU.add, ALU.add).then_inc(acc_step, 1)
                nc.vector.tensor_tensor(x[:, n - w:n], sc[:, n - w:n], bsel[b % 2][:, h, 256 - w:], ALU.add
                                        ).then_inc(logits_done, 1)
                if n > w:
                    dve.wait_ge(acc_step, AH * (b - 2) + h + 1)
                dve.wait_ge(logits_done, u + 1)
                nc.vector.tensor_reduce(nmax[b % 2][:, h:h + 1], x[:, 0:n], AX, ALU.max, negate=True).then_inc(max_ready, 1)

            def take_far(u):
                b, h = units[u]
                if b >= 4:
                    n = P * (b + 1)
                    dve.wait_ge(turned, u + 1)
                    dve.wait_ge(pv_ready, u - 2)
                    nc.vector.tensor_copy(pt[u % 3][:, HALF:n], m.ps[:, 5, 0:n - HALF]).then_inc(pt1, 1)

            def scale(b):
                dve.wait_ge(exp_ready, AH * (b + 1))
                rec.done(nc.vector.reciprocal(recip, sums[b % 2]))
                dve.wait_ge(o_done, AH * (b + 1))
                if b >= 1:
                    dve.wait_ge(o_turned, b)
                nc.vector.tensor_tensor(otok.rearrange("p (h d) -> p h d", h=AH),
                                        m.ps[:, 7, :].rearrange("p (h d) -> p h d", h=AH),
                                        recip.unsqueeze(2).to_broadcast([P, AH, 64]), ALU.mult).then_inc(o_scaled, 1)
            logits(0)
            for u in range(len(units)):
                if u + 1 < len(units):
                    logits(u + 1)
                take_far(u)
                if u >= 2 and units[u - 2][1] == AH - 1:
                    scale(units[u - 2][0])
            scale(NB - 1)


def shift_tokens(nc, m):
    S = new_semaphore(nc)
    differed, shifted = S("shift_differed"), S("shifted")
    own_differed, tanh_done, loaded = S("shift_own_differed"), S("lora_tanh"), S("receptance_loaded")
    order = list(range(4, 13)) + list(range(4))

    def at(n):
        return m.chunk(RWKV_CHUNKS[order[n]]), m.tflat[:, (n % 4) * 1024:(n % 4 + 1) * 1024]
    with nc.Block() as block:
        @block.sync
        def _(sp):
            for k in range(4):
                load_recurrence_input(sp, m, k, loaded)

        @block.gpsimd
        def _(pool):
            for n in range(0, 13, 2):
                if n == 10:
                    pool.wait_ge(loaded, 64)
                if n >= 4:
                    pool.wait_ge(shifted, n - 3)
                p, t = at(n)
                nc.gpsimd.tensor_tensor(t[:, 1:], p[:, 0:T - 1], p[:, 1:], ALU.subtract)
                nc.gpsimd.tensor_scalar(t[:, 0:1], p[:, 0:1], -1.0, 0.0, ALU.mult, ALU.add).then_inc(differed, 1)

        @block.vector
        def _(dve):
            for n in range(13):
                p, t = at(n)
                if n % 2:
                    if n == 9:
                        dve.wait_ge(loaded, 64)
                    if n >= 4:
                        dve.wait_ge(shifted, n - 3)
                    nc.vector.tensor_tensor(t[:, 1:], p[:, 0:T - 1], p[:, 1:], ALU.subtract).then_inc(own_differed, 1)
                    nc.vector.tensor_scalar(t[:, 0:1], p[:, 0:1], -1.0, None, ALU.mult).then_inc(own_differed, 1)
                    dve.wait_ge(own_differed, n + 1)
                else:
                    dve.wait_ge(differed, n // 2 + 1)
                nc.vector.scalar_tensor_tensor(p, t, m.par("mu", order[n]), p, ALU.mult, ALU.add).then_inc(shifted, 1)

        @block.scalar
        def _(act):
            act.wait_ge(shifted, 9)
            nc.scalar.activation(m.chunk(LORA, rows=slice(0, 64)), m.chunk(LORA, rows=slice(0, 64)), ACT.Tanh).then_inc(tanh_done, 1)


def rwkv_lora(nc, m):
    S = new_semaphore(nc)
    loaded, products, emptied = S("lora_loaded"), S("lora_products"), S("lora_emptied")
    zeroed = S("lora_zeroed")
    lora_w = [m.tflat[:, 512 * q:512 * q + 512] for q in range(2)]
    with nc.Block() as block:
        @block.sync
        def _(sp):
            sp.wait_ge(zeroed, 1)
            for q in range(2):
                r = slice(64 * q, 64 * q + 64)
                sp.dma_start(lora_w[q][r], m.d["w_lora"][r]).then_inc(loaded, 16)

        @block.vector
        def _(dve):
            nc.vector.memset(m.tflat[:, 0:1024], 0.0).then_inc(zeroed, 1)

        @block.tensor
        def _(pe):
            pe.wait_ge(loaded, 32)
            for n in range(4 * RP):
                p, q, hf = n // 4, (n // 2) % 2, n % 2
                if n >= 8:
                    pe.wait_ge(emptied, n - 7)
                nc.tensor.matmul(m.ps[:, n % 8, :], lora_w[q][:, p * P:(p + 1) * P], m.chunk(LORA, half(hf)),
                                 start=True, stop=True).then_inc(products, 1)

        @block.scalar
        def _(act):
            for n in range(4 * RP):
                p, q, hf = n // 4, (n // 2) % 2, n % 2
                act.wait_ge(products, n + 1)
                nc.scalar.activation(m.chunk((RB if q else RA) + p, half(hf)), m.ps[:, n % 8, :], ACT.Sigmoid,
                                     bias=m.par("a0" if q else "w0", p)).then_inc(emptied, 1)


def rwkv_keys(nc, m):
    S = new_semaphore(nc)
    kk_raw, squared, summed, clamped, rooted = S("kk_raw"), S("kk_squared"), S("kk_summed"), S("kk_clamped"), S("kk_rooted")
    steps, scale_step, k_scaled = S("kk_steps"), S("k_scale_step"), S("k_scaled")
    kk = m.wflat[:, 0:4096].rearrange("p (a t) -> p a t", a=RP)
    N = 2 * RP
    with nc.Block() as block:
        @block.vector
        def _(dve):
            step = Steps(dve, steps)
            for p in range(RP):
                nc.vector.tensor_scalar(kk[:, p, :], m.chunk(RK + p), m.par("k_k", p), None, ALU.mult).then_inc(kk_raw, 1)
            for n in range(N):
                dve.wait_ge(summed, n + 1)
                nc.vector.tensor_scalar(m.tmp[:, n, :], m.ps[:, n, :], 1e-24, None, ALU.max).then_inc(clamped, 1)
            for n in range(N):
                p, hf = divmod(n, 2)
                dve.wait_ge(rooted, n + 1)
                step.done(nc.vector.reciprocal(m.tmp[:, n, :], m.tmp[:, n, :]))
                step.done(nc.vector.tensor_tensor(kk[:, p, half(hf)], kk[:, p, half(hf)], m.tmp[:, n, :], ALU.mult))
            dve.wait_ge(k_scaled, RP)
            for p in range(RP):
                nc.vector.tensor_tensor(m.chunk(RB + p), m.chunk(RB + p), kk[:, p, :], ALU.mult)

        @block.gpsimd
        def _(pool):
            for p in range(RP):
                t = m.chunk(RC + p)
                nc.gpsimd.tensor_scalar(t, m.chunk(RB + p), -1.0, m.par("k_a", p), ALU.add, ALU.mult).then_inc(scale_step, 1)
                pool.wait_ge(scale_step, 3 * p + 1)
                nc.gpsimd.tensor_scalar(t, t, 1.0, 1.0, ALU.add, ALU.mult).then_inc(scale_step, 1)
                pool.wait_ge(scale_step, 3 * p + 2)
                pool.wait_ge(kk_raw, RP)
                nc.gpsimd.tensor_tensor(m.chunk(RK + p), m.chunk(RK + p), t, ALU.mult).then_inc(k_scaled, 1)
                pool.sem_inc(scale_step, 1)

        @block.scalar
        def _(act):
            for n in range(N):
                p, hf = divmod(n, 2)
                act.wait_ge(kk_raw, p + 1)
                nc.scalar.activation(m.tmp[:, n, :], kk[:, p, half(hf)], ACT.Square).then_inc(squared, 1)
            for n in range(N):
                act.wait_ge(clamped, n + 1)
                nc.scalar.activation(m.tmp[:, n, :], m.tmp[:, n, :], ACT.Sqrt).then_inc(rooted, 1)

        @block.tensor
        def _(pe):
            for n in range(N):
                pe.wait_ge(squared, n + 1)
                nc.tensor.matmul(m.ps[:, n, :], m.const("head_ones"), m.tmp[:, n, :], start=True, stop=True).then_inc(summed, 1)


def rwkv_bonus(nc, m):
    S = new_semaphore(nc)
    ready, summed, weighted, stored = S("bonus_ready"), S("bonus_summed"), S("bonus_weighted"), S("bonus_stored")
    N = 2 * RP
    with nc.Block() as block:
        @block.vector
        def _(dve):
            for n in range(N):
                p, hf = divmod(n, 2)
                nc.vector.scalar_tensor_tensor(m.tmp[:, n, :], m.chunk(RR + p, half(hf)), m.par("r_k", p),
                                               m.chunk(RK + p, half(hf)), ALU.mult, ALU.mult).then_inc(ready, 1)
            for n in range(N):
                p, hf = divmod(n, 2)
                dve.wait_ge(summed, n + 1)
                nc.vector.tensor_tensor(m.tmp[:, n, :], m.ps[:, n, :], m.chunk(RV + p, half(hf)), ALU.mult
                                        ).then_inc(weighted, 1)

        @block.tensor
        def _(pe):
            for n in range(N):
                pe.wait_ge(ready, n + 1)
                nc.tensor.matmul(m.ps[:, n, :], m.const("head_ones"), m.tmp[:, n, :], start=True, stop=True).then_inc(summed, 1)

        @block.sync
        def _(sp):
            for n in range(N):
                sp.wait_ge(weighted, n + 1)
                sp.dma_start(m.d["bonus"][n], m.tmp[:, n, :]).then_inc(stored, 16)
            sp.wait_ge(stored, 16 * N)


def rwkv_scale(nc, m):
    S = new_semaphore(nc)
    steps, zeroed, summed, before_ready = S("cum_steps"), S("reset_ready"), S("cum_ready"), S("cum_before_ready")
    exps = S("decay_exps")
    scaled_r = S("r_scaled")
    kk = m.wflat[:, 0:4096].rearrange("p (a t) -> p a t", a=RP)
    keep = m.wflat[:, 4096:5120]
    up = m.tflat[:].rearrange("p (a t) -> p a t", a=RP)
    with nc.Block() as block:
        @block.vector
        def _(dve):
            step = Steps(dve, steps)
            step.done(nc.vector.memset(keep, 1.0))
            step.done(nc.vector.memset(keep[:, 0:T:RL], 0.0))
            for p in range(RP):
                lw, cum = m.chunk(RA + p), m.chunk(RC + p)
                step.done(nc.vector.tensor_scalar(lw, lw, -float(np.exp(-0.5)), None, ALU.mult))
                nc.vector.tensor_tensor_scan(cum, keep, lw, 0.0, ALU.mult, ALU.add).then_inc(summed, 1)
                dve.wait_ge(summed, p + 1)
                nc.vector.tensor_tensor(lw, cum, lw, ALU.subtract).then_inc(before_ready, 1)
            for p in range(RP):
                lw, cum = m.chunk(RA + p), m.chunk(RC + p)
                dve.wait_ge(exps, 3 * p + 3)
                nc.vector.scalar_tensor_tensor(lw, lw, -1.0, kk[:, p, :], ALU.mult, ALU.mult)
                nc.vector.tensor_tensor(m.chunk(RK + p), m.chunk(RK + p), cum, ALU.mult)
                nc.vector.tensor_tensor(m.chunk(RB + p), m.chunk(RB + p), cum, ALU.mult)

        @block.scalar
        def _(act):
            for p in range(RP):
                lw, cum = m.chunk(RA + p), m.chunk(RC + p)
                act.wait_ge(before_ready, p + 1)
                nc.scalar.activation(lw, lw, ACT.Exp).then_inc(exps, 1)
                nc.scalar.activation(up[:, p, :], cum, ACT.Exp).then_inc(exps, 1)
                nc.scalar.activation(cum, cum, ACT.Exp, scale=-1.0).then_inc(exps, 1)

        @block.gpsimd
        def _(pool):
            for p in range(RP):
                pool.wait_ge(exps, 3 * p + 3)
                nc.gpsimd.tensor_tensor(m.chunk(RR + p), m.chunk(RR + p), up[:, p, :], ALU.mult)
                nc.gpsimd.tensor_copy(m.pl[:, p, :], up[:, p, RL - 1:T:RL]).then_inc(scaled_r, 1)


def rwkv_scan(nc, m):
    S = new_semaphore(nc)
    mats, mats_masked = S("chunk_products"), S("chunk_products_masked")
    turned, tok_copied = S("tok_turned"), S("tok_copied")
    first_rows, first_cols, first_level, zero_state = S("inverse_rows0"), S("inverse_cols0"), S("inverse_level0"), S("zero_state")
    y1, y1_masked, ty, t_grown = S("inverse_y1"), S("inverse_y1_masked"), S("inverse_ty"), S("inverse_grown")
    g_ready, g_copied, wt_ready, wt_copied = S("g_ready"), S("g_copied"), S("wt_ready"), S("wt_copied")
    uv_ready, uv_copied = S("uv_ready"), S("uv_copied")
    u_ready, u_added, rs_ready, rs_copied = S("u_ready"), S("u_added"), S("rs_ready"), S("rs_copied")
    y_ready, y_added = S("y_ready"), S("y_added")
    s_ready, s_added, s_scaled = S("s_ready"), S("s_added"), S("s_scaled")
    w, t = m.wflat, m.tflat

    mb = w[:, 0:2048].rearrange("p (d h a x) -> p d h a x", d=2, h=2, a=RP)
    mk = w[:, 2048:4096].rearrange("p (d h a x) -> p d h a x", d=2, h=2, a=RP)
    wt = w[:, 4096:5120].rearrange("p (d q a x) -> p d q a x", d=2, q=2, a=RP)
    uv = w[:, 5120:6144].rearrange("p (d x) -> p d x", d=2)
    both = t[:, 0:1024].rearrange("p (q x) -> p q x", q=2)
    inv, invt = both[:, 0, :], both[:, 1, :]
    y1s, g_s, u = t[:, 1024:1536], t[:, 1536:2048], t[:, 2048:2560]
    st = t[:, 2560:2816].rearrange("p (a v) -> p a v", a=RP)
    NPAIR = NC
    GROWS = LEVELS - 1
    eye = m.const("eye2")

    def tile64(q):
        return slice(64 * q, 64 * q + 64)

    def heads(ap):
        return ap.rearrange("p (a b c) -> p a b c", a=RP, b=2)

    def hx(ap, p, hh):
        return heads(ap)[:, p, hh, :]

    def by_token(g, i, r, p, hh):
        return m.chunk(g + p, slice(i * P + 64 * hh, i * P + 64 * hh + 64), rows=r)

    def chunk_cols(c):
        return slice(RL * c, RL * c + RL)

    def cell(p, hh):
        return slice((2 * (p % 2) + hh) * 64, (2 * (p % 2) + hh + 1) * 64)

    def over_half(h):
        return [(p, hh, tile64(par)) for p in (2 * h, 2 * h + 1) for hh in range(2) for par in range(2)]

    with nc.Block() as block:
        @block.tensor
        def _(pe):
            def chunk_products(i):
                if i:
                    pe.wait_ge(uv_copied, 2 * i)
                    pe.wait_ge(wt_copied, 2 * i)
                for q, g in enumerate((RB, RK)):
                    for hh in range(2):
                        for p in range(RP):
                            for par in range(2):
                                cols = chunk_cols(2 * i + par)
                                last = nc.tensor.matmul(m.ps[tile64(par), 2 * q + hh, p * P:(p + 1) * P],
                                                        m.chunk(g + p, cols, rows=tile64(hh)),
                                                        m.ra[tile64(hh), :, p, cols], start=True, stop=True)
                        last.then_inc(mats, 1)

            def turn(i):
                for q, g in enumerate((RB, RK, RA, RV)):
                    pe.wait_ge(mats_masked, 4 * i + q + 1)
                    for p in range(RP):
                        last = nc.tensor.transpose(m.ps[:, q, p * P:(p + 1) * P],
                                                   m.chunk(g + p, slice(i * P, (i + 1) * P)), m.const("ident"))
                    last.then_inc(turned, 1)

            def level0(i):
                for h in range(2):
                    pe.wait_ge(tok_copied, 4 * i + h + 1)
                    for p, hh, r in over_half(h):
                        last = nc.tensor.matmul(m.ps[r, h, cell(p, hh)], mb[r, i % 2, hh, p, 64:128], eye[r],
                                                start=True, stop=True)
                    last.then_inc(y1, 1)

            def level(i, l):
                n = 2 * (GROWS * i + l - 1)
                if l == 1:
                    pe.wait_ge(first_level, i + 1)
                for h in range(2):
                    if l > 1:
                        pe.wait_ge(t_grown, n - 2 + h + 1)
                    for p, hh, r in over_half(h):
                        last = nc.tensor.matmul(m.ps[r, h, cell(p, hh)], mb[r, i % 2, hh, p, 64:128],
                                                hx(inv, p, hh)[r], start=True, stop=True)
                    last.then_inc(y1, 1)
                for h in range(2):
                    pe.wait_ge(y1_masked, n + h + 1)
                    if l == 1:
                        pe.wait_ge(tok_copied, 4 * i + 2 + h + 1)
                    for q, (a, b) in enumerate(((invt, y1s), (y1s, invt))):
                        if l < LEVELS - 1 or q == 1:
                            for p, hh, r in over_half(h):
                                at = 256 * q + cell(p, hh).start
                                last = nc.tensor.matmul(m.ps[r, 2 + h, at:at + 64], hx(a, p, hh)[r], hx(b, p, hh)[r],
                                                        start=True, stop=True)
                    last.then_inc(ty, 1)

            def apply_inverse(i):
                pe.wait_ge(tok_copied, 4 * (i + 1))
                for h in range(2):
                    for p, hh, r in over_half(h):
                        last = nc.tensor.matmul(m.ps[r, h, cell(p, hh)], mk[r, i % 2, hh, p, 64:128],
                                                by_token(RV, i, r, p, hh), start=True, stop=True)
                    last.then_inc(g_ready, 1)
                pe.wait_ge(t_grown, 2 * GROWS * (i + 1))
                for par in range(2):
                    for p in range(RP):
                        for hh in range(2):
                            r = tile64(par)
                            last = nc.tensor.matmul(m.ps[tile64(hh), 2 + par, p * 64:(p + 1) * 64],
                                                    by_token(RA, i, r, p, hh), hx(invt, p, hh)[r], start=True, stop=True)
                    last.then_inc(wt_ready, 1)
                for h in range(2):
                    pe.wait_ge(g_copied, 2 * i + h + 1)
                    for p, hh, r in over_half(h):
                        last = nc.tensor.matmul(m.ps[r, h, cell(p, hh)], hx(invt, p, hh)[r], hx(g_s, p, hh)[r],
                                                start=True, stop=True)
                    last.then_inc(uv_ready, 1)

            def read_state(c):
                r = tile64(c % 2)
                if c:
                    pe.wait_ge(s_scaled, c)
                    pe.wait_ge(y_added, c)
                else:
                    pe.wait_ge(zero_state, 1)
                if c % 2 == 0:
                    pe.wait_ge(wt_copied, c + 2)
                for hh in range(2):
                    for p in range(RP):
                        last = nc.tensor.matmul(m.ps[r, 4 + hh, p * 64:(p + 1) * 64], wt[tile64(hh), c // 2 % 2, c % 2, p, :],
                                                st[tile64(hh), p, :], start=True, stop=True)
                last.then_inc(u_ready, 1)
                if c:
                    pe.wait_ge(rs_copied, c)
                for p in range(RP):
                    for hh in range(2):
                        last = nc.tensor.matmul(m.ps[tile64(hh), 6, p * 64:(p + 1) * 64], st[tile64(hh), p, :],
                                                m.chunk(RR + p, chunk_cols(c), rows=tile64(hh)), start=True, stop=True)
                last.then_inc(rs_ready, 1)

            def use_u(c):
                i, r = c // 2, tile64(c % 2)
                pe.wait_ge(u_added, 2 * c + 2)
                for p in range(RP):
                    for hh in range(2):
                        out = m.ps[tile64(hh), 7, p * 64:(p + 1) * 64]
                        nc.tensor.matmul(out, by_token(RB, i, r, p, hh), hx(u, p, hh)[r], start=True, stop=False)
                        last = nc.tensor.matmul(out, by_token(RK, i, r, p, hh), by_token(RV, i, r, p, hh),
                                                start=False, stop=True)
                last.then_inc(s_ready, 1)
                for p in range(RP):
                    for hh in range(2):
                        out = m.ps[tile64(hh), 4, p * 64:(p + 1) * 64]
                        nc.tensor.matmul(out, hx(u, p, hh)[r], mb[r, i % 2, hh, p, 0:64], start=True, stop=False)
                        last = nc.tensor.matmul(out, by_token(RV, i, r, p, hh), mk[r, i % 2, hh, p, 0:64],
                                                start=False, stop=True)
                last.then_inc(y_ready, 1)

            for i in range(NPAIR):
                chunk_products(i)
                if i:
                    read_state(2 * i - 2)
                turn(i)
                level0(i)
                if i:
                    use_u(2 * i - 2)
                level(i, 1)
                if i:
                    read_state(2 * i - 1)
                level(i, 2)
                if i:
                    use_u(2 * i - 1)
                for l in range(3, LEVELS):
                    level(i, l)
                apply_inverse(i)
            for c in (2 * NPAIR - 2, 2 * NPAIR - 1):
                read_state(c)
                use_u(c)

        @block.gpsimd
        def _(pool):
            nc.gpsimd.memset(st, 0.0).then_inc(zero_state, 1)
            lv = m.const("level0t").unsqueeze(1).to_broadcast([P, RP, RL])
            for i in range(NPAIR):
                pool.wait_ge(mats_masked, 4 * i + 2)
                for hh in range(2):
                    nc.gpsimd.tensor_tensor(heads(invt)[:, :, hh, :], mb[:, i % 2, hh, :, 64:128], lv, ALU.mult
                                            ).then_inc(first_cols, 1)
                pool.wait_ge(first_cols, 2 * i + 2)
                pool.wait_ge(first_rows, 2 * i + 2)
                x = t[:, 0:1024].rearrange("p (a b) -> p a b", b=RL)
                nc.gpsimd.tensor_tensor(x, x, eye.unsqueeze(1).to_broadcast([P, 4 * RP, RL]), ALU.add
                                        ).then_inc(first_level, 1)

        @block.scalar
        def _(act):
            def by_pair(ap):
                return ap.rearrange("p (a x) -> p a x", a=RP)

            def state_output(c):
                act.wait_ge(rs_ready, c + 1)
                nc.scalar.copy(m.chunk(RC, chunk_cols(c), n=RP), by_pair(m.ps[:, 6, 0:256])).then_inc(rs_copied, 1)
            for i in range(NPAIR):
                if i:
                    state_output(2 * i - 2)
                for q, g in enumerate((RB, RK, RA, RV)):
                    act.wait_ge(turned, 4 * i + q + 1)
                    nc.scalar.copy(m.chunk(g, slice(i * P, (i + 1) * P), n=RP), by_pair(m.ps[:, q, :])).then_inc(tok_copied, 1)
                if i:
                    state_output(2 * i - 1)
                for h in range(2):
                    act.wait_ge(g_ready, 2 * i + h + 1)
                    nc.scalar.copy(g_s[:, 256 * h:256 * h + 256], m.ps[:, h, 0:256]).then_inc(g_copied, 1)
                for par in range(2):
                    act.wait_ge(wt_ready, 2 * i + par + 1)
                    nc.scalar.copy(wt[:, i % 2, par, :, :], by_pair(m.ps[:, 2 + par, 0:256])).then_inc(wt_copied, 1)
                for h in range(2):
                    act.wait_ge(uv_ready, 2 * i + h + 1)
                    nc.scalar.copy(uv[:, i % 2, 256 * h:256 * h + 256], m.ps[:, h, 0:256]).then_inc(uv_copied, 1)
            for c in (2 * NPAIR - 2, 2 * NPAIR - 1):
                state_output(c)

        @block.vector
        def _(dve):
            def by_pair(ap):
                return ap.rearrange("p (a x) -> p a x", a=RP)

            def by_head(ap):
                return ap.rearrange("p (a b) -> p a b", b=RL)

            def mask_products(i):
                ra = m.const("mask_ra").unsqueeze(1).to_broadcast([P, RP, P])
                for n, (dst, hh) in enumerate(((mb, 0), (mb, 1), (mk, 0), (mk, 1))):
                    dve.wait_ge(mats, 4 * i + n + 1)
                    nc.vector.tensor_tensor(dst[:, i % 2, hh], by_pair(m.ps[:, n, :]), ra, ALU.mult).then_inc(mats_masked, 1)

            def mask_level(i, l):
                dst, sem = (y1s, y1_masked) if l else (inv, first_rows)
                lv = m.const("levels")[:, l * RL:(l + 1) * RL].unsqueeze(1).to_broadcast([P, RP, RL])
                for h in range(2):
                    dve.wait_ge(y1, 2 * (LEVELS * i + l) + h + 1)
                    nc.vector.tensor_tensor(by_head(dst[:, 256 * h:256 * h + 256]), by_head(m.ps[:, h, 0:256]), lv, ALU.mult
                                            ).then_inc(sem, 1)

            def grow(i, l):
                q = 0 if l < LEVELS - 1 else 1
                for h in range(2):
                    dve.wait_ge(ty, 2 * (GROWS * i + l - 1) + h + 1)
                    x = both[:, q:2, 256 * h:256 * h + 256]
                    nc.vector.tensor_tensor(x, x, m.ps[:, 2 + h, 256 * q:512].rearrange("p (q x) -> p q x", q=2 - q),
                                            ALU.add).then_inc(t_grown, 1)

            def add_u(c):
                i, r = c // 2, tile64(c % 2)
                dve.wait_ge(uv_copied, 2 * i + 2)
                dve.wait_ge(u_ready, c + 1)
                for hh in range(2):
                    nc.vector.tensor_tensor(heads(u)[r, :, hh, :], by_pair(m.ps[r, 4 + hh, 0:256]),
                                            heads(uv[:, i % 2, :])[r, :, hh, :], ALU.add).then_inc(u_added, 1)

            def add_state_and_output(c):
                dve.wait_ge(s_ready, c + 1)
                nc.vector.tensor_tensor(st, st, by_pair(m.ps[:, 7, 0:256]), ALU.add).then_inc(s_added, 1)
                dve.wait_ge(s_added, c + 1)
                nc.vector.tensor_tensor(st, st, m.pl[:, :, c:c + 1].to_broadcast([P, RP, RL]), ALU.mult
                                        ).then_inc(s_scaled, 1)
                dve.wait_ge(y_ready, c + 1)
                dve.wait_ge(rs_copied, c + 1)
                y = m.chunk(RC, chunk_cols(c), n=RP)
                nc.vector.tensor_tensor(y, y, by_pair(m.ps[:, 4, 0:256]), ALU.add).then_inc(y_added, 1)

            dve.wait_ge(zero_state, 1)
            for i in range(NPAIR):
                mask_products(i)
                if i:
                    add_u(2 * i - 2)
                mask_level(i, 0)
                if i:
                    add_state_and_output(2 * i - 2)
                mask_level(i, 1)
                grow(i, 1)
                if i:
                    add_u(2 * i - 1)
                mask_level(i, 2)
                grow(i, 2)
                if i:
                    add_state_and_output(2 * i - 1)
                for l in range(3, LEVELS):
                    mask_level(i, l)
                    grow(i, l)
            for c in (2 * NPAIR - 2, 2 * NPAIR - 1):
                add_u(c)
                add_state_and_output(c)


GATES_EARLY = [4, 5, 6, 7, 12, 13, 14, 15]


def load_gate(sp, m, k, loaded):
    sp.dma_start(m.chunk(GA + k).rearrange("p (h t) -> p h t", h=2),
                 m.d["hn_out"][21 + k].rearrange("h p t -> p h t")).then_inc(loaded, 16)


def rwkv_group_norm(nc, m):
    S = new_semaphore(nc)
    loaded, meaned, centred, squared, summed, var, rooted = [S("gn_" + x) for x in
                                                             ("bonus_loaded", "mean", "centred", "squared", "summed", "var", "rooted")]
    z_loaded = S("z_loaded")
    steps, normed, biased, done = S("gn_steps"), S("gn_normed"), S("gn_biased"), S("gn_done")
    N = 2 * RP
    unit = [(divmod(n, 2)) for n in range(N)]
    sq = [m.wflat[:, n * 512:(n + 1) * 512] for n in range(N)]
    with nc.Block() as block:
        @block.sync
        def _(sp):
            for n, (p, hf) in enumerate(unit):
                sp.dma_start(m.chunk(RK + p, half(hf)), m.d["bonus"][n]).then_inc(loaded, 16)
            for k in range(KT):
                sp.dma_start(m.chunk(Z + k).rearrange("p (h t) -> p h t", h=2),
                             m.d["hn_out"][13 + k].rearrange("h p t -> p h t")).then_inc(z_loaded, 16)
            for k in GATES_EARLY:
                load_gate(sp, m, k, z_loaded)
            sp.wait_ge(z_loaded, 16 * (KT + len(GATES_EARLY)))

        @block.tensor
        def _(pe):
            for n, (p, hf) in enumerate(unit):
                nc.tensor.matmul(m.ps[:, n, :], m.const("head_ones"), m.chunk(RC + p, half(hf)),
                                 start=True, stop=True).then_inc(meaned, 1)
            for n in range(N):
                pe.wait_ge(squared, n + 1)
                nc.tensor.matmul(m.ps[:, n, :], m.const("head_ones"), sq[n], start=True, stop=True).then_inc(summed, 1)

        @block.scalar
        def _(act):
            for n, (p, hf) in enumerate(unit):
                act.wait_ge(centred, n + 1)
                nc.scalar.activation(sq[n], m.chunk(RC + p, half(hf)), ACT.Square).then_inc(squared, 1)
            for n in range(N):
                act.wait_ge(var, n + 1)
                nc.scalar.activation(m.tmp[:, n, :], m.tmp[:, n, :], ACT.Sqrt).then_inc(rooted, 1)
            for n, (p, hf) in enumerate(unit):
                act.wait_ge(normed, n + 1)
                nc.scalar.activation(m.chunk(YA + p, half(hf)), m.chunk(RC + p, half(hf)), ACT.Identity,
                                     bias=m.par("lnx_b", p), scale=m.par("lnx_g", p)).then_inc(biased, 1)

        @block.vector
        def _(dve):
            step = Steps(dve, steps)
            for n, (p, hf) in enumerate(unit):
                y = m.chunk(RC + p, half(hf))
                dve.wait_ge(meaned, n + 1)
                nc.vector.scalar_tensor_tensor(y, m.ps[:, n, :], -1.0 / RL, y, ALU.mult, ALU.add).then_inc(centred, 1)
            for n in range(N):
                dve.wait_ge(summed, n + 1)
                nc.vector.tensor_scalar(m.tmp[:, n, :], m.ps[:, n, :], 1.0 / RL, GN_EPS, ALU.mult, ALU.add).then_inc(var, 1)
            for n, (p, hf) in enumerate(unit):
                y = m.chunk(RC + p, half(hf))
                dve.wait_ge(rooted, n + 1)
                step.done(nc.vector.reciprocal(m.tmp[:, n, :], m.tmp[:, n, :]))
                dve.wait_ge(squared, n + 1)
                nc.vector.tensor_tensor(y, y, m.tmp[:, n, :], ALU.mult).then_inc(normed, 1)

        @block.gpsimd
        def _(pool):
            pool.wait_ge(loaded, 16 * N)
            for n, (p, hf) in enumerate(unit):
                y = m.chunk(YA + p, half(hf))
                pool.wait_ge(biased, n + 1)
                nc.gpsimd.tensor_tensor(y, y, m.chunk(RK + p, half(hf)), ALU.add).then_inc(done, 1)


def branch_gates(nc, m):
    S = new_semaphore(nc)
    g_loaded, gated, hi_done, lo_done = S("g_loaded"), S("branches_gated"), S("branches_hi"), S("branches_lo")
    with nc.Block() as block:
        @block.sync
        def _(sp):
            for k in range(2 * KT):
                if k not in GATES_EARLY:
                    load_gate(sp, m, k, g_loaded)
            sp.wait_ge(g_loaded, 16 * (2 * KT - len(GATES_EARLY)))

        @block.vector
        def _(dve):
            for k in range(KT):
                y = m.chunk(YL + k)
                nc.vector.tensor_tensor(y, y, m.chunk(Z + k), ALU.mult).then_inc(gated, 1)
            for k in range(1, KT, 2):
                dve.wait_ge(hi_done, k + 1)
                nc.vector.tensor_tensor(m.rounded(YL + k), m.chunk(YL + k), m.rounded(YH + k).bitcast(F32), ALU.subtract)

        @block.scalar
        def _(act):
            for k in range(KT):
                act.wait_ge(gated, k + 1)
                nc.scalar.copy(m.rounded(YH + k), m.chunk(YL + k)).then_inc(hi_done, 1)

        @block.gpsimd
        def _(pool):
            for k in range(0, KT, 2):
                pool.wait_ge(hi_done, k + 1)
                nc.gpsimd.tensor_tensor(m.rounded(YL + k), m.chunk(YL + k), m.rounded(YH + k).bitcast(F32), ALU.subtract
                                        ).then_inc(lo_done, 1)


def merge(nc, m):
    S = new_semaphore(nc)
    st = Stream(nc, m, "merge")
    weighted, merged, hi_done, lo_done = S("merge_weighted"), S("merged"), S("merged_hi"), S("merged_lo")
    with nc.Block() as block:
        @block.sync
        def _(sp):
            st.loads(sp, m.d["w_pab"], KT)

        @block.scalar
        def _(act):
            st.his(act, KT)

        @block.tensor
        def _(pe):
            pe.sem_inc(st.products, 2)
            with pe.Fori(0, KT // 2) as i:
                for s in range(2):
                    n = i * 2 + s
                    pe.wait_ge(st.lo_ready, n + 1)
                    for hf in range(2):
                        pe.wait_ge(st.emptied[hf], n + 1)
                        st.half_products(pe, n, s, hf, [(4 * s + 2 * hf + k // 4, YH + k, YL + k, k % 4 == 0, k % 4 == 3)
                                                        for k in range(KT)])

        @block.vector
        def _(dve):
            for hf in range(2):
                dve.sem_inc(st.emptied[hf], 2)
            with dve.Fori(0, KT // 2) as i:
                for s in range(2):
                    for hf in range(2):
                        u, bank = 2 * s + hf, 4 * s + 2 * hf
                        dve.wait_ge(st.products, i * 4 + (u + 3))
                        nc.vector.tensor_tensor(m.tmp[:, 2 * u, :], m.ps[:, bank, :], m.chunk(GA, half(hf), plus=i * 2 + s),
                                                ALU.mult).then_inc(weighted, 1)
                        nc.vector.tensor_tensor(m.tmp[:, 2 * u + 1, :], m.ps[:, bank + 1, :],
                                                m.chunk(GB, half(hf), plus=i * 2 + s), ALU.mult).then_inc(st.emptied[hf], 1)
                        dve.wait_ge(weighted, i * 4 + (u + 1))
                        wait_apart(dve, st.emptied[hf], i * 2 + (s + 3), st.passed)
                        y = m.chunk(ML, half(hf), plus=i * 2 + s)
                        nc.vector.tensor_tensor(y, m.tmp[:, 2 * u, :], m.tmp[:, 2 * u + 1, :], ALU.add).then_inc(merged, 1)
                        wait_apart(dve, merged, i * 4 + (u + 1), st.passed)
                        nc.vector.tensor_copy(m.rounded(MH_, half(hf), plus=i * 2 + s), y).then_inc(hi_done, 1)

        @block.gpsimd
        def _(pool):
            def merged_lo(before, q):
                for hf in range(2):
                    pool.wait_ge(hi_done, before + (hf + 1))
                    nc.gpsimd.tensor_tensor(m.rounded(ML, half(hf), plus=q), m.chunk(ML, half(hf), plus=q),
                                            m.rounded(MH_, half(hf), plus=q).bitcast(F32), ALU.subtract).then_inc(lo_done, 1)

            def weights_lo(n, s):
                pool.wait_ge(st.hi_ready, n + 1)
                nc.gpsimd.tensor_tensor(m.w_lo[:, s, :], m.w_raw[:, s, :], m.w_hi[:, s, :].bitcast(F32),
                                        ALU.subtract).then_inc(st.lo_ready, 1)
            weights_lo(0, 0)
            weights_lo(1, 1)
            with pool.Fori(0, KT // 2 - 1) as i:
                for s in range(2):
                    weights_lo(i * 2 + (s + 2), s)
                    merged_lo(i * 4 + 2 * s, i * 2 + s)
            for n in (KT - 2, KT - 1):
                merged_lo(2 * n, n)


INPUTS = [("xT", (KT, P, T)), ("pT", (2, P, T)), ("params", (P, NPARAM)), ("consts", (P, NCONST)),
          ("hot", (32, NDIST)), ("w_in", (25, P, 1024)), ("w_out", (8, P, 1024)), ("w_mlp", (64, P, 1024)),
          ("w_pgate", (8, P, 1024)), ("w_ple", (8, P, 256)), ("w_ada", (24, P, 1024)),
          ("w_att", (10, P, 1024)), ("w_hn", (HN_UNITS, P, 1024)), ("w_pab", (8, P, 1024)),
          ("w_o", (8, P, 1024)), ("w_ukT", (P, 4, P)), ("w_uv", (P, 512)), ("w_lora", (P, 512)),
          ("rel_bias", (32, AH))]
SCRATCH = [("gates", (4, NC, MH, L)), ("ends", (64, 2)), ("mprev", (64,)), ("scan_rows", (2, 64, L)),
           ("decay", (64,)), ("bias_rows", (AH, NDIST)), ("bias_copies", (AH, P, NDIST)), ("bonus", (8, P, HALF)), ("residual", (KT, P, T)),
           ("hn_out", (HN_UNITS, 2, P, HALF))]


def build(nc, stop=None):
    m = Mem()
    m.d = {}
    for name, shape in INPUTS:
        m.d[name] = nc.dram_tensor(name, list(shape), F32, kind="ExternalInput").ap()
    for name, shape in SCRATCH:
        m.d[name] = nc.dram_tensor("scratch_" + name, list(shape), F32).ap()
    out = nc.dram_tensor("out", [KT, P, T], F32, kind="ExternalOutput").ap()

    def sb(name, shape):
        return nc.alloc_sbuf_tensor(name, shape, F32)

    def rounded(name, shape, offset):
        return nc.alloc_sbuf_tensor_at(name, shape, F32R, offset=offset)
    sb("pad", [P, -(nc.sbuf_base // 4) % 8 + 8])
    at = nc.sbuf_base
    m.wbuf = sb("wbuf", [P, 6, 1024])
    regions = [sb(f"region{q}", [P, 8, T]) for q in range(5)]
    regions_r = [rounded(f"region{q}_rounded", [P, 8, T], at + 4 * (6 + 8 * q) * 1024) for q in range(5)]
    m.w_hi = rounded("weights_hi", [P, 2, 1024], at + 4 * 2048)
    m.w_lo = rounded("weights_lo", [P, 2, 1024], at + 4 * 4096)

    def view(stores):
        def chunk(c, cols=slice(None), rows=slice(None), n=None, plus=None):
            store, k = stores[c // 8], c % 8
            if n is not None:
                return store[rows, k:k + n, cols]
            return store[rows, k if plus is None else plus + k, cols]
        return chunk
    m.chunk, m.rounded = view(regions), view(regions_r)
    m.tmp = sb("tmp", [P, 8, HALF])
    m.params = sb("par", [P, NPARAM])
    m.consts = sb("con", [P, NCONST])
    m.gcols = sb("gcols", [P, 3, 64])
    m.decay_b = sb("decay_b", [P, 64])
    m.mod, m.gain2, m.cact = sb("mod", [P, 24]), sb("gain2", [P, 8]), sb("cact", [P, 8])
    m.relfar, m.wi = sb("relfar", [P, AH]), sb("wi", [P, 8, AH])
    m.pl = sb("pl", [P, RP, 16])
    m.ps = nc.alloc_psum_tensor("ps", [P, 8, HALF], F32)
    m.w_raw = m.wbuf[:, 0:2, :]
    m.wflat = m.wbuf[:].rearrange("p a b -> p (a b)")
    m.tflat = m.tmp[:].rearrange("p a b -> p (a b)")
    m.psflat = m.ps[:].rearrange("p a b -> p (a b)")
    m.ra = m.chunk(RR, n=8).rearrange("p (g a) t -> p g a t", a=4)

    m.flat = lambda c, n: m.chunk(c, n=n).rearrange("p a b -> p (a b)")
    m.ktok = lambda c: m.flat(KTOK, 4)[:, c * 512:(c + 1) * 512]
    m.const = lambda name: m.consts[:, CCOL[name]:CCOL[name] + dict(CONSTS)[name]]
    m.par = lambda name, k: m.params[:, PCOL[name] + k:PCOL[name] + k + 1]
    m.par_at = lambda name, i: m.params[:, bass.ds(i + PCOL[name], 1)]
    m.pars = lambda name: m.params[:, PCOL[name]:PCOL[name] + dict(PARAMS)[name]]

    def by_chunk(a):
        return a.rearrange("k p t -> p k t")

    def gains(name):
        return lambda k: m.par(name, k)
    stages = [
        ("load", lambda: load_inputs(nc, m)),
        ("norm_mix", lambda: rms_norm(nc, m, "norm_mix", XIN, gains("norm_mix"), hi=XH, lo=XL)),
        ("in", lambda: mlstm_inputs(nc, m)),
        ("values", lambda: values_by_token(nc, m)),
        ("gates", lambda: mlstm_gates(nc, m)),
        ("scan", lambda: mlstm_scan(nc, m)),
        ("head_norm", lambda: mlstm_head_norm(nc, m)),
        ("w_out", lambda: add_projection(nc, m, "w_out", m.d["w_out"], GH, GL, m.d["xT"], XAGAIN, X0)),
        ("norm_mlp", lambda: rms_norm(nc, m, "norm_mlp", X0, gains("norm_mlp"), hi=NH, lo=NL)),
        ("mlp", lambda: mlp(nc, m)),
        ("norm_ple", lambda: rms_norm(nc, m, "norm_ple", X0, gains("norm_ple"), hi=NH, lo=NL)),
        ("ple", lambda: ple(nc, m)),
        ("norm_final", lambda: rms_norm(nc, m, "norm_final", X0, gains("norm_final"), dst=X0,
                                        store=by_chunk(m.d["residual"]), ahead=load_modulation_ahead(nc, m),
                                        products=lambda pe: modulation_products(nc, m, range(KT)))),
        ("modulation", lambda: modulation(nc, m)),
        ("norm_in", lambda: rms_norm(nc, m, "norm_in", X0, lambda k: m.gain2[:, k:k + 1], hi=NH, lo=NL,
                                     shift=lambda k: m.mod[:, k:k + 1])),
        ("att_in", lambda: project(nc, m, "att", m.d["w_att"], 10, NH, NL, QA)),
        ("latents", lambda: latents(nc, m)),
        ("qabs", lambda: absorbed_queries(nc, m)),
        ("index", lambda: index_scores(nc, m)),
        ("select", lambda: select_and_project(nc, m)),
        ("attention", lambda: sparse_attention(nc, m)),
        ("shift", lambda: shift_tokens(nc, m)),
        ("lora", lambda: rwkv_lora(nc, m)),
        ("keys", lambda: rwkv_keys(nc, m)),
        ("bonus", lambda: rwkv_bonus(nc, m)),
        ("scale", lambda: rwkv_scale(nc, m)),
        ("rscan", lambda: rwkv_scan(nc, m)),
        ("gn", lambda: rwkv_group_norm(nc, m)),
        ("z", lambda: branch_gates(nc, m)),
        ("merge", lambda: merge(nc, m)),
        ("w_o", lambda: add_projection(nc, m, "w_o", m.d["w_o"], MH_, ML, m.d["residual"], RES, OUT,
                                       gate=lambda n: m.mod[:, bass.ds(n + 16, 1)])),
        ("final", lambda: rms_norm(nc, m, "final", OUT, gains("final_g"), dst=OUT, store=by_chunk(out))),
    ]
    IN_USE.clear()
    for name, stage in stages:
        stage()
        if name in ("head_norm", "ple", "index", "attention", "gn"):
            recycle_semaphores(nc)
        if name == stop:
            break


def layout(inp):
    def a(name):
        x = np.asarray(inp[name])
        return x

    def chunked(w):
        k, n = w.shape
        return np.ascontiguousarray(w.reshape(k // P, P, n // P, P).transpose(2, 1, 0, 3).reshape(n // P, P, k))

    def cols(v):
        return np.ascontiguousarray(v.reshape(-1, P).T)

    o = {"xT": np.ascontiguousarray(a("x")[0].T).reshape(KT, P, T),
         "pT": np.ascontiguousarray(a("p")[0, 0].T).reshape(2, P, T), "consts": constant_tile(),
         "hot": distance_buckets()}
    src = {"norm_mix": "norm_mix", "norm_mlp": "norm_mlp", "norm_ple": "norm_ple", "norm_final": "norm_final",
           "head_norm": "mlstm_head_norm", "ple_gate_b": "ple_gate_b", "c": "c_2", "ada_b": "ada_b_2",
           "norm_g": "norm_g_2", "mu": "shift_mu_2", "w0": "w0_2", "a0": "a0_2", "k_k": "k_k_2", "k_a": "k_a_2",
           "r_k": "r_k_2", "lnx_g": "lnx_g_2", "lnx_b": "lnx_b_2", "kv_norm": "kv_norm_g_2", "final_g": "final_g_2"}
    par = np.zeros((P, NPARAM), np.float32)
    for name, s in src.items():
        c = cols(a(s).reshape(-1))
        par[:, PCOL[name]:PCOL[name] + c.shape[1]] = c
    par[0:16, PCOL["b_gates"]] = a("mlstm_b_gates").reshape(-1)
    o["params"] = par
    w = a("mlstm_w_in")[0]
    gate = np.zeros((D, P), np.float32)
    gate[:, 0:16] = w[:, 3072:3088]
    o["w_in"] = chunked(np.concatenate([w[:, 0:2048], gate, w[:, 2048:3072]], axis=1))
    o["w_out"] = chunked(a("mlstm_w_out")[0])
    w1, w2 = chunked(a("mlp_w1")[0]), a("mlp_w2")[0]
    o["w_mlp"] = np.concatenate([x for g in range(FF_GROUPS)
                                 for x in (w1[8 * g:8 * g + 8], chunked(w2[1024 * g:1024 * g + 1024]))])
    o["w_pgate"], o["w_ple"] = chunked(a("ple_gate_w")[0]), chunked(a("ple_w")[0])
    o["w_ada"] = chunked(a("ada_w_2")[0])
    w = a("w_in_2")[0]
    kw = np.zeros((D, P), np.float32)
    kw[:, 0:72] = w[:, 3840:3912]
    o["w_att"] = chunked(np.concatenate([w[:, 2176:2688], w[:, 3328:3840], w[:, 2688:2816], kw], axis=1))
    o["w_hn"] = chunked(np.concatenate([w[:, 0:1664], w[:, 1664:2176], w[:, 2816:3328], w[:, 3912:5960]], axis=1))
    o["w_pab"] = np.concatenate([chunked(a("w_pa_2")[0]), chunked(a("w_pb_2")[0])], axis=2)
    o["w_o"] = chunked(a("w_o_2")[0])
    o["w_ukT"] = np.ascontiguousarray(a("w_uk_2")[0].reshape(P, 4, 2, 64).transpose(2, 3, 1, 0).reshape(P, 4, P))
    o["w_uv"] = np.ascontiguousarray(a("w_uv_2")[0].reshape(P, 512))
    o["w_lora"] = np.concatenate([a("w2_2")[0], a("a2_2")[0]], axis=0)
    o["rel_bias"] = np.ascontiguousarray(a("rel_bias_2"))
    return o


def kernel(**inputs):
    import concourse.bacc as bacc
    from concourse.bass_utils import run_bass_kernel_spmd
    nc = bacc.Bacc("TRN2", target_bir_lowering=False, num_devices=1)
    build(nc)
    r = run_bass_kernel_spmd(nc, [layout(inputs)], core_ids=[0])
    return np.ascontiguousarray(r.results[0]["out"].reshape(D, T).T).reshape(1, T, D)
```
